# Optimizing a Trainium2 kernel written in Bass

```python
import functools
import jax, jax.numpy as jnp
from jax import lax
import numpy as np

D_MODEL = 1024
BATCH = 1
SEQ = 512
DEPTH = 1
DEC_BATCH = 8
DEC_SEQ = 1
PAST_LEN = 2048
PAGE_SIZE = 128

PLE_DIM = 256
D_FF = 2816
EPS = 1e-6
H_GLA = 4
DK_GLA = 64
DV_GLA = 128
GLA_RANK = 16
GLA_GATE_TEMP = 16.0
GLA_CHUNK = 64
H_NSA = 8
G_NSA = 2
R_NSA = H_NSA // G_NSA
D_NSA = 64
CMP_LEN = 32
CMP_STRIDE = 16
CMP_HIDDEN = 128
SEL_BLOCK = 64
N_SELECT = 16
WINDOW = 512
Q_BLOCK = 128
FORCE_SCORE = 1e4
NEG_INF = -1e30
ATTN_SCALE = D_NSA ** -0.5
ROPE_THETA = 500000.0
ROPE_DIM = D_NSA // 4
MIX_WIDTH = H_GLA * DV_GLA + H_NSA * D_NSA
IN_SPLITS = (H_GLA * DK_GLA, H_GLA * DK_GLA, H_GLA * DV_GLA, H_GLA * DV_GLA, GLA_RANK,
             H_NSA * D_NSA, 6 * G_NSA * D_NSA, 3 * H_NSA)
IN_COLS = sum(IN_SPLITS)

kernel_name = 'hymba_gla_nsa_macaron_decoder_step'

def rmsnorm(x, g):
    xf = x.astype(jnp.float32)
    y = xf * lax.rsqrt(jnp.mean(xf * xf, axis=-1, keepdims=True) + EPS)
    return (y * g.astype(jnp.float32)).astype(x.dtype)

def swiglu(x, w_in, w_out):
    g, u = jnp.split(x @ w_in, 2, axis=-1)
    return (jax.nn.silu(g) * u) @ w_out

def partial_rope(x, pos):
    half = ROPE_DIM // 2
    inv_freq = ROPE_THETA ** (-jnp.arange(half, dtype=jnp.float32) * 2.0 / ROPE_DIM)
    ang = pos.astype(jnp.float32)[:, None] * inv_freq[None, :]
    cos = jnp.cos(ang)[:, None, :]
    sin = jnp.sin(ang)[:, None, :]
    xf = x.astype(jnp.float32)
    x1, x2, rest = xf[..., :half], xf[..., half:ROPE_DIM], xf[..., ROPE_DIM:]
    out = jnp.concatenate([x1 * cos - x2 * sin, x2 * cos + x1 * sin, rest], axis=-1)
    return out.astype(x.dtype)

def masked_softmax(s, valid):
    return jax.nn.softmax(jnp.where(valid, s, NEG_INF), axis=-1) * valid

def split_cols(z):
    outs, off = [], 0
    for n in IN_SPLITS:
        outs.append(z[..., off:off + n])
        off += n
    return outs

def project_mixers(n, pos, w_in, w_a2, b_a):
    B, T, _ = n.shape
    q_g, k_g, v_g, r_g, a_lr, q_n, kv_n, gate_n = split_cols(n @ w_in)
    q_g = q_g.reshape(B, T, H_GLA, DK_GLA) * DK_GLA ** -0.5
    k_g = k_g.reshape(B, T, H_GLA, DK_GLA)
    v_g = v_g.reshape(B, T, H_GLA, DV_GLA)
    log_a = jax.nn.log_sigmoid((a_lr @ w_a2 + b_a).astype(jnp.float32)) / GLA_GATE_TEMP
    log_a = log_a.reshape(B, T, H_GLA, DK_GLA)
    q_n = q_n.reshape(B, T, H_NSA, D_NSA)
    kv = kv_n.reshape(B, T, 6, G_NSA, D_NSA)
    k_sel = partial_rope(kv[:, :, 2], pos)
    k_win = partial_rope(kv[:, :, 4], pos)
    nsa_rows = jnp.stack([kv[:, :, 0], kv[:, :, 1], k_sel, kv[:, :, 3]], axis=2)
    win_rows = jnp.stack([k_win, kv[:, :, 5]], axis=2)
    gates = jax.nn.sigmoid(gate_n.reshape(B, T, H_NSA, 3).astype(jnp.float32))
    return (q_g, k_g, v_g, log_a, r_g), (q_n, gates), nsa_rows, win_rows

def gla_scan(q, k, v, log_a, s0, chunk):
    B, T, H, _ = q.shape
    DV = v.shape[-1]
    nc = T // chunk

    def to_chunks(t):
        return t.astype(jnp.float32).reshape(B, nc, chunk, H, t.shape[-1]).transpose(1, 0, 3, 2, 4)

    tri = jnp.tril(jnp.ones((chunk, chunk), dtype=bool))

    def step(S, inp):
        qc, kc, vc, ac = inp
        b = jnp.cumsum(ac, axis=2)
        o_inter = jnp.einsum('bhtd,bhde->bhte', qc * jnp.exp(b), S)
        rel = jnp.where(tri[None, None, :, :, None], b[:, :, :, None, :] - b[:, :, None, :, :], -jnp.inf)
        attn = jnp.einsum('bhtd,bhtsd,bhsd->bhts', qc, jnp.exp(rel), kc)
        o_intra = jnp.einsum('bhts,bhse->bhte', attn, vc)
        b_last = b[:, :, -1:, :]
        S_new = jnp.exp(b_last[:, :, 0, :, None]) * S + jnp.einsum('bhsd,bhse->bhde', kc * jnp.exp(b_last - b), vc)
        return S_new, o_inter + o_intra

    S_fin, o = lax.scan(step, s0, (to_chunks(q), to_chunks(k), to_chunks(v), to_chunks(log_a)))
    o = o.transpose(1, 0, 3, 2, 4).reshape(B, T, H, DV)
    return o, S_fin

def gla_output(o, r, gain):
    B, T = o.shape[:2]
    o = rmsnorm(o, gain).reshape(B, T, H_GLA * DV_GLA)
    return (o * jax.nn.silu(r.astype(jnp.float32))).astype(r.dtype)

def compress(k, pos_emb, w1, w2):
    B, Tk = k.shape[:2]
    nc = (Tk - CMP_LEN) // CMP_STRIDE + 1
    idx = jnp.arange(nc)[:, None] * CMP_STRIDE + jnp.arange(CMP_LEN)[None, :]
    blocks = k[:, idx] + pos_emb[None, None, :, None, :]
    flat = blocks.transpose(0, 1, 3, 2, 4).reshape(B, nc, G_NSA, CMP_LEN * D_NSA)
    return jax.nn.gelu(flat @ w1) @ w2

def to_blocks(k):
    B, Tk = k.shape[:2]
    ns = -(-Tk // SEL_BLOCK)
    k = jnp.pad(k, ((0, 0), (0, ns * SEL_BLOCK - Tk), (0, 0), (0, 0)))
    return k.reshape(B, ns, SEL_BLOCK, G_NSA, D_NSA).transpose(0, 3, 1, 2, 4)

def overlap_matrix(nc, ns):
    start = jnp.arange(nc) * CMP_STRIDE
    sstart = jnp.arange(ns) * SEL_BLOCK
    m = (start[:, None] < sstart[None, :] + SEL_BLOCK) & (start[:, None] + CMP_LEN > sstart[None, :])
    return m.astype(jnp.float32)

def nsa_compressed(q, pos_q, kcmp, vcmp):
    s = jnp.einsum('bqgrd,bngd->bqgrn', q, kcmp).astype(jnp.float32) * ATTN_SCALE
    end = jnp.arange(kcmp.shape[1]) * CMP_STRIDE + CMP_LEN - 1
    valid = (end[None, :] <= pos_q[:, None])[None, :, None, None, :]
    p = masked_softmax(s, valid)
    return jnp.einsum('bqgrn,bngd->bqgrd', p, vcmp.astype(jnp.float32)), p

def nsa_selected(q_rot, pos_q, p_cmp, overlap, kb, vb):
    B, Tq = q_rot.shape[:2]
    ns = kb.shape[2]
    imp = jnp.einsum('bqgrn,ns->bqgs', p_cmp, overlap)
    blk = jnp.arange(ns, dtype=jnp.int32)[None, :]
    cur = (pos_q // SEL_BLOCK)[:, None]
    forced = (blk == 0) | (blk == cur) | (blk == cur - 1)
    causal = blk * SEL_BLOCK <= pos_q[:, None]
    imp = jnp.where(forced[None, :, None, :], FORCE_SCORE, jnp.where(causal[None, :, None, :], imp, -1.0))
    _, idx = lax.top_k(imp, min(N_SELECT, ns))
    kk = idx.shape[-1]
    idx_t = jnp.swapaxes(idx, 1, 2)
    bi = jnp.arange(B)[:, None, None, None]
    gi = jnp.arange(G_NSA)[None, :, None, None]
    kg = kb[bi, gi, idx_t]
    vg = vb[bi, gi, idx_t]
    s = jnp.einsum('bqgrd,bgqksd->bqgrks', q_rot, kg).astype(jnp.float32) * ATTN_SCALE
    kpos = idx[..., None] * SEL_BLOCK + jnp.arange(SEL_BLOCK, dtype=jnp.int32)
    valid = (kpos <= pos_q[None, :, None, None, None]).reshape(B, Tq, G_NSA, 1, kk * SEL_BLOCK)
    shp = s.shape
    p = masked_softmax(s.reshape(B, Tq, G_NSA, R_NSA, kk * SEL_BLOCK), valid).reshape(shp)
    return jnp.einsum('bqgrks,bgqksd->bqgrd', p, vg.astype(jnp.float32))

def nsa_window(q_rot, pos_q, kw, vw, pos_kw):
    s = jnp.einsum('bqgrd,bkgd->bqgrk', q_rot, kw).astype(jnp.float32) * ATTN_SCALE
    diff = pos_q[:, None] - pos_kw[None, :]
    valid = (diff >= 0) & (diff < WINDOW) & (pos_kw[None, :] >= 0)
    p = masked_softmax(s, valid[None, :, None, None, :])
    return jnp.einsum('bqgrk,bkgd->bqgrd', p, vw.astype(jnp.float32))

def nsa_mix(q, gates, pos_q, kcmp, vcmp, overlap, kb, vb, kw, vw, pos_kw):
    B, Tq = q.shape[:2]
    q_raw = q.reshape(B, Tq, G_NSA, R_NSA, D_NSA)
    q_rot = partial_rope(q, pos_q).reshape(B, Tq, G_NSA, R_NSA, D_NSA)
    o_cmp, p_cmp = nsa_compressed(q_raw, pos_q, kcmp, vcmp)
    o_sel = nsa_selected(q_rot, pos_q, p_cmp, overlap, kb, vb)
    o_win = nsa_window(q_rot, pos_q, kw, vw, pos_kw)
    g = gates.reshape(B, Tq, G_NSA, R_NSA, 3)
    o = g[..., 0:1] * o_cmp + g[..., 1:2] * o_sel + g[..., 2:3] * o_win
    return o.reshape(B, Tq, H_NSA * D_NSA).astype(q.dtype)

def mixer_prompt(n, mix_w):
    (w_in, w_a2, b_a, gla_norm, pos_k, w_k1, w_k2, pos_v, w_v1, w_v2) = mix_w
    B, T, _ = n.shape
    pos = jnp.arange(T, dtype=jnp.int32)
    (q_g, k_g, v_g, log_a, r_g), (q_n, gates), nsa_rows, win_rows = project_mixers(n, pos, w_in, w_a2, b_a)
    s0 = jnp.zeros((B, H_GLA, DK_GLA, DV_GLA), jnp.float32)
    o_g, s_fin = gla_scan(q_g, k_g, v_g, log_a, s0, GLA_CHUNK)
    o_gla = gla_output(o_g, r_g, gla_norm)
    kcmp = compress(nsa_rows[:, :, 0], pos_k, w_k1, w_k2)
    vcmp = compress(nsa_rows[:, :, 1], pos_v, w_v1, w_v2)
    kb = to_blocks(nsa_rows[:, :, 2])
    vb = to_blocks(nsa_rows[:, :, 3])
    overlap = overlap_matrix(kcmp.shape[1], kb.shape[2])
    kw_pad = jnp.pad(win_rows, ((0, 0), (WINDOW, 0), (0, 0), (0, 0), (0, 0)))
    nqb = T // Q_BLOCK
    qb = q_n.reshape(B, nqb, Q_BLOCK, H_NSA, D_NSA).swapaxes(0, 1)
    gb = gates.reshape(B, nqb, Q_BLOCK, H_NSA, 3).swapaxes(0, 1)
    starts = jnp.arange(nqb, dtype=jnp.int32) * Q_BLOCK

    def query_block(args):
        q_b, g_b, qs = args
        pos_q = qs + jnp.arange(Q_BLOCK, dtype=jnp.int32)
        kw_b = lax.dynamic_slice_in_dim(kw_pad, qs, WINDOW + Q_BLOCK, axis=1)
        pos_kw = qs - WINDOW + jnp.arange(WINDOW + Q_BLOCK, dtype=jnp.int32)
        return nsa_mix(q_b, g_b, pos_q, kcmp, vcmp, overlap, kb, vb, kw_b[:, :, 0], kw_b[:, :, 1], pos_kw)

    o_nsa = lax.map(query_block, (qb, gb, starts))
    o_nsa = o_nsa.swapaxes(0, 1).reshape(B, T, H_NSA * D_NSA)
    mix = jnp.concatenate([o_gla, o_nsa.astype(o_gla.dtype)], axis=-1)
    return mix, nsa_rows, win_rows[:, T - min(WINDOW, T):], s_fin.astype(n.dtype)

def mixer_sample(n, cache_l, win_l, gla_l, page_table, mix_w):
    (w_in, w_a2, b_a, gla_norm, pos_k, w_k1, w_k2, pos_v, w_v1, w_v2) = mix_w
    B, T, _ = n.shape
    past_len = page_table.shape[1] * cache_l.shape[1]
    pos = past_len + jnp.arange(T, dtype=jnp.int32)
    (q_g, k_g, v_g, log_a, r_g), (q_n, gates), nsa_rows, win_rows = project_mixers(n, pos, w_in, w_a2, b_a)
    o_g, s_fin = gla_scan(q_g, k_g, v_g, log_a, gla_l.astype(jnp.float32), T)
    o_gla = gla_output(o_g, r_g, gla_norm)
    past = cache_l[page_table].reshape(B, past_len, 4, G_NSA, D_NSA)
    full = jnp.concatenate([past, nsa_rows.astype(past.dtype)], axis=1)
    kcmp = compress(full[:, :, 0], pos_k, w_k1, w_k2)
    vcmp = compress(full[:, :, 1], pos_v, w_v1, w_v2)
    kb = to_blocks(full[:, :, 2])
    vb = to_blocks(full[:, :, 3])
    overlap = overlap_matrix(kcmp.shape[1], kb.shape[2])
    wb = win_l.shape[1]
    kw = jnp.concatenate([win_l, win_rows.astype(win_l.dtype)], axis=1)
    pos_kw = past_len - wb + jnp.arange(wb + T, dtype=jnp.int32)
    o_nsa = nsa_mix(q_n, gates, pos, kcmp, vcmp, overlap, kb, vb, kw[:, :, 0], kw[:, :, 1], pos_kw)
    keep = min(WINDOW, wb + T)
    mix = jnp.concatenate([o_gla, o_nsa.astype(o_gla.dtype)], axis=-1)
    return mix, nsa_rows, kw[:, wb + T - keep:], s_fin.astype(gla_l.dtype)

def trunk_layer(x, p, mixer, f1_pre, f1_post, f1_in, f1_out, m_pre, m_post, w_out,
                f2_pre, f2_post, f2_in, f2_out, ple_pre, ple_gate, ple_proj, ple_post):
    h = x + 0.5 * rmsnorm(swiglu(rmsnorm(x, f1_pre), f1_in, f1_out), f1_post)
    mix, nsa_rows, win_state, gla_state = mixer(rmsnorm(h, m_pre))
    h = h + rmsnorm(mix @ w_out, m_post)
    h = h + 0.5 * rmsnorm(swiglu(rmsnorm(h, f2_pre), f2_in, f2_out), f2_post)
    gate = jax.nn.sigmoid(rmsnorm(h, ple_pre) @ ple_gate)
    h = h + rmsnorm(gate * (p @ ple_proj), ple_post)
    return h, nsa_rows, win_state, gla_state

def setup_inputs(seed: int = 0) -> dict:
    key = jax.random.key(seed)
    ks = iter(jax.random.split(key, 48))
    f32 = jnp.float32

    def nrm(shape, scale):
        return jax.random.normal(next(ks), shape, f32) * scale

    def gain(n):
        return 1.0 + 0.05 * jax.random.normal(next(ks), (DEPTH, n), f32)

    n_pages = PAST_LEN // PAGE_SIZE
    n_used = DEC_BATCH * n_pages
    n_pool = n_used + (n_used + 3) // 4
    win_buf = min(WINDOW, PAST_LEN)
    page_table = jax.random.permutation(next(ks), n_pool)[:n_used].reshape(DEC_BATCH, n_pages).astype(jnp.int32)
    return {
        'x_prompt': nrm((BATCH, SEQ, D_MODEL), 1.0),
        'x_sample': nrm((DEC_BATCH, DEC_SEQ, D_MODEL), 1.0),
        'cache_nsa': nrm((DEPTH, n_pool, PAGE_SIZE, 4, G_NSA, D_NSA), 1.0),
        'state_win': nrm((DEPTH, DEC_BATCH, win_buf, 2, G_NSA, D_NSA), 1.0),
        'state_gla': nrm((DEPTH, DEC_BATCH, H_GLA, DK_GLA, DV_GLA), 1.0),
        'page_table': page_table,
        'p_prompt': nrm((DEPTH, BATCH, SEQ, PLE_DIM), 1.0),
        'p_sample': nrm((DEPTH, DEC_BATCH, DEC_SEQ, PLE_DIM), 1.0),
        'ffn1_norm_pre': gain(D_MODEL),
        'ffn1_norm_post': gain(D_MODEL),
        'ffn1_w_in': nrm((DEPTH, D_MODEL, 2 * D_FF), D_MODEL ** -0.5),
        'ffn1_w_out': nrm((DEPTH, D_FF, D_MODEL), D_FF ** -0.5),
        'mix_norm_pre': gain(D_MODEL),
        'mix_norm_post': gain(D_MODEL),
        'w_mix_in': nrm((DEPTH, D_MODEL, IN_COLS), D_MODEL ** -0.5),
        'w_gla_a2': nrm((DEPTH, GLA_RANK, H_GLA * DK_GLA), GLA_RANK ** -0.5),
        'b_gla_a': nrm((DEPTH, H_GLA * DK_GLA), 0.1),
        'gla_out_norm': gain(DV_GLA),
        'cmp_pos_k': nrm((DEPTH, CMP_LEN, D_NSA), 0.5),
        'w_cmp_k1': nrm((DEPTH, CMP_LEN * D_NSA, CMP_HIDDEN), (CMP_LEN * D_NSA) ** -0.5),
        'w_cmp_k2': nrm((DEPTH, CMP_HIDDEN, D_NSA), CMP_HIDDEN ** -0.5),
        'cmp_pos_v': nrm((DEPTH, CMP_LEN, D_NSA), 0.5),
        'w_cmp_v1': nrm((DEPTH, CMP_LEN * D_NSA, CMP_HIDDEN), (CMP_LEN * D_NSA) ** -0.5),
        'w_cmp_v2': nrm((DEPTH, CMP_HIDDEN, D_NSA), CMP_HIDDEN ** -0.5),
        'w_mix_out': nrm((DEPTH, MIX_WIDTH, D_MODEL), MIX_WIDTH ** -0.5),
        'ffn2_norm_pre': gain(D_MODEL),
        'ffn2_norm_post': gain(D_MODEL),
        'ffn2_w_in': nrm((DEPTH, D_MODEL, 2 * D_FF), D_MODEL ** -0.5),
        'ffn2_w_out': nrm((DEPTH, D_FF, D_MODEL), D_FF ** -0.5),
        'ple_norm_pre': gain(D_MODEL),
        'ple_w_gate': nrm((DEPTH, D_MODEL, D_MODEL), D_MODEL ** -0.5),
        'ple_w_proj': nrm((DEPTH, PLE_DIM, D_MODEL), PLE_DIM ** -0.5),
        'ple_norm_post': gain(D_MODEL),
    }

def reference(x_prompt, x_sample, cache_nsa, state_win, state_gla, page_table, p_prompt, p_sample,
              ffn1_norm_pre, ffn1_norm_post, ffn1_w_in, ffn1_w_out,
              mix_norm_pre, mix_norm_post, w_mix_in, w_gla_a2, b_gla_a, gla_out_norm,
              cmp_pos_k, w_cmp_k1, w_cmp_k2, cmp_pos_v, w_cmp_v1, w_cmp_v2, w_mix_out,
              ffn2_norm_pre, ffn2_norm_post, ffn2_w_in, ffn2_w_out,
              ple_norm_pre, ple_w_gate, ple_w_proj, ple_norm_post):
    hp, hs = x_prompt, x_sample
    nsa_p, win_p, gla_p, nsa_s, win_s, gla_s = [], [], [], [], [], []
    for i in range(DEPTH):
        mix_w = (w_mix_in[i], w_gla_a2[i], b_gla_a[i], gla_out_norm[i], cmp_pos_k[i], w_cmp_k1[i],
                 w_cmp_k2[i], cmp_pos_v[i], w_cmp_v1[i], w_cmp_v2[i])
        shared = (ffn1_norm_pre[i], ffn1_norm_post[i], ffn1_w_in[i], ffn1_w_out[i],
                  mix_norm_pre[i], mix_norm_post[i], w_mix_out[i],
                  ffn2_norm_pre[i], ffn2_norm_post[i], ffn2_w_in[i], ffn2_w_out[i],
                  ple_norm_pre[i], ple_w_gate[i], ple_w_proj[i], ple_norm_post[i])
        hp, r_p, w_p, s_p = trunk_layer(hp, p_prompt[i], functools.partial(mixer_prompt, mix_w=mix_w), *shared)
        mix_s = functools.partial(mixer_sample, cache_l=cache_nsa[i], win_l=state_win[i], gla_l=state_gla[i],
                                  page_table=page_table, mix_w=mix_w)
        hs, r_s, w_s, s_s = trunk_layer(hs, p_sample[i], mix_s, *shared)
        nsa_p.append(r_p); win_p.append(w_p); gla_p.append(s_p)
        nsa_s.append(r_s); win_s.append(w_s); gla_s.append(s_s)
    return (hp, hs, jnp.stack(nsa_p), jnp.stack(win_p), jnp.stack(gla_p),
            jnp.stack(nsa_s), jnp.stack(win_s), jnp.stack(gla_s))


_drawn_inputs = setup_inputs


def setup_inputs(seed=0):
    import zlib

    import numpy as np

    out = dict(_drawn_inputs(seed))
    spreads = {}
    factors = {'cmp_pos_k': 3.278,
     'ffn2_norm_pre': 2.761,
     'ffn2_norm_post': 3.97,
     'ple_norm_pre': 18.916,
     'ple_norm_post': 2.905}
    for name, (base, spread) in spreads.items():
        noise = np.random.default_rng([zlib.crc32(name.encode()), seed]).standard_normal(out[name].shape)
        drawn = base * np.exp(spread * noise) if base else spread * noise
        out[name] = __import__('jax').numpy.asarray(drawn.astype(out[name].dtype))
    for name, factor in factors.items():
        out[name] = (out[name] * factor).astype(out[name].dtype)
    return out
```

```python
from contextlib import ExitStack

import numpy as np

import concourse.bass as bass
from concourse import mybir

F32 = mybir.dt.float32
I32 = mybir.dt.int32
ACT = mybir.ActivationFunctionType
ALU = mybir.AluOpType
AX_X = mybir.AxisListType.X

P = 128
D_MODEL, D_FF, PLE_DIM = 1024, 2816, 256
SEQ, NB = 512, 8
T = SEQ + NB
HT = T // 2
KC = D_MODEL // P
FC = D_FF // P
GW = 256
EPS = 1e-6
H_GLA, DK, DV, RANK = 4, 64, 128, 16
H_NSA, G, R, D = 8, 2, 4, 64
PAST, PAGE = 2048, 128
NPG = PAST // PAGE
CMP_LEN, STRIDE, HIDDEN = 32, 16, 128
SELB, N_SEL, WINDOW = 64, 16, 512
NCP = (SEQ - CMP_LEN) // STRIDE + 1
NCS = (PAST + 1 - CMP_LEN) // STRIDE + 1
NSB = PAST // SELB + 1
SCALE = D ** -0.5
NEG = -1e30
C_QG, C_KG, C_VG, C_RG = 0, 256, 512, 1024
C_LR, C_QN, C_KV, C_GT = 1536, 1552, 2064, 2832
COL_GO, COL_BA, COL_PK, COL_PV = 64, 65, 67, 83
NCOL = 99
QG, KG, VG, RG, QN, KCM, VCM, KSL, VSL, KWN, VWN = 0, 2, 4, 8, 12, 16, 17, 18, 19, 20, 21
NT = SEQ // P


def constants():
    f = np.float32
    c = {}
    c["ident"] = np.eye(P, dtype=f)
    s, t = np.arange(P)[:, None], np.arange(P)[None, :]
    c["causal_t"] = (s <= t).astype(f)
    c["causal_add"] = np.where(t <= s, 0.0, NEG).astype(f)
    half = 8
    inv = (f(500000.0) ** (-np.arange(half, dtype=f) * f(2.0) / f(16))).astype(f)
    pos = np.concatenate([np.arange(SEQ), np.full(NB, PAST)]).astype(f)
    ang = (pos[:, None] * inv[None, :]).astype(f)
    cos, sin = np.cos(ang).astype(f), np.sin(ang).astype(f)
    rc, rs, sw = np.ones((P, T), f), np.zeros((P, T), f), np.zeros((P, P), f)
    for g in range(2):
        for j in range(half):
            a, b = g * D + j, g * D + half + j
            rc[a], rc[b] = cos[:, j], cos[:, j]
            rs[a], rs[b] = -sin[:, j], sin[:, j]
            sw[b, a] = sw[a, b] = 1.0
    c["rope_cos"], c["rope_sin"], c["rope_swap"] = rc, rs, sw
    n = np.arange(NCP)
    q = np.arange(SEQ)
    ok = (n[None, :] * STRIDE + CMP_LEN - 1 <= q[:, None]).astype(f)
    c["cmp_ok"] = ok.reshape(NT, P, NCP).transpose(1, 0, 2).copy()
    c["cmp_add"] = ((c["cmp_ok"] - 1) * f(1e30)).astype(f)
    st, ss = np.arange(NCS) * STRIDE, np.arange(NSB) * SELB
    c["overlap"] = ((st[:, None] < ss[None, :] + SELB) & (st[:, None] + CMP_LEN > ss[None, :])).astype(f)
    r = np.arange(NB * H_NSA)
    c["group_sum"] = (r[:, None] // R == r[None, :] // R).astype(f)
    c["own_row"] = (r[:, None] // H_NSA == np.arange(NB)[None, :]).astype(f)
    forced = np.zeros(NSB, f)
    forced[[0, NSB - 2, NSB - 1]] = 1
    c["forced"] = np.tile(np.stack([1 - forced, forced * f(1e4)]), (NB * H_NSA, 1, 1)).astype(f)
    c["earlier"] = np.tile((np.arange(NSB)[None, :] < np.arange(NSB)[:, None]).astype(f).reshape(1, -1), (NB * H_NSA, 1))
    c["pick"] = np.repeat(np.eye(NB, dtype=f)[:, :, None], P, 2).copy()
    return c


CONSTS = {k: v.shape for k, v in constants().items()}


def build(nc, ins, outs, consts):
    ctx = ExitStack()
    with ctx:
        def sb(name, cols, dt=F32, parts=P):
            return ctx.enter_context(nc.sbuf_tensor(name, [parts, cols], dt))

        def sem(name):
            return ctx.enter_context(nc.semaphore(name))

        banks = ctx.enter_context(nc.psum_tensor("banks", [P, 8, 512], F32))

        ARENA = 53080
        arena = sb("arena", ARENA)
        ptab = sb("page_table", NB * NPG, I32, 1)[:, :]
        top = [0]

        def cut(cols):
            o = top[0]
            top[0] += cols
            assert top[0] <= ARENA, top[0]
            return o

        def at(o, *dims):
            n = int(np.prod(dims))
            v = arena[:, o:o + n]
            if len(dims) == 1:
                return v
            names = "abcde"[:len(dims)]
            return v.rearrange(f"p ({' '.join(names)}) -> p {' '.join(names)}",
                               **{k: d for k, d in zip(names, dims)})

        o_h, o_n, o_hid = cut(KC * T), cut(KC * T), cut(FC * T)
        o_win, o_wout = cut(2 * 2 * KC * GW), cut(2 * FC * GW)
        o_spare = top[0]
        hT = at(o_h, KC, T)
        nT = at(o_n, KC, T)
        hid = at(o_hid, FC, T)
        win = at(o_win, 4, KC, GW)
        wout = at(o_wout, 2, FC, GW)

        ident = at(cut(P), P)
        ones = at(cut(P), P)
        causal_t = at(cut(P), P)
        causal_add = at(cut(P), P)
        cols = at(cut(NCOL), NCOL)
        gains = cols[:, 0:8 * KC].rearrange("p (i k) -> p i k", k=KC)
        o_tmp = top[0]
        gtmp = at(cut(T), T)
        gtmp2 = at(cut(T), T)
        sq2 = at(cut(2 * T), 2, T)
        ssum = at(cut(T), T)
        rs = at(cut(T), T)
        small = at(cut(64), 64)
        eps_col = small[:, 0:1]
        ckv = small[:, 1:3]
        sq = at(o_hid, KC, T)

        kct = at(cut((NB + 1) * NCS), NB + 1, NCS)
        vcm = at(cut((NB + 1) * P), NB + 1, P)
        qb_raw, qb_rot = at(cut(NB * 72), NB, 72), at(cut(NB * 72), NB, 72)
        o_qbraw, o_qbrot = top[0] - 2 * NB * 72, top[0] - NB * 72
        qb_cur = at(cut(64), 64)
        o_kvtok = top[0]
        kvtok = at(cut(NT * 6 * P), NT, 6, P)
        kvs = at(cut(6 * P), 6, P)[0:NB]
        vts = at(cut(H_GLA * DV), H_GLA * DV)[0:NB]
        ag = at(cut(T), T)
        wa2 = at(cut(256), 256)
        la = at(cut(2 * T), 2, T)
        gates = at(cut(NT * 24), NT, 24)
        gates_s = at(cut(24), 24)[0:NB]
        gates_h = at(cut(3), 3)[0:64]
        overlap = at(cut(NSB), NSB)
        group_sum = at(cut(64), 64)
        own_row = at(cut(NB), NB)
        forced = at(cut(2 * NSB), 2, NSB)
        w1 = at(o_wout, 2, 16, HIDDEN)
        pages = at(o_wout + 4096, 4, 2, 2, 3 * P)
        kvr = [at(o, 2, 4, 2, D) for o in (o_n + R * T, o_n + R * T + 1024, o_tmp, o_tmp + 1024)]
        kwin = at(o_tmp + 2048, 2, NT, P)
        hk = at(o_wout + 10240, 2, 2 * NCS)
        w2 = at(o_wout + 10748, 2, D)
        rope_c, rope_s = at(o_wout + 8828, T), at(o_wout + 9348, T)
        rope_swap = at(o_wout + 9868, P)
        agw = at(o_wout + 9996, KC, 56)
        assert 10748 + 2 * D <= 2 * FC * GW and 2048 + 2 * SEQ <= 6 * T
        xk, xv = at(o_win, 2, 1024), at(o_win + 2048, 2, 1024)
        xs_ = at(o_win + 4096, 16, P)
        vtok = at(o_win + 6144, NT, H_GLA * DV)
        qr = at(o_n, R, T)
        ssel = at(o_n + R * T, PAST + 1)[0:64]
        o_b = o_wout
        gb = at(o_b, 2, SEQ)
        e1, e2 = at(o_b + 1024, 2, SEQ), at(o_b + 2048, 2, SEQ)
        kft = at(o_b + 3072, NT, 2, P)
        gs, gsd = at(o_b + 4096, 2, DV), at(o_b + 4352, 2, DV)
        att = at(o_b + 4608, H_GLA, P)
        cp = at(o_b + 5120, G, R, NCP)
        ptc = at(o_b + 5368, G, R * P)
        cmp_ok, cmp_add = at(o_b + 6392, NT, NCP), at(o_b + 6516, NT, NCP)
        sst = at(o_b + 6640, NB, 2, DV)
        earlier = at(o_b + 8688, NSB, NSB)[0:64]
        pick = at(o_b + 9777, NB, P)[0:NB]
        pr = at(o_win + 4096, 2, G, 512)
        prt = at(o_win + 6144, 2, G, 512)
        pts = at(o_hid + KCM * T, 16, 64)
        sw = at(o_hid + VSL * T, WINDOW + 1)[0:64]
        o_m = o_hid + VWN * T
        pcs, pcg = at(o_m, NCS)[0:64], at(o_m + NCS, NCS)[0:64]
        pct, pcgt = at(o_m + 256, 64), at(o_m + 320, 64)
        imp1, imp = at(o_m + 384, NSB)[0:64], at(o_m + 417, NSB)[0:64]
        rank = at(o_m + 450, NSB)[0:64]
        cmps = at(o_tmp, 2, NSB, NSB)[0:64]

        gname = ["ffn1_norm_pre", "ffn1_norm_post", "mix_norm_pre", "mix_norm_post",
                 "ffn2_norm_pre", "ffn2_norm_post", "ple_norm_pre", "ple_norm_post"]

        x_loaded, const_loaded = sem("x_loaded"), sem("const_loaded")
        rows_loaded = sem("rows_loaded")
        cols_turned = sem("cols_turned")
        x_turned = sem("x_turned")
        h_ready = sem("h_ready")
        sq_ready = sem("sq_ready")
        ysq_ready = sem("ysq_ready")
        ssum_ready = sem("ssum_ready")
        ysq_used = sem("ysq_used")
        stat_ready = sem("stat_ready")
        n_ready = sem("n_ready")
        win_loaded = [sem(f"win_loaded{i}") for i in range(4)]
        g_ready, u_ready = sem("g_ready"), sem("u_ready")
        silu_ready, hid_ready = sem("silu_ready"), sem("hid_ready")
        wout_loaded = [sem(f"wout_loaded{i}") for i in range(2)]
        y_ready = sem("y_ready")
        y_kept = sem("y_kept")
        proj_ready, proj_kept_a, proj_kept_v = sem("proj_ready"), sem("proj_kept_a"), sem("proj_kept_v")
        lrgt_loaded = sem("lrgt_loaded")
        rs_read = sem("rs_read")
        init_done = sem("init_done")
        dve_step, act_step, pool_step = sem("dve_step"), sem("act_step"), sem("pool_step")
        stored = sem("stored")
        n_stored = [0]

        block = ctx.enter_context(nc.Block())

        def pair(b):
            return banks[:, b:b + 2, 0:HT]

        def halves(v):
            return v.rearrange("p (a t) -> p a t", a=2)

        NG = FC * P // GW
        PROJ_G = 11
        win_base = {}
        cnt = [0, 0, 0, 0]
        for phase in ("ffn1", "proj", "out", "ffn2", "ple"):
            win_base[phase] = list(cnt)
            if phase.startswith("ffn"):
                for j in range(NG):
                    cnt[2 * (j % 2)] += 16
                    cnt[2 * (j % 2) + 1] += 16
            elif phase == "proj":
                for j in range(PROJ_G):
                    cnt[j % 4] += 64 if j in (6, 7) else 16
            elif phase == "out":
                for j in range(4):
                    cnt[j] += 48
            else:
                for j in range(4):
                    cnt[j] += 16

        def sp_ffn_in(sp, n, w_in, prev_use):
            base = win_base[f"ffn{n + 1}"]
            src = w_in.rearrange("(k p) n -> p k n", p=P)

            def group(j, s, i):
                sp.dma_start(win[:, 2 * s], src[:, :, bass.ds(j * GW, GW)]).then_inc(win_loaded[2 * s], 16)
                sp.dma_start(win[:, 2 * s + 1], src[:, :, bass.ds(D_FF + j * GW, GW)]).then_inc(win_loaded[2 * s + 1], 16)

            prev_use(sp)
            group(0, 0, 0)
            group(1, 1, 0)
            with sp.Fori(1, 5) as i:
                for s in range(2):
                    sp.wait_ge(u_ready, 22 * n + 4 * i + 2 * s - 2)
                    group(2 * i + s, s, i)
            sp.wait_ge(u_ready, 22 * n + 18)
            group(10, 0, 5)

        def sp_ffn_out(sp, n, w_out, first):
            src = w_out.rearrange("(k p) n -> p k n", p=P)
            for q in (range(2) if first else range(2, 4)):
                if q >= 2:
                    sp.wait_ge(y_ready, Y0[f"ffn{n + 1}"] + 2 * (q - 1))
                sp.dma_start(wout[:, q % 2], src[:, :, q * GW:(q + 1) * GW]).then_inc(wout_loaded[q % 2], 16)

        Y0 = {"ffn1": 0, "out": 8, "ffn2": 16, "ple": 24}

        agw_zeroed, small_loaded = sem("agw_zeroed"), sem("small_loaded")
        rope_loaded = sem("rope_loaded")
        swapped, roped, cos_made = sem("swapped"), sem("roped"), sem("cos_made")
        z_ready, z_read, z_log, la_ready = sem("z_ready"), sem("z_read"), sem("z_log"), sem("la_ready")
        turned, kept_a, kept_v = sem("turned"), sem("kept_a"), sem("kept_v")
        w1_loaded, pages_loaded = sem("w1_loaded"), [sem(f"pages_loaded{i}") for i in range(4)]
        table_loaded = sem("table_loaded")
        ring_filled = sem("ring_filled")
        ring_a, ring_v = sem("ring_a"), sem("ring_v")
        ckv_ready, ckv_made = sem("ckv_ready"), sem("ckv_made")
        qcur_ready, sel_scored = sem("qcur_ready"), sem("sel_scored")
        gates_made = sem("gates_made")

        ROPE = [KSL, KWN, QN, QN + 1, QN + 2, QN + 3]

        def rope_out(q):
            return hid[:, ROPE[q]] if q < 2 else qr[:, q - 2]

        def sp_mixer_small(sp):
            sp.dma_start(wa2[0:RANK], ins["w_gla_a2"][0]).then_inc(small_loaded, 16)
            sp.dma_start(overlap[0:NCS], consts["overlap"]).then_inc(small_loaded, 16)
            sp.dma_start(group_sum[0:64], consts["group_sum"]).then_inc(small_loaded, 16)
            sp.dma_start(own_row[0:64], consts["own_row"]).then_inc(small_loaded, 16)
            sp.dma_start(forced[0:64], consts["forced"]).then_inc(small_loaded, 16)
            sp.wait_ge(y_ready, 8)
            sp.wait_ge(agw_zeroed, 1)
            wm = ins["w_mix_in"][0].rearrange("(k p) n -> p k n", p=P)
            with nc.allow_non_contiguous_dma(reason="narrow columns"):
                sp.dma_start(agw[:, :, 0:RANK], wm[:, :, C_LR:C_LR + RANK]).then_inc(rope_loaded, 16)
                sp.dma_start(agw[:, :, 32:56], wm[:, :, C_GT:C_GT + 24]).then_inc(rope_loaded, 16)
            sp.dma_start(rope_c, consts["rope_cos"]).then_inc(rope_loaded, 16)
            sp.dma_start(rope_s, consts["rope_sin"]).then_inc(rope_loaded, 16)
            sp.dma_start(rope_swap, consts["rope_swap"]).then_inc(rope_loaded, 16)
            for i, (a, b) in enumerate((("w_cmp_k1", "w_cmp_k2"), ("w_cmp_v1", "w_cmp_v2"))):
                sp.dma_start(w1[:, i], ins[a][0].rearrange("(m p) h -> p m h", p=P)).then_inc(w1_loaded, 16)
                sp.dma_start(w2[:, i], ins[b][0]).then_inc(w1_loaded, 16)

        def sp_cache(sp):
            cache = ins["cache_nsa"][0].rearrange("n (p t) k g d -> n p t (k g d)", t=2)
            sp.dma_start(ptab, ins["page_table"].rearrange("b (o n) -> o (b n)", o=1)).then_inc(table_loaded, 16)
            sp.wait_ge(table_loaded, 16)

            def quarter(b, qd, first=False):
                if not first:
                    sp.wait_ge(ring_filled, 16 * b + 3 * qd - 13)
                elif qd == 2:
                    sp.wait_ge(roped, 6)
                    sp.wait_ge(proj_ready, 23)
                for tile in range(2):
                    for hh in range(2):
                        n = sp.value_load(ptab[0:1, bass.ds(b * NPG + qd * 4 + tile * 2 + hh, 1)],
                                          min_val=0, max_val=cache.shape[0] - 1)
                        sp.dma_start(pages[64 * hh:64 * hh + 64, qd, tile],
                                     cache[bass.ds(n, 1), :, :, 0:3 * P].rearrange("o p t c -> p (o t) c"))\
                            .then_inc(pages_loaded[qd], 16)

            for qd in range(4):
                quarter(0, qd, first=True)
            with sp.Fori(1, NB) as b:
                for qd in range(4):
                    quarter(b, qd)

        kvr_made, kvr_begun = sem("kvr_made"), sem("kvr_begun")

        def pool_cache(pool):
            pool.wait_ge(proj_ready, 23)
            pool.wait_ge(la_ready, 2)

            def quarter(b, qd, first=False):
                pool.wait_ge(pages_loaded[qd], 64 * b + 64)
                if not first:
                    pool.wait_ge(ring_filled, 16 * b + 3 * qd - 13)
                    pool.sem_inc(kvr_begun, 1)
                for tile in range(2):
                    cp_ = pool.tensor_copy(kvr[qd][:, tile], pages[:, qd, tile, :, 0:4 * D].rearrange("p t (c d) -> p c t d", d=D))
                cp_.then_inc(kvr_made, 1)

            for qd in range(4):
                quarter(0, qd, first=True)
            with pool.Fori(1, NB) as b:
                for qd in range(4):
                    quarter(b, qd)

        def pe_mixer_prep(pe):
            pe.wait_ge(rope_loaded, 80)
            pe.wait_ge(proj_kept_a, 10)
            for k in range(KC):
                for a in range(2):
                    last = pe.matmul(banks[0:56, 4 + a, 0:HT], agw[:, k, :], nT[:, k, a * HT:(a + 1) * HT],
                                     start=(k == 0), stop=(k == KC - 1))
            last.then_inc(proj_ready, 1)
            pe.wait_ge(proj_kept_a, 12)
            pe.wait_ge(proj_kept_v, 11)
            for q in range(6):
                if q >= 4:
                    pe.wait_ge(roped, q - 3)
                for a in range(2):
                    last = pe.matmul(banks[:, 2 * (q % 4) + a, 0:HT], rope_swap, hid[:, ROPE[q], a * HT:(a + 1) * HT],
                                     start=True, stop=True)
                last.then_inc(swapped, 1)
            pe.wait_ge(small_loaded, 80)
            for hp in range(2):
                pe.wait_ge(roped, 3 + hp)
                for a in range(2):
                    last = pe.matmul(banks[:, 4 + 2 * hp + a, 0:HT], wa2[0:RANK, hp * P:(hp + 1) * P],
                                     ag[0:RANK, a * HT:(a + 1) * HT], start=True, stop=True)
                last.then_inc(z_ready, 1)

        def pool_mixer_prep(pool):
            pool.wait_ge(y_ready, 8)
            pool.memset(agw[:, :, RANK:32], 0.0).then_inc(agw_zeroed, 1)
            pool.wait_ge(rope_loaded, 80)
            pool.wait_ge(proj_kept_a, 12)
            pool.wait_ge(proj_kept_v, 11)
            for q in range(6):
                if q >= 2:
                    pool.wait_ge(roped, q - 1)
                pool.tensor_tensor(sq2[:, q % 2], hid[:, ROPE[q]], rope_c, ALU.mult).then_inc(cos_made, 1)

        def act_mixer_prep(act, link):
            act.wait_ge(proj_ready, 23)
            act.activation(halves(ag[0:56]), pair(4)[0:56], ACT.Copy).then_inc(proj_kept_a, 1)
            for hp in range(2):
                v = gtmp2 if hp else gtmp
                act.wait_ge(z_read, hp + 1)
                act.wait_ge(roped, 6)
                link(act.activation(v, la[:, hp], ACT.Abs))
            for hp in range(2):
                v = gtmp2 if hp else gtmp
                link(act.activation(v, v, ACT.Exp, scale=-1.0))
                act.activation(v, v, ACT.Ln, bias=1.0).then_inc(z_log, 1)

        def dve_mixer_prep(dve, link):
            dve.wait_ge(rope_loaded, 80)
            for q in range(6):
                dve.wait_ge(swapped, q + 1)
                if q >= 2:
                    dve.wait_ge(roped, q - 1)
                v = gtmp2 if q % 2 else gtmp
                link(dve.tensor_tensor(halves(v), pair(2 * (q % 4)), halves(rope_s), ALU.mult))
                dve.wait_ge(cos_made, q + 1)
                dve.tensor_tensor(rope_out(q), v, sq2[:, q % 2], ALU.add).then_inc(roped, 1)
            for hp in range(2):
                dve.wait_ge(z_ready, hp + 1)
                dve.tensor_scalar(halves(la[:, hp]), pair(4 + 2 * hp), cols[:, COL_BA + hp:COL_BA + hp + 1], None,
                                  ALU.add).then_inc(z_read, 1)
            for hp in range(2):
                dve.wait_ge(z_log, hp + 1)
                dve.scalar_tensor_tensor(out=la[:, hp], in0=la[:, hp], scalar=0.0, in1=gtmp2 if hp else gtmp,
                                         op0=ALU.min, op1=ALU.subtract).then_inc(la_ready, 1)
            link(dve.memset(arena[:, o_qbraw:o_qbraw + 2 * NB * 72], 0.0))
            dve.wait_ge(roped, 6)
            for o, src in ((qb_raw, hid[:, QN:QN + R, SEQ:T]), (qb_rot, qr[:, :, SEQ:T])):
                for g in range(G):
                    link(dve.tensor_copy(o[D * g:D * g + D, :, R * g:R * g + R],
                                         src[D * g:D * g + D].rearrange("p r b -> p b r")))

        def turn_jobs():
            jobs = []
            for i in range(NT):
                t0 = i * P
                for hf in range(2):
                    jobs.append(([(c * P, hid[:, KCM + 3 * hf + c, t0:t0 + P], P) for c in range(3)],
                                 kvtok[:, i, 3 * hf:3 * hf + 3].rearrange("p k c -> p (k c)"), 3 * P, P))
                jobs.append(([(c * P, hid[:, VG + c, t0:t0 + P], P) for c in range(4)], vtok[:, i], 4 * P, P))
            jobs.append(([(c * P, hid[:, KCM + c, SEQ:T], NB) for c in range(4)],
                         kvs[:, 0:4].rearrange("p k c -> p (k c)"), 4 * P, NB))
            jobs.append(([(c * P, hid[:, KCM + 4 + c, SEQ:T], NB) for c in range(2)],
                         kvs[:, 4:6].rearrange("p k c -> p (k c)"), 2 * P, NB))
            jobs.append(([(c * P, hid[:, VG + c, SEQ:T], NB) for c in range(4)], vts, 4 * P, NB))
            return jobs

        JOBS = turn_jobs()

        def pe_turn(pe):
            for n, (moves, _, _, m) in enumerate(JOBS):
                if n >= 8:
                    pe.wait_ge(kept_v if n % 2 else kept_a, (n - 8) // 2 + 1)
                elif n == 0:
                    pe.wait_ge(la_ready, 2)
                for c, src, _ in moves:
                    last = pe.transpose(banks[0:m, n % 8, c:c + P], src, ident)
                last.then_inc(turned, 1)
            pe.wait_ge(kept_v, 4)
            for i in range(NT):
                pe.transpose(banks[:, 7, 24 * i:24 * i + 24], ag[32:56, i * P:(i + 1) * P], ident[32:56, 32:56])
            pe.transpose(banks[0:NB, 7, 96:120], ag[32:56, SEQ:T], ident[32:56, 32:56]).then_inc(turned, 1)

        def keep_turned(eng, copy, sem_, parity):
            for n, (_, dst, width, m) in enumerate(JOBS):
                if n % 2 == parity:
                    eng.wait_ge(turned, n + 1)
                    copy(dst, banks[0:m, n % 8, 0:width]).then_inc(sem_, 1)

        def act_gates(act):
            act.wait_ge(turned, len(JOBS) + 1)
            act.activation(gates.rearrange("p i c -> p (i c)"), banks[:, 7, 0:96], ACT.Sigmoid)
            act.activation(gates_s, banks[0:NB, 7, 96:120], ACT.Sigmoid).then_inc(gates_made, 1)

        def free(pe, b, u, first):
            if not first or u >= 4:
                pe.wait_ge(ring_v if u % 2 else ring_a, 8 * b + (u - 4) // 2 + 1)

        def pe_hidden(pe, bank, kind, n):
            src = xv if kind else xk
            for m in range(16):
                rhs = src.rearrange("p g (n s) -> p g n s", s=8)[:, :, m // 8:m // 8 + n, m % 8]
                mm = pe.matmul(banks[:, bank, 0:2 * n].rearrange("p (g n) -> p g n", g=G), w1[:, kind, m, :], rhs,
                               start=(m == 0), stop=(m == 15))
            mm.then_inc(ring_filled, 1)

        def pe_second(pe, bank, kind, n):
            for g in range(G):
                h = hk[:, kind, g * n:(g + 1) * n]
                if kind == 0:
                    mm = pe.matmul(banks[D * g:D * g + D, bank, 0:n], w2[:, 0, :], h, start=True, stop=True)
                else:
                    mm = pe.matmul(banks[0:n, bank, g * D:g * D + D], h, w2[:, 1, :], start=True, stop=True)
            mm.then_inc(ring_filled, 1)

        def pe_position(pe):
            pe.wait_ge(w1_loaded, 64)
            pe.wait_ge(kept_a, len(JOBS) // 2 + 1)
            pe.wait_ge(kept_v, len(JOBS) // 2)
            for kind, o in ((0, COL_PK), (1, COL_PV)):
                for m in range(16):
                    mm = pe.matmul(banks[:, 4, kind:kind + 1], w1[:, kind, m, :], cols[:, o + m:o + m + 1],
                                   start=(m == 0), stop=(m == 15))
            mm.then_inc(ckv_ready, 1)

        def pe_sample(pe, b, first=False, last_b=False):
            for qd in range(4):
                pe.wait_ge(kvr_made, 4 * b + qd + 1)
                for kind in range(3):
                    u = 3 * qd + kind
                    free(pe, b, u, first)
                    for tile in range(2):
                        for x in range(2):
                            src = (kvr[qd][:, tile, 2 * kind + x].rearrange("p t d -> p (t d)") if kind < 2
                                   else pages[:, qd, tile, x, 2 * P:3 * P])
                            c = x * 256 + tile * P if kind < 2 else (2 * tile + x) * P
                            tr = pe.transpose(banks[:, u % 4, c:c + P], src, ident)
                    tr.then_inc(ring_filled, 1)
            if first:
                pe.wait_ge(ckv_made, 1)
            pe.wait_ge(qcur_ready, b + 1)
            pe.wait_ge(ring_a, 8 * b + 2)
            pe.wait_ge(ring_v, 8 * b + 3)

            def scores(js):
                for j in js:
                    sc = pe.matmul(banks[0:64, 4 + j, :], qb_cur, xs_[:, 4 * j:4 * j + 4, :],
                                   start=first, stop=last_b, skip_group_check=True)
                return sc

            scores(range(2))
            pe.wait_ge(ring_a, 8 * b + 6)
            pe.wait_ge(ring_v, 8 * b + 6)
            pe_hidden(pe, 0, 0, NCS)
            pe_hidden(pe, 2, 1, NCS)
            scores(range(2, 4)).then_inc(sel_scored, 1)
            pe.wait_ge(ring_a, 8 * b + 7)
            pe_second(pe, 1, 0, NCS)
            pe.wait_ge(ring_a, 8 * b + 8)
            pe_second(pe, 3, 1, NCS)

        def pe_cache(pe):
            pe_sample(pe, 0, first=True)
            with pe.Fori(1, NB - 1) as b:
                pe_sample(pe, b)
            pe_sample(pe, NB - 1, last_b=True)
            for kind, src in ((0, KCM), (1, VCM)):
                free(pe, NB, kind, False)
                for g in range(G):
                    for t in range(2):
                        mm = pe.matmul(banks[D * t:D * t + D, kind, g * 256:(g + 1) * 256], ident[:, D * g:D * g + D],
                                       hid[:, src, 0:SEQ].rearrange("p (n t) -> p n t", t=2)[:, :, t],
                                       start=True, stop=True)
                mm.then_inc(ring_filled, 1)
            pe.wait_ge(ring_a, 8 * NB + 1)
            pe.wait_ge(ring_v, 8 * NB + 1)
            pe_hidden(pe, 2, 0, NCP)
            pe.wait_ge(ring_a, 8 * NB + 2)
            pe_second(pe, 3, 0, NCP)
            pe_hidden(pe, 0, 1, NCP)
            pe.wait_ge(ring_a, 8 * NB + 3)
            pe_second(pe, 1, 1, NCP)

        def read_turn(copy, b, u):
            kind, qd = u % 3, u // 3
            if kind < 2:
                return copy((xv if kind else xk)[:, :, qd * 256:(qd + 1) * 256],
                            banks[:, u % 4, :].rearrange("p (g c) -> p g c", g=G)).then_inc(ring_v if u % 2 else ring_a, 1)
            return copy(xs_[:, 4 * qd:4 * qd + 4].rearrange("p j c -> p (j c)"), banks[:, u % 4, :])\
                .then_inc(ring_v if u % 2 else ring_a, 1)

        def act_gelu(act, bank, kind, n):
            act.activation(hk[:, kind, 0:2 * n], banks[:, bank, 0:2 * n], ACT.Gelu_apprx_tanh,
                           bias=ckv[:, kind:kind + 1]).then_inc(ring_a, 1)

        def act_cache(act, link):
            act.wait_ge(ckv_ready, 1)
            link(act.activation(ckv, banks[:, 4, 0:2], ACT.Copy))
            act.sem_inc(ckv_made, 1)

            def copy(o, i):
                return act.activation(o, i, ACT.Copy)

            with act.Fori(0, NB) as b:
                for u in range(0, 12, 2):
                    act.wait_ge(ring_filled, 16 * b + u + 1)
                    read_turn(copy, b, u)
                for kind in range(2):
                    act.wait_ge(ring_filled, 16 * b + 13 + kind)
                    act_gelu(act, 2 * kind, kind, NCS)
            act.wait_ge(ring_filled, 16 * NB + 1)
            copy(xk[:, :, 0:256], banks[:, 0, :].rearrange("p (g c) -> p g c", g=G)).then_inc(ring_a, 1)
            for kind in range(2):
                act.wait_ge(ring_filled, 16 * NB + 3 + 2 * kind)
                act_gelu(act, 2 - 2 * kind, kind, NCP)

        def dve_cache(dve, link):
            def copy(o, i):
                return dve.tensor_copy(o, i)

            dve.wait_ge(ckv_made, 1)
            def sample(b, first=False):
                if not first:
                    dve.wait_ge(sel_scored, b)
                dve.tensor_copy(qb_cur, at(o_qbrot, 9, 64)[:, bass.ds(b, 1)].rearrange("p o c -> p (o c)")).then_inc(qcur_ready, 1)
                for u in range(1, 12, 2):
                    dve.wait_ge(ring_filled, 16 * b + u + 1)
                    read_turn(copy, b, u)
                dve.wait_ge(ring_filled, 16 * b + 15)
                copy(kct[:, bass.ds(b, 1)].rearrange("p o c -> p (o c)"), banks[:, 1, 0:NCS]).then_inc(ring_v, 1)
                dve.wait_ge(ring_filled, 16 * b + 16)
                copy(vcm[0:NCS, bass.ds(b, 1)].rearrange("p o c -> p (o c)"), banks[0:NCS, 3, 0:P]).then_inc(ring_v, 1)

            sample(0, first=True)
            with dve.Fori(1, NB) as b:
                sample(b)
            dve.wait_ge(ring_filled, 16 * NB + 2)
            copy(xv[:, :, 0:256], banks[:, 1, :].rearrange("p (g c) -> p g c", g=G)).then_inc(ring_v, 1)
            dve.wait_ge(ring_filled, 16 * NB + 4)
            copy(kct[:, NB, 0:NCP], banks[:, 3, 0:NCP]).then_inc(ring_v, 1)
            dve.wait_ge(ring_filled, 16 * NB + 6)
            copy(vcm[0:NCP, NB], banks[0:NCP, 1, 0:P]).then_inc(ring_v, 1)

        kwin_loaded = [sem("kwin_loaded0"), sem("kwin_loaded1")]
        kwin_turned, kwt_made, win_scored = sem("kwin_turned"), sem("kwt_made"), sem("win_scored")
        rest_scored = sem("rest_scored")
        kwts = at(o_wout + 4096, 2, 512)

        def sp_window(sp):
            for b in range(NB):
                if b >= 2:
                    sp.wait_ge(kwin_turned, b - 1)
                sp.dma_start(kwin[:, b % 2], ins["state_win"][0, b].rearrange("(w p) v g d -> p w v (g d)", p=P)[:, :, 0])\
                    .then_inc(kwin_loaded[b % 2], 16)

        def pe_window(pe):
            for b in range(NB + 1):
                if b < NB:
                    pe.wait_ge(kwin_loaded[b % 2], 16 * (b // 2 + 1))
                    if b == 0:
                        pe.wait_ge(ring_a, 8 * NB + 3)
                        pe.wait_ge(ring_v, 8 * NB + 3)
                    else:
                        if b >= 2:
                            pe.wait_ge(kwt_made, b - 1)
                    for w in range(NT):
                        tr = pe.transpose(banks[:, b % 2, w * P:(w + 1) * P], kwin[:, b % 2, w], ident)
                    tr.then_inc(kwin_turned, 1)
                if b >= 1:
                    pe.wait_ge(kwt_made, b)
                    q = at(o_qbrot, 9, 64)[:, b - 1]
                    mm = pe.matmul(banks[0:64, 2, :], q, kwts[:, (b - 1) % 2], start=(b == 1), stop=(b == NB))
                    mm.then_inc(win_scored, 1)
            for col, key in ((0, KWN), (1, KSL)):
                for b in range(NB):
                    pe.matmul(banks[0:64, 3, col:col + 1], at(o_qbrot, 9, 64)[:, b], hid[:, key, SEQ + b:SEQ + b + 1],
                              start=(b == 0), stop=(b == NB - 1))
            for b in range(NB):
                mm = pe.matmul(banks[0:64, 3, 8:8 + NCS], at(o_qbraw, 9, 64)[:, b], kct[:, b], start=(b == 0), stop=(b == NB - 1))
            mm.then_inc(rest_scored, 1)

        def act_window(act):
            for b in range(NB):
                act.wait_ge(kwin_turned, b + 1)
                if b >= 2:
                    act.wait_ge(win_scored, b - 1)
                act.activation(kwts[:, b % 2], banks[:, b % 2, :], ACT.Copy).then_inc(kwt_made, 1)

        gla_stored, rows_stored, st_stored = sem("gla_stored"), sem("rows_stored"), sem("st_stored")
        dscan = sem("dscan")
        st = small[0:64, 16:32]
        new2 = small[0:64, 32:34]
        ptw = at(o_m, NT, 64)
        pn = at(o_m + 484, 2, NB)[0:64]
        pnt = at(o_qbraw, 2, 64)[0:NB]
        o_dec = o_b + 10801
        dec = at(o_dec, 3, 2, NT)
        ea = at(o_dec + 24, 2, NB)
        gates_moved = sem("gates_moved")
        cmp_max, cmp_exp, cmp_probs, cmp_turned, pct_made = (
            sem("cmp_max"), sem("cmp_exp"), sem("cmp_probs"), sem("cmp_turned"), sem("pct_made"))
        imp1_ready, imp1_kept, imp_ready = sem("imp1_ready"), sem("imp1_kept"), sem("imp_ready")
        win_max, win_exp, win_probs = sem("win_max"), sem("win_exp"), sem("win_probs")
        sel_max, sel_exp, sel_probs = sem("sel_max"), sem("sel_exp"), sem("sel_probs")
        p_turned, pt_made = sem("p_turned"), sem("pt_made")
        late_loaded = sem("late_loaded")
        st_loaded = sem("st_loaded")

        def sp_late(sp):
            sp.wait_ge(rest_scored, 1)
            sp.dma_start(earlier, consts["earlier"].rearrange("p (a b) -> p a b", a=NSB)).then_inc(late_loaded, 16)
            sp.dma_start(cmp_ok, consts["cmp_ok"]).then_inc(late_loaded, 16)
            sp.dma_start(cmp_add, consts["cmp_add"]).then_inc(late_loaded, 16)
            sp.dma_start(pick, consts["pick"]).then_inc(late_loaded, 16)
            for hh in range(2):
                sp.dma_start(sst[DK * hh:DK * hh + DK].rearrange("p b c e -> p (b c) e"),
                             ins["state_gla"][0].rearrange("b (c h) d e -> h d (b c) e", h=2)[hh]).then_inc(st_loaded, 16)

        def dve_softmaxes(dve, link):
            X = AX_X
            dve.wait_ge(rest_scored, 1)
            dve.wait_ge(gates_moved, 16)
            link(dve.tensor_copy(new2, banks[0:64, 3, 0:2]))
            link(dve.tensor_reduce(st[:, 0:1], banks[0:64, 3, 8:8 + NCS], X, ALU.max))
            dve.tensor_scalar(st[:, 1:2], st[:, 0:1], -SCALE, None, ALU.mult).then_inc(cmp_max, 1)
            link(dve.tensor_copy(sw[:, 1:WINDOW], banks[0:64, 2, 1:WINDOW]))
            link(dve.memset(sw[:, 0:1], NEG))
            link(dve.tensor_copy(sw[:, WINDOW:WINDOW + 1], new2[:, 0:1]))
            link(dve.tensor_reduce(st[:, 4:5], sw, X, ALU.max))
            dve.tensor_scalar(st[:, 5:6], st[:, 4:5], -SCALE, None, ALU.mult).then_inc(win_max, 1)
            dve.wait_ge(cmp_exp, 1)
            link(dve.reciprocal(st[:, 3:4], st[:, 2:3]))
            link(dve.tensor_scalar(pcs, pcs, st[:, 3:4], None, ALU.mult))
            dve.tensor_scalar(pcg, pcs, gates_h[:, 0:1], None, ALU.mult).then_inc(cmp_probs, 1)
            dve.wait_ge(win_exp, 1)
            link(dve.reciprocal(st[:, 7:8], st[:, 6:7]))
            link(dve.tensor_tensor(st[:, 7:8], st[:, 7:8], gates_h[:, 2:3], ALU.mult))
            link(dve.tensor_scalar(sw, sw, st[:, 7:8], None, ALU.mult))
            dve.tensor_scalar(pn[:, 1], own_row[0:64], sw[:, WINDOW:WINDOW + 1], None, ALU.mult).then_inc(win_probs, 1)
            dve.wait_ge(imp1_ready, 1)
            dve.tensor_copy(imp1, banks[0:64, 1, 0:NSB]).then_inc(imp1_kept, 1)
            dve.wait_ge(imp_ready, 1)
            link(dve.tensor_tensor(imp, banks[0:64, 1, 0:NSB], forced[0:64, 0], ALU.mult))
            link(dve.tensor_tensor(imp, imp, forced[0:64, 1], ALU.add))
            other = imp.unsqueeze(1).broadcast_to([64, NSB, NSB])
            mine = imp.unsqueeze(2).broadcast_to([64, NSB, NSB])
            link(dve.tensor_tensor(cmps[:, 1], other, mine, ALU.is_equal))
            dve.wait_ge(late_loaded, 64)
            link(dve.tensor_tensor(cmps[:, 1], cmps[:, 1], earlier, ALU.mult))
            link(dve.tensor_tensor(cmps[:, 0], other, mine, ALU.is_gt))
            link(dve.tensor_tensor(cmps[:, 0], cmps[:, 0], cmps[:, 1], ALU.add))
            link(dve.tensor_reduce(rank, cmps[:, 0], X, ALU.add))
            link(dve.tensor_scalar(rank, rank, N_SEL - 0.5, 1.0, ALU.is_lt, ALU.subtract))
            link(dve.tensor_scalar(rank, rank, -NEG, None, ALU.mult))
            sv = ssel[:, 0:PAST].rearrange("p (j t s q) -> p j t s q", j=8, t=2, s=4)
            bv = banks[0:64, 4:8, :].rearrange("p k c -> p (k c)").rearrange("p (j t s q) -> p j t s q", j=8, t=2, s=4)
            mask = rank[:, 0:NSB - 1].rearrange("p (j s) -> p j s", j=8).unsqueeze(3).broadcast_to([64, 8, 4, 32])
            for t in range(2):
                link(dve.tensor_tensor(sv[:, :, t], bv[:, :, t], mask, ALU.add))
            link(dve.tensor_copy(ssel[:, PAST:PAST + 1], new2[:, 1:2]))
            link(dve.tensor_reduce(st[:, 8:9], ssel, X, ALU.max))
            dve.tensor_scalar(st[:, 9:10], st[:, 8:9], -SCALE, None, ALU.mult).then_inc(sel_max, 1)
            dve.wait_ge(sel_exp, 1)
            link(dve.reciprocal(st[:, 11:12], st[:, 10:11]))
            link(dve.tensor_tensor(st[:, 11:12], st[:, 11:12], gates_h[:, 1:2], ALU.mult))
            link(dve.tensor_scalar(ssel, ssel, st[:, 11:12], None, ALU.mult))
            dve.tensor_scalar(pn[:, 0], own_row[0:64], ssel[:, PAST:PAST + 1], None, ALU.mult).then_inc(sel_probs, 1)

        def act_softmaxes(act):
            act.wait_ge(cmp_max, 1)
            act.activation(pcs, banks[0:64, 3, 8:8 + NCS], ACT.Exp, bias=st[:, 1:2], scale=SCALE,
                           accum_out=st[:, 2:3]).then_inc(cmp_exp, 1)
            act.wait_ge(win_max, 1)
            act.activation(sw, sw, ACT.Exp, bias=st[:, 5:6], scale=SCALE, accum_out=st[:, 6:7]).then_inc(win_exp, 1)
            act.wait_ge(cmp_turned, 1)
            act.activation(at(o_m + 256, P)[0:NCS], banks[0:NCS, 0, 0:P], ACT.Copy).then_inc(pct_made, 1)
            act.wait_ge(sel_max, 1)
            act.activation(ssel, ssel, ACT.Exp, bias=st[:, 9:10], scale=SCALE, accum_out=st[:, 10:11]).then_inc(sel_exp, 1)
            for k, (o, i) in enumerate((
                    (pts[:, 0:8].rearrange("p a c -> p (a c)"), banks[:, 4, :]),
                    (pts[:, 8:16].rearrange("p a c -> p (a c)"), banks[:, 5, :]),
                    (ptw.rearrange("p a c -> p (a c)"), banks[:, 6, 0:256]),
                    (pnt.rearrange("p a c -> p (a c)"), banks[0:NB, 7, 0:P]))):
                act.wait_ge(p_turned, k + 1)
                act.activation(o, i, ACT.Copy).then_inc(pt_made, 1)

        def pe_softmaxes(pe):
            pe.wait_ge(cmp_probs, 1)
            pe.transpose(banks[0:NCS, 0, 0:64], pcs, ident[0:64, 0:64])
            pe.transpose(banks[0:NCS, 0, 64:128], pcg, ident[0:64, 0:64]).then_inc(cmp_turned, 1)
            pe.wait_ge(pct_made, 1)
            pe.matmul(banks[0:64, 1, 0:NSB], pct[0:NCS], overlap[0:NCS], start=True, stop=True).then_inc(imp1_ready, 1)
            pe.wait_ge(imp1_kept, 1)
            pe.matmul(banks[0:64, 1, 0:NSB], group_sum[0:64], imp1, start=True, stop=True).then_inc(imp_ready, 1)
            pe.wait_ge(sel_probs, 1)
            pe.wait_ge(win_probs, 1)
            for j in range(16):
                tr = pe.transpose(banks[:, 4 + j // 8, j % 8 * 64:(j % 8 + 1) * 64], ssel[:, j * P:(j + 1) * P], ident[0:64, 0:64])
                if j % 8 == 7:
                    tr.then_inc(p_turned, 1)
            for w in range(NT):
                tr = pe.transpose(banks[:, 6, w * 64:(w + 1) * 64], sw[:, w * P:(w + 1) * P], ident[0:64, 0:64])
            tr.then_inc(p_turned, 1)
            for k in range(2):
                tr = pe.transpose(banks[0:NB, 7, k * 64:(k + 1) * 64], pn[:, k], ident[0:64, 0:64])
            tr.then_inc(p_turned, 1)

        b_ready, e_ready, qk_ready = sem("b_ready"), sem("e_ready"), sem("qk_ready")
        kf_turned, kf_made = sem("kf_turned"), sem("kf_made")
        a_ready, att_made, o_ready, o_kept = sem("a_ready"), sem("att_made"), sem("o_ready"), sem("o_kept")
        kv_ready, kv_used, gs_ready, gs_done = sem("kv_ready"), sem("kv_used"), sem("gs_ready"), sem("gs_done")
        vb_ready, vb_used, os_ready, os_kept = sem("vb_ready"), sem("vb_used"), sem("os_ready"), sem("os_kept")
        gsq, gstat, groot, gsilu, mix_g = sem("gsq"), sem("gstat"), sem("groot"), sem("gsilu"), sem("mix_g")

        def dve_gla(dve, link):
            for hp in range(2):
                for c in range(NT):
                    x = slice(c * P, (c + 1) * P)
                    dve.tensor_tensor_scan(gb[:, hp, x], la[:, hp, x], la[:, hp, x], 0.0, ALU.add, ALU.bypass).then_inc(dscan, 1)
            dve.wait_ge(dscan, 8)
            for hp in range(2):
                for c in range(NT):
                    x = slice(c * P, (c + 1) * P)
                    dve.tensor_scalar(e1[:, hp, x], gb[:, hp, x], gb[:, hp, c * P + 63:c * P + 64], None,
                                      ALU.subtract).then_inc(b_ready, 1)
            dve.wait_ge(e_ready, 1)
            link(dve.tensor_copy(dec[:, 2], e1.rearrange("p h (c t) -> p h c t", c=NT)[:, :, :, P - 1]))
            dve.scalar_tensor_tensor(out=e1, in0=hid[:, QG:QG + 2, 0:SEQ], scalar=DK ** -0.5, in1=e1,
                                     op0=ALU.mult, op1=ALU.mult).then_inc(qk_ready, 1)
            dve.tensor_tensor(e2, hid[:, KG:KG + 2, 0:SEQ], e2, ALU.mult).then_inc(qk_ready, 1)
            for c in range(NT):
                dve.wait_ge(o_ready, 2 * c)
                for hh in range(2):
                    dve.wait_ge(a_ready, 2 * c + hh + 1)
                    dve.scalar_tensor_tensor(out=att.rearrange("p (c h) t -> p h c t", h=2)[:, hh],
                                             in0=banks[:, 2 + hh, 0:256].rearrange("p (c t) -> p c t", c=2), scalar=-NEG,
                                             in1=causal_t.unsqueeze(1).broadcast_to([P, 2, P]),
                                             op0=ALU.min, op1=ALU.mult).then_inc(att_made, 1)
                dve.wait_ge(kv_ready, c + 1)
                for hp in range(2):
                    kv = banks[:, 6, hp * P:(hp + 1) * P]
                    if c == 0:
                        link(dve.tensor_scalar(gs[:, hp], kv, dec[:, 2, hp, c:c + 1], None, ALU.mult))
                    else:
                        link(dve.tensor_scalar(gs[:, hp], gs[:, hp], dec[:, 1, hp, c:c + 1], None, ALU.mult))
                        link(dve.scalar_tensor_tensor(out=gs[:, hp], in0=kv, scalar=dec[:, 2, hp, c:c + 1], in1=gs[:, hp],
                                                      op0=ALU.mult, op1=ALU.add))
                dve.sem_inc(kv_used, 1)
                if c < NT - 1:
                    dve.wait_ge(o_ready, 2 * c + 2)
                    for hp in range(2):
                        dve.tensor_scalar(gsd[:, hp], gs[:, hp], dec[:, 0, hp, c + 1:c + 2], None, ALU.mult).then_inc(gs_ready, 1)
                else:
                    dve.sem_inc(gs_done, 1)
            dve.wait_ge(st_loaded, 32)
            for b in range(NB):
                for hp in range(2):
                    dve.tensor_scalar(sst[:, b, hp], sst[:, b, hp], ea[:, hp, b:b + 1], None, ALU.mult).then_inc(dscan, 1)
            dve.wait_ge(dscan, 8 + 2 * NB)
            for b in range(NB):
                dve.wait_ge(vb_ready, b + 1)
                for h in range(H_GLA):
                    hp, x = h // 2, slice(DK * (h % 2), DK * (h % 2) + DK)
                    up = dve.scalar_tensor_tensor(out=sst[x, b, hp], in0=banks[x, b % 2, h * DV:(h + 1) * DV],
                                                  scalar=hid[x, KG + hp, SEQ + b:SEQ + b + 1], in1=sst[x, b, hp],
                                                  op0=ALU.mult, op1=ALU.add)
                    up.then_inc(vb_used, 1)
            for h in range(H_GLA):
                v = ssum if h % 2 else rs
                dve.wait_ge(groot, h + 1)
                link(dve.reciprocal(v, v))
                link(dve.scalar_tensor_tensor(out=hid[:, VG + h], in0=hid[:, VG + h], scalar=cols[:, COL_GO:COL_GO + 1],
                                              in1=v, op0=ALU.mult, op1=ALU.mult))
                dve.wait_ge(gsilu, h + 1)
                dve.tensor_tensor(hid[:, RG + h], hid[:, RG + h], hid[:, VG + h], ALU.mult).then_inc(mix_g, 1)


        def act_gla(act, link):
            T16 = 1.0 / 16.0
            act.wait_ge(b_ready, 8)
            g4 = gb.rearrange("p h (c t) -> p h c t", c=NT)
            act.activation(dec[:, 0], g4[:, :, :, 63], ACT.Exp, scale=T16)
            act.activation(dec[:, 1], g4[:, :, :, P - 1], ACT.Exp, scale=T16)
            act.activation(ea, la[:, :, SEQ:T], ACT.Exp, scale=T16)
            link(act.activation(e2, e1, ACT.Exp, scale=-T16))
            act.activation(e1, e1, ACT.Exp, scale=T16).then_inc(e_ready, 1)
            for k in range(2):
                act.wait_ge(kf_turned, k + 1)
                act.activation(kft[:, 2 * k:2 * k + 2].rearrange("p c h d -> p (c h d)"), banks[:, k, :], ACT.Copy).then_inc(kf_made, 1)
            for c in range(NT):
                for hh in range(2):
                    act.wait_ge(o_ready, 2 * c + hh + 1)
                    act.activation(hid[:, VG + hh:VG + hh + 3:2, c * P:(c + 1) * P],
                                   banks[:, 4 + hh, 0:256].rearrange("p (c t) -> p c t", c=2), ACT.Copy).then_inc(o_kept, 1)
            act.wait_ge(os_ready, 1)
            for hh in range(2):
                act.activation(hid[:, VG + hh:VG + hh + 3:2, SEQ:T],
                               banks[:, 2 + hh, 0:2 * NB].rearrange("p (c b) -> p c b", c=2), ACT.Copy,
                               scale=DK ** -0.5).then_inc(os_kept, 1)
            act.wait_ge(os_kept, 2)
            act.wait_ge(o_kept, 8)
            for h in range(H_GLA):
                act.activation(hid[:, RG + h], hid[:, RG + h], ACT.Silu).then_inc(gsilu, 1)
            for h in range(H_GLA):
                if h >= 2:
                    act.wait_ge(gstat, h - 1)
                act.activation(sq2[:, h % 2], hid[:, VG + h], ACT.Square).then_inc(gsq, 1)
            for h in range(H_GLA):
                if h >= 2:
                    act.wait_ge(mix_g, h - 1)
                act.wait_ge(gstat, h + 1)
                act.activation(halves(ssum if h % 2 else rs), pair(4 + 2 * (h % 2)), ACT.Sqrt, bias=eps_col,
                               scale=float(D_MODEL // DV)).then_inc(groot, 1)

        def pe_gla(pe):
            pe.wait_ge(qk_ready, 2)
            for k in range(2):
                for c in range(2):
                    for hp in range(2):
                        x = (2 * k + c) * P
                        tr = pe.transpose(banks[:, k, (2 * c + hp) * P:(2 * c + hp + 1) * P], e2[:, hp, x:x + P], ident)
                tr.then_inc(kf_turned, 1)
            pe.wait_ge(kf_made, 2)
            pe.wait_ge(pt_made, 4)
            for c in range(NT):
                x = slice(c * P, (c + 1) * P)
                pe.wait_ge(att_made, 2 * c)
                for hh in range(2):
                    r_ = slice(DK * hh, DK * hh + DK)
                    for hp in range(2):
                        mm = pe.matmul(banks[:, 2 + hh, hp * P:(hp + 1) * P], e2[r_, hp, x], e1[r_, hp, x], start=True, stop=True)
                    mm.then_inc(a_ready, 1)
                pe.wait_ge(kv_used, c)
                for hh in range(2):
                    for hp in range(2):
                        h = 2 * hp + hh
                        mm = pe.matmul(banks[DK * hh:DK * hh + DK, 6, hp * P:(hp + 1) * P],
                                       kft[:, c, hp, DK * hh:DK * hh + DK], vtok[:, c, h * DV:(h + 1) * DV],
                                       start=True, stop=True)
                mm.then_inc(kv_ready, 1)
                pe.wait_ge(o_kept, 2 * c)
                pe.wait_ge(gs_ready, 2 * c)
                for hh in range(2):
                    pe.wait_ge(att_made, 2 * c + hh + 1)
                    r_ = slice(DK * hh, DK * hh + DK)
                    for hp in range(2):
                        h = 2 * hp + hh
                        o = banks[:, 4 + hh, hp * P:(hp + 1) * P]
                        mm = pe.matmul(o, vtok[:, c, h * DV:(h + 1) * DV], att[:, h], start=True, stop=(c == 0))
                        if c > 0:
                            mm = pe.matmul(o, gsd[r_, hp], e1[r_, hp, x], start=False, stop=True)
                    mm.then_inc(o_ready, 1)
            pe.wait_ge(late_loaded, 64)
            for b in range(NB):
                if b >= 2:
                    pe.wait_ge(vb_used, H_GLA * (b - 1))
                pe.matmul(banks[:, b % 2, :], pick[:, b], vts, start=True, stop=True).then_inc(vb_ready, 1)
            pe.wait_ge(vb_used, H_GLA * NB)
            for hh in range(2):
                r_ = slice(DK * hh, DK * hh + DK)
                for hp in range(2):
                    for b in range(NB):
                        mm = pe.matmul(banks[:, 2 + hh, hp * NB + b:hp * NB + b + 1], sst[r_, b, hp],
                                       hid[r_, QG + hp, SEQ + b:SEQ + b + 1], start=True, stop=True)
            mm.then_inc(os_ready, 1)
            pe.wait_ge(o_kept, 8)
            for h in range(H_GLA):
                pe.wait_ge(gsq, h + 1)
                if h >= 2:
                    pe.wait_ge(groot, h - 1)
                for a in range(2):
                    mm = pe.matmul(banks[:, 4 + 2 * (h % 2) + a, 0:HT], ones, sq2[:, h % 2, a * HT:(a + 1) * HT], start=True, stop=True)
                mm.then_inc(gstat, 1)

        UNITS = []
        for i in range(NT):
            UNITS.append(("c", i, 0))
            for r in range(R):
                UNITS += [("s", i, r), ("w", i, r)]
        before = lambda u, kinds: sum(x[0] in kinds for x in UNITS[:u])
        s_scored, c_read, c_sub, m_made, p_made = (sem("s_scored"), sem("c_read"), sem("c_sub"), sem("m_made"), sem("p_made"))
        c_exp, p_scaled, t_done, pt_kept, pv_done = sem("c_exp"), sem("p_scaled"), sem("t_done"), sem("pt_kept"), sem("pv_done")
        ao_kept = sem("ao_kept")
        amx, anm = small[:, 34:38], small[:, 38:42]
        asu, acf = small[:, 42:46], small[:, 46:50]
        amx8, acf8 = small[:, 50:58], at(o_dec + 40, 8)

        def pe_scores(pe, u):
            kind, i, r = UNITS[u]
            q = slice(i * P, (i + 1) * P)
            if u >= 2:
                k2 = UNITS[u - 2][0]
                if k2 == "c":
                    pe.wait_ge(c_read, 2 * (before(u - 2, "c") + 1))
                else:
                    pe.wait_ge(p_made, 2 * (before(u - 2, "sw") + 1))
            for g in range(G):
                rows_ = slice(D * g, D * g + D)
                b = 2 * (u % 2) + g
                if kind == "c":
                    for r in range(R):
                        mm = pe.matmul(banks[:, b, r * NCP:(r + 1) * NCP], hid[rows_, QN + r, q], kct[rows_, NB, 0:NCP],
                                       start=True, stop=True)
                else:
                    key = hid[rows_, KSL if kind == "s" else KWN, 0:(i + 1) * P]
                    mm = pe.matmul(banks[:, b, 0:(i + 1) * P], qr[rows_, r, q], key, start=True, stop=True)
            mm.then_inc(s_scored, 1)

        def pe_turn_probs(pe, u):
            kind, i, r = UNITS[u]
            pe.wait_ge(p_scaled, 2 * (u + 1))
            if u:
                pe.wait_ge(pt_kept, u)
            for g in range(G):
                if kind == "c":
                    for r in range(R):
                        tr = pe.transpose(banks[0:NCP, 4 + g, r * P:(r + 1) * P], cp[:, g, r], ident)
                else:
                    for j in range(i + 1):
                        tr = pe.transpose(banks[:, 4 + g, j * P:(j + 1) * P], pr[:, u % 2, g, j * P:(j + 1) * P], ident)
            tr.then_inc(t_done, 1)

        def pe_values(pe, u):
            kind, i, r = UNITS[u]
            if kind == "c":
                return
            pe.wait_ge(pt_kept, u + 1)
            if kind == "s" and r == 0 and i >= 1:
                pe.wait_ge(ao_kept, i)
            for g in range(G):
                o = banks[D * g:D * g + D, 6, r * P:(r + 1) * P]
                if kind == "s":
                    pe.matmul(o, vcm[0:NCP, NB, D * g:D * g + D], ptc[0:NCP, g, r * P:(r + 1) * P], start=True, stop=False,
                              skip_group_check=True)
                for j in range(i + 1):
                    mm = pe.matmul(o, kvtok[:, j, 3 if kind == "s" else 5, D * g:D * g + D],
                                   prt[:, u % 2, g, j * P:(j + 1) * P], start=False, stop=(kind == "w" and j == i),
                                   skip_group_check=True)
            mm.then_inc(pv_done, 1)

        def pe_attention(pe):
            pe.wait_ge(os_kept, 2)
            pe.wait_ge(groot, 4)
            pe_scores(pe, 0)
            pe_scores(pe, 1)
            pe_sample_start(pe)
            assert len(UNITS) == 4 + 4 * NB
            for u in range(len(UNITS)):
                pe_turn_probs(pe, u)
                if u + 2 < len(UNITS):
                    pe_scores(pe, u + 2)
                if u >= 4:
                    pe_sample_values(pe, u // 4 - 1, u % 4)
                if u:
                    pe_values(pe, u - 1)
            pe_values(pe, len(UNITS) - 1)
            pe_sample_end(pe)

        def dve_attention(dve, link):
            dve.wait_ge(late_loaded, 64)

            def maxima(u):
                kind, i, r = UNITS[u]
                b = 2 * (u % 2)
                dve.wait_ge(s_scored, u + 1)
                if kind == "c":
                    if i:
                        dve.wait_ge(t_done, u - 2 * R)
                    add = cmp_add[:, i].unsqueeze(1).broadcast_to([P, R, NCP])
                    for g in range(G):
                        dve.tensor_tensor(cp[:, g], banks[:, b + g, 0:R * NCP].rearrange("p (r n) -> p r n", r=R), add,
                                          ALU.add).then_inc(c_read, 1)
                    dve.wait_ge(c_read, 2 * (i + 1))
                    c8 = cp.rearrange("p g r n -> p (g r) n")
                    link(dve.tensor_reduce(amx8, c8, AX_X, ALU.max))
                    dve.tensor_tensor(c8, c8, amx8.unsqueeze(2).broadcast_to([P, G * R, NCP]), ALU.subtract).then_inc(c_sub, 1)
                else:
                    d = banks[:, b:b + 2, i * P:(i + 1) * P]
                    link(dve.tensor_tensor(d, d, causal_add.unsqueeze(1).broadcast_to([P, 2, P]), ALU.add))
                    m = slice(2 * (u % 2), 2 * (u % 2) + 2)
                    link(dve.tensor_reduce(amx[:, m], banks[:, b:b + 2, 0:(i + 1) * P], AX_X, ALU.max))
                    dve.tensor_scalar(anm[:, m], amx[:, m], -SCALE, None, ALU.mult).then_inc(m_made, 1)

            def scales(u):
                kind, i, r = UNITS[u]
                if kind == "c":
                    dve.wait_ge(c_exp, i + 1)
                    c8 = cp.rearrange("p g r n -> p (g r) n")
                    link(dve.tensor_reduce(acf8, c8, AX_X, ALU.add))
                    link(dve.reciprocal(acf8, acf8))
                    link(dve.tensor_tensor(acf8, acf8, gates[:, i, 0:24:3], ALU.mult))
                    link(dve.tensor_tensor(c8, c8, cmp_ok[:, i].unsqueeze(1).broadcast_to([P, G * R, NCP]), ALU.mult))
                    dve.tensor_tensor(c8, c8, acf8.unsqueeze(2).broadcast_to([P, G * R, NCP]), ALU.mult).then_inc(p_scaled, 2)
                else:
                    m = 2 * (u % 2)
                    dve.wait_ge(p_made, 2 * (before(u, "sw") + 1))
                    link(dve.reciprocal(acf[:, m:m + 2], asu[:, m:m + 2]))
                    br = 1 if kind == "s" else 2
                    link(dve.tensor_tensor(acf[:, m:m + 2], acf[:, m:m + 2], gates[:, i, 3 * r + br:24:12], ALU.mult))
                    for g in range(G):
                        w = pr[:, u % 2, g, 0:(i + 1) * P]
                        dve.tensor_scalar(w, w, acf[:, m + g:m + g + 1], None, ALU.mult).then_inc(p_scaled, 1)

            maxima(0)
            maxima(1)
            for u in range(len(UNITS)):
                scales(u)
                if u + 2 < len(UNITS):
                    maxima(u + 2)

        def act_attention(act):
            def exps(u):
                kind, i, r = UNITS[u]
                if kind == "c":
                    act.wait_ge(c_sub, i + 1)
                    act.activation(cp.rearrange("p g r n -> p (g r n)"), cp.rearrange("p g r n -> p (g r n)"), ACT.Exp,
                                   scale=SCALE).then_inc(c_exp, 1)
                    return
                act.wait_ge(m_made, before(u, "sw") + 1)
                if u >= 2:
                    act.wait_ge(t_done, u - 1)
                for g in range(G):
                    m = 2 * (u % 2) + g
                    act.activation(pr[:, u % 2, g, 0:(i + 1) * P], banks[:, m, 0:(i + 1) * P], ACT.Exp,
                                   bias=anm[:, m:m + 1], scale=SCALE, accum_out=asu[:, m:m + 1]).then_inc(p_made, 1)

            def keep_out(i):
                act.wait_ge(pv_done, 2 * R * (i + 1))
                act.activation(hid[:, QN:QN + R, i * P:(i + 1) * P], banks[:, 6, :].rearrange("p (r t) -> p r t", r=R),
                               ACT.Copy).then_inc(ao_kept, 1)

            exps(0)
            exps(1)
            for u in range(len(UNITS)):
                kind, i, r = UNITS[u]
                act.wait_ge(t_done, u + 1)
                if kind == "c":
                    if i:
                        act.wait_ge(pv_done, 2 * R * i - 1)
                    act.activation(ptc[0:NCP], banks[0:NCP, 4:6, :], ACT.Copy).then_inc(pt_kept, 1)
                else:
                    if before(u, "sw") >= 2:
                        act.wait_ge(pv_done, before(u - 1, "sw") if UNITS[u - 2][0] != "c" else before(u - 2, "sw"))
                    act.activation(prt[:, u % 2, :, 0:(i + 1) * P], banks[:, 4:6, 0:(i + 1) * P], ACT.Copy).then_inc(pt_kept, 1)
                if kind == "c" and i:
                    keep_out(i - 1)
                if u + 2 < len(UNITS):
                    exps(u + 2)
            keep_out(NT - 1)

        vbuf = [at(o_b + 2560 * s, 8, 2, P) for s in range(2)]
        vwbuf = [at(o_b + 2560 * s + 2048, NT, P) for s in range(2)]
        v_loaded = [sem("v_loaded0"), sem("v_loaded1")]
        so_used, so_ready, mix_s = sem("so_used"), sem("so_ready"), sem("mix_s")

        def sp_values(sp):
            cache = ins["cache_nsa"][0].rearrange("n (p t) k g d -> n p t (k g d)", t=2)
            sp.wait_ge(o_ready, 2 * NT)
            sp.wait_ge(o_kept, 2 * NT)
            sp.wait_ge(gla_stored, 32)

            def sample(b, s):
                for pg in range(NPG):
                    n = sp.value_load(ptab[0:1, bass.ds(b * NPG + pg, 1)], min_val=0, max_val=cache.shape[0] - 1)
                    sp.dma_start(vbuf[s][64 * (pg % 2):64 * (pg % 2) + 64, pg // 2],
                                 cache[bass.ds(n, 1), :, :, 3 * P:4 * P].rearrange("o p t c -> p (o t) c")).then_inc(v_loaded[s], 16)
                sp.dma_start(vwbuf[s], ins["state_win"][0, bass.ds(b, 1)].rearrange("o (w p) v g d -> p (o w) v (g d)", p=P)[:, :, 1])\
                    .then_inc(v_loaded[s], 16)

            sample(0, 0)
            sample(1, 1)
            with sp.Fori(1, NB // 2) as i:
                for s in range(2):
                    sp.wait_ge(so_used, 2 * i + s - 1)
                    sample(2 * i + s, s)

        def add(pe, o, w, x, start=False, stop=False):
            return pe.matmul(o, w, x, start=start, stop=stop, skip_group_check=True)

        def pe_sample_start(pe):
            add(pe, banks[:, 7, 0:64], kvs[:, 3], pnt[:, 0], start=True)
            for b in range(NB):
                add(pe, banks[:, 7, 8 * b:8 * b + 8], vcm[0:NCS, b], pcgt[0:NCS, 8 * b:8 * b + 8])

        def pe_sample_values(pe, b, part):
            s = b % 2
            if part == 0:
                pe.wait_ge(v_loaded[s], 16 * (NPG + 1) * (b // 2 + 1))
            o = banks[:, 7, 8 * b:8 * b + 8]
            for j in range(4 * part, 4 * part + 4):
                add(pe, o, vbuf[s][:, j // 2, j % 2], pts[:, j, 8 * b:8 * b + 8])
            mm = add(pe, o, vwbuf[s][:, part], ptw[:, part, 8 * b:8 * b + 8])
            if part == 3:
                mm.then_inc(so_used, 1)

        def pe_sample_end(pe):
            add(pe, banks[:, 7, 0:64], kvs[:, 5], pnt[:, 1], stop=True).then_inc(so_ready, 1)

        def dve_sample_out(dve):
            dve.wait_ge(so_ready, 1)
            for g in range(G):
                x = slice(D * g, D * g + D)
                dve.tensor_copy(hid[x, QN:QN + R, SEQ:T],
                                banks[x, 7, 0:64].rearrange("p (b h r) -> p h r b", h=G, r=R)[:, g]).then_inc(mix_s, 1)

        p_loaded, p_turned2, p_kept = sem("p_loaded"), sem("p_turned2"), sem("p_kept")
        sig_made, ple_y = sem("sig_made"), sem("ple_y")
        wp_loaded = sem("wp_loaded")
        yo_turned, yo_a, yo_v, y_stored = sem("yo_turned"), sem("yo_a"), sem("yo_v"), sem("y_stored")
        o_kv = o_kvtok
        pstage = at(o_kv, 5, PLE_DIM)
        pT = at(o_kv + 5 * PLE_DIM, 2, T)
        wp = at(o_wout, 2, D_MODEL)
        yo = at(o_n, 2, D_MODEL)

        def pool_stores(pool):
            pool.wait_ge(kept_a, 8)
            pool.wait_ge(kept_v, 7)
            rp = outs["nsa_rows_prompt"].rearrange("l b (i p) k g d -> p (l b i) (k g d)", p=P)
            pool.dma_start(rp, kvtok[:, :, 0:4].rearrange("p i k c -> p i (k c)")).then_inc(rows_stored, 16)
            wpo = outs["win_prompt"].rearrange("l b (i p) k g d -> p (l b i) (k g d)", p=P)
            pool.dma_start(wpo, kvtok[:, :, 4:6].rearrange("p i k c -> p i (k c)")).then_inc(rows_stored, 16)
            pool.dma_start(outs["nsa_rows_sample"].rearrange("l b s k g d -> (l b s) (k g d)"),
                           kvs[:, 0:4].rearrange("p k c -> p (k c)")).then_inc(rows_stored, 16)
            ws = outs["win_sample"].rearrange("l b s k g d -> (l b) s (k g d)")
            pool.dma_start(ws[:, WINDOW - 1, :], kvs[:, 4:6].rearrange("p k c -> p (k c)")).then_inc(rows_stored, 16)
            pool.wait_ge(gates_made, 1)
            pool.dma_start(gates_h, gates_s.rearrange("b (h k) -> b h k", k=3)).then_inc(gates_moved, 16)
            pool.dma_start(ws[:, 0:WINDOW - 1, :], ins["state_win"].rearrange("l b s k g d -> (l b) s (k g d)")[:, 1:WINDOW, :])\
                .then_inc(rows_stored, 16)
            pool_cache(pool)
            pool.wait_ge(gs_done, 1)
            for hh in range(2):
                pool.dma_start(outs["gla_prompt"].rearrange("l b (c h) d e -> h d (l b c) e", h=2)[hh],
                               gs[DK * hh:DK * hh + DK]).then_inc(gla_stored, 16)
            pool.wait_ge(vb_used, H_GLA * NB)
            for hh in range(2):
                pool.dma_start(outs["gla_sample"][0].rearrange("b (c h) d e -> h d (b c) e", h=2)[hh],
                               sst[DK * hh:DK * hh + DK].rearrange("p b c e -> p (b c) e")).then_inc(st_stored, 16)
            pool.wait_ge(rows_stored, 80)
            pool.wait_ge(gla_stored, 32)
            pool.wait_ge(st_stored, 32)


        def sp_out_first(sp):
            sp_out_weights(sp, (0, 1))

        def sp_out_last(sp):
            sp_out_weights(sp, (2, 3))

        def sp_out_weights(sp, groups):
            wo = ins["w_mix_out"][0]
            for q in groups:
                sp.wait_ge(rest_scored, 1) if q < 2 else sp.wait_ge(pv_done, 2 * R * NT)
                c = slice(q * GW, (q + 1) * GW)
                sp.dma_start(win[:, q, 0:4], wo[0:512, c].rearrange("(k p) n -> p k n", p=P)).then_inc(win_loaded[q], 16)
                for g in range(G):
                    sp.dma_start(win[D * g:D * g + D, q, 4:8],
                                 wo[512 + g * 256:512 + (g + 1) * 256, c].rearrange("(r d) n -> d r n", d=D)).then_inc(win_loaded[q], 16)

        def sp_rest(sp):
            sp.wait_ge(rows_stored, 80)
            sp.wait_ge(so_ready, 1)
            sp.wait_ge(pv_done, 2 * R * NT)
            sp.dma_start(pstage[:, 0:4], ins["p_prompt"][0, 0].rearrange("(i p) d -> p i d", p=P)).then_inc(p_loaded, 16)
            sp.dma_start(pstage[0:NB, 4], ins["p_sample"][0].rearrange("b s d -> (b s) d")).then_inc(p_loaded, 16)
            sp.wait_ge(st_stored, 32)
            sp_ffn_out(sp, 1, ins["ffn2_w_out"][0], first=True)
            sp_ffn_in(sp, 1, ins["ffn2_w_in"][0], lambda e: e.wait_ge(y_ready, 16))
            sp_ffn_out(sp, 1, ins["ffn2_w_out"][0], first=False)
            wg = ins["ple_w_gate"][0].rearrange("(k p) n -> p k n", p=P)
            for q in range(4):
                sp.wait_ge(u_ready, 44 if q < 2 else 42)
                sp.dma_start(win[:, q], wg[:, :, q * GW:(q + 1) * GW]).then_inc(win_loaded[q], 16)
            sp.wait_ge(y_ready, 22)
            sp.dma_start(wp, ins["ple_w_proj"][0].rearrange("(k p) n -> p k n", p=P)).then_inc(wp_loaded, 16)
            yp = outs["y_prompt"][0].rearrange("(i p) d -> p i d", p=P)
            for i in range(NT + 1):
                sp.wait_ge(yo_a, i + 1)
                sp.wait_ge(yo_v, i + 1)
                if i < NT:
                    sp.dma_start(yp[:, i], yo[:, i % 2]).then_inc(y_stored, 16)
                else:
                    sp.dma_start(outs["y_sample"].rearrange("b s d -> (b s) d"), yo[0:NB, i % 2]).then_inc(y_stored, 16)
                sp.wait_ge(y_stored, 16 * (i + 1))

        def pe_out(pe):
            pe.wait_ge(ao_kept, NT)
            pe.wait_ge(mix_s, 2)
            pe.wait_ge(mix_g, 4)
            for m in range(KC):
                if m % 2 == 0:
                    pe.wait_ge(win_loaded[m // 2], win_base["out"][m // 2] + 48)
                if m >= 4:
                    pe.wait_ge(y_kept, Y0["out"] + m - 3)
                pe_chunk(pe, 2 * (m % 4), lambda k: win[:, m // 2, k, m % 2 * P:(m % 2 + 1) * P], hid[:, RG:RG + KC], KC)\
                    .then_inc(y_ready, 1)
            pe.wait_ge(y_kept, Y0["out"] + KC)
            pe_post_stats(pe, 1)
            pe.wait_ge(p_loaded, 32)
            for c in range(2):
                for i in range(NT):
                    tr = pe.transpose(banks[:, 2 + c, i * P:(i + 1) * P], pstage[:, i, c * P:(c + 1) * P], ident)
            for c in range(2):
                tr = pe.transpose(banks[:, 4, c * NB:(c + 1) * NB], pstage[0:NB, 4, c * P:(c + 1) * P], ident[0:NB, 0:NB])
            tr.then_inc(p_turned2, 1)
            pe.wait_ge(p_kept, 1)

        def act_embedding(act):
            act.wait_ge(p_turned2, 1)
            act.activation(pT[:, :, 0:SEQ], banks[:, 2:4, :], ACT.Copy)
            act.activation(pT[:, :, SEQ:T], banks[:, 4, 0:2 * NB].rearrange("p (c t) -> p c t", c=2), ACT.Copy).then_inc(p_kept, 1)

        def pe_ple(pe):
            pe.wait_ge(wp_loaded, 16)
            for m in range(KC):
                if m % 2 == 0:
                    pe.wait_ge(win_loaded[m // 2], win_base["ple"][m // 2] + 16)
                if m == 0:
                    pe.wait_ge(rs_read, 7)
                if m >= 2:
                    pe.wait_ge(ple_y, m - 1)
                n_wait = (lambda k: pe.wait_ge(n_ready, 3 * KC + k + 1)) if m == 0 else None
                b = 4 * (m % 2)
                pe_chunk(pe, b, lambda k: win[:, m // 2, k, m % 2 * P:(m % 2 + 1) * P], nT, KC, n_wait).then_inc(g_ready, 1)
                pe_chunk(pe, b + 2, lambda k: wp[:, k, m * P:(m + 1) * P], pT, 2).then_inc(u_ready, 1)

        def act_ple(act):
            def square(m):
                act.wait_ge(ple_y, m + 1)
                act.wait_ge(ysq_used, Y0["ple"] + m - 1)
                act.activation(sq2[:, m % 2], hid[:, m], ACT.Square).then_inc(y_kept, 1)

            for m in range(KC):
                act.wait_ge(g_ready, 44 + m + 1)
                if m >= 2:
                    act.wait_ge(ple_y, m - 1)
                act.activation(halves(gtmp2 if m % 2 else gtmp), pair(4 * (m % 2)), ACT.Sigmoid).then_inc(sig_made, 1)
                if m:
                    square(m - 1)
            square(KC - 1)

        def dve_ple(dve):
            y0 = Y0["ple"]
            def total(m):
                dve.wait_ge(y_kept, y0 + m + 1)
                dve.wait_ge(ysq_used, y0 + m)
                if m == 0:
                    dve.tensor_copy(ssum, sq2[:, 0]).then_inc(ysq_used, 1)
                else:
                    dve.tensor_tensor(ssum, ssum, sq2[:, m % 2], ALU.add).then_inc(ysq_used, 1)

            for m in range(KC):
                dve.wait_ge(u_ready, 44 + m + 1)
                dve.wait_ge(sig_made, m + 1)
                dve.tensor_tensor(halves(hid[:, m]), halves(gtmp2 if m % 2 else gtmp), pair(4 * (m % 2) + 2), ALU.mult).then_inc(ple_y, 1)
                if m:
                    total(m - 1)
            total(KC - 1)
            dve.wait_ge(ysq_used, y0 + KC)
            dve.sem_inc(ssum_ready, 1)

        def pe_outputs(pe):
            pe.wait_ge(h_ready, 5 * KC)
            pe.wait_ge(rs_read, 8)
            for i in range(NT + 1):
                m = P if i < NT else NB
                if i >= 2:
                    pe.wait_ge(yo_a, i - 1)
                    pe.wait_ge(yo_v, i - 1)
                for c in range(KC):
                    tr = pe.transpose(banks[0:m, 2 * (i % 2) + c // 4, c % 4 * P:(c % 4 + 1) * P], hT[:, c, i * P:i * P + m], ident)
                tr.then_inc(yo_turned, 1)

        def keep_outputs(eng, copy, sem_, half):
            for i in range(NT + 1):
                m = P if i < NT else NB
                eng.wait_ge(yo_turned, i + 1)
                if i >= 2:
                    eng.wait_ge(y_stored, 16 * (i - 1))
                copy(yo[0:m, i % 2, half * 512:(half + 1) * 512], banks[0:m, 2 * (i % 2) + half, :]).then_inc(sem_, 1)

        @block.sync
        def _(sp):
            xs = at(o_wout, 5, D_MODEL)
            sp.dma_start(xs[:, 0:4], ins["x_prompt"][0].rearrange("(i p) d -> p i d", p=P)).then_inc(x_loaded, 16)
            sp.dma_start(xs[0:NB, 4], ins["x_sample"].rearrange("b s d -> (b s) d")).then_inc(x_loaded, 16)
            sp.dma_start(ident, consts["ident"]).then_inc(x_loaded, 16)
            rows = at(o_n, P)
            for i, name in enumerate(gname):
                sp.dma_start(rows[KC * i:KC * (i + 1)], ins[name][0].rearrange("(k p) -> k p", p=P)).then_inc(rows_loaded, 16)
            sp.dma_start(rows[COL_GO:COL_GO + 1], ins["gla_out_norm"]).then_inc(rows_loaded, 16)
            sp.dma_start(rows[COL_BA:COL_BA + 2], ins["b_gla_a"][0].rearrange("(k p) -> k p", p=P)).then_inc(rows_loaded, 16)
            for o, name in ((COL_PK, "cmp_pos_k"), (COL_PV, "cmp_pos_v")):
                sp.dma_start(rows[o:o + 16], ins[name][0].rearrange("(m t) d -> m (t d)", t=2)).then_inc(rows_loaded, 16)
            sp.dma_start(causal_t, consts["causal_t"]).then_inc(const_loaded, 16)
            sp.dma_start(causal_add, consts["causal_add"]).then_inc(const_loaded, 16)
            sp_ffn_in(sp, 0, ins["ffn1_w_in"][0], lambda e: None)
            sp.wait_ge(x_turned, KC)
            sp_ffn_out(sp, 0, ins["ffn1_w_out"][0], first=True)
            sp_ffn_out(sp, 0, ins["ffn1_w_out"][0], first=False)
            wm = ins["w_mix_in"][0].rearrange("(k p) n -> p k n", p=P)
            for j in range(PROJ_G):
                if j < 4:
                    sp.wait_ge(u_ready, 22 if j < 2 else 20)
                else:
                    sp.wait_ge(proj_ready, 2 * (j - 3))
                if j in (6, 7):
                    for rr in range(2):
                        for g in range(G):
                            c0 = C_QN + g * R * D + (2 * (j - 6) + rr) * D
                            sp.dma_start(win[:, j % 4, :, rr * P + g * D:rr * P + (g + 1) * D],
                                         wm[:, :, c0:c0 + D]).then_inc(win_loaded[j % 4], 16)
                else:
                    c0 = j * GW if j < 6 else C_KV + (j - 8) * GW
                    sp.dma_start(win[:, j % 4], wm[:, :, c0:c0 + GW]).then_inc(win_loaded[j % 4], 16)
            sp_mixer_small(sp)
            sp_cache(sp)
            sp_window(sp)
            sp_late(sp)
            sp_out_first(sp)
            sp_values(sp)
            sp_out_last(sp)
            sp_rest(sp)

        def pe_pre_stats(pe, k):
            for c in range(KC):
                pe.wait_ge(sq_ready, KC * k + c + 1)
                for a in range(2):
                    last = pe.matmul(banks[:, a, 0:HT], ones[:, :], sq[:, c, a * HT:(a + 1) * HT],
                                     start=(c == 0), stop=(c == KC - 1))
            last.then_inc(stat_ready, 1)

        def pe_post_stats(pe, k):
            pe.wait_ge(ssum_ready, k + 1)
            for a in range(2):
                last = pe.matmul(banks[:, a, 0:HT], ones[:, :], ssum[:, a * HT:(a + 1) * HT], start=True, stop=True)
            last.then_inc(stat_ready, 1)

        def pe_chunk(pe, b, w, src, nk, first_wait=None):
            for k in range(nk):
                if first_wait:
                    first_wait(k)
                for a in range(2):
                    last = pe.matmul(banks[:, b + a, 0:HT], w(k), src[:, k, a * HT:(a + 1) * HT],
                                     start=(k == 0), stop=(k == nk - 1))
            return last

        def pe_ffn(pe, n):
            base = win_base[f"ffn{n + 1}"]

            def group(j, s, i, first=False):
                pe.wait_ge(win_loaded[2 * s], base[2 * s] + 16 * (i + 1))
                pe.wait_ge(win_loaded[2 * s + 1], base[2 * s + 1] + 16 * (i + 1))
                for c in range(2):
                    if first:
                        if c == 0:
                            pe.wait_ge(rs_read, 2 * n * 2 + 1)
                    else:
                        pe.wait_ge(hid_ready, 22 * n + 2 * j + c - 1)
                    n_wait = (lambda k: pe.wait_ge(n_ready, KC * (2 * n) + k + 1)) if first and c == 0 else None
                    pe_chunk(pe, 4 * c, lambda k: win[:, 2 * s, k, c * P:(c + 1) * P], nT, KC, n_wait).then_inc(g_ready, 1)
                    pe_chunk(pe, 4 * c + 2, lambda k: win[:, 2 * s + 1, k, c * P:(c + 1) * P], nT, KC).then_inc(u_ready, 1)

            group(0, 0, 0, True)
            group(1, 1, 0)
            with pe.Fori(1, 5) as i:
                for s in range(2):
                    group(2 * i + s, s, i)
            group(10, 0, 5)
            pe.wait_ge(hid_ready, 22 * (n + 1))
            for m in range(KC):
                if m % 2 == 0:
                    pe.wait_ge(wout_loaded[m // 2 % 2], 32 * n + 16 * (m // 4 + 1))
                if m >= 4:
                    pe.wait_ge(y_kept, Y0[f"ffn{n + 1}"] + m - 3)
                pe_chunk(pe, 2 * (m % 4), lambda k: wout[:, m // 2 % 2, k, m % 2 * P:(m % 2 + 1) * P], hid, FC)\
                    .then_inc(y_ready, 1)


        @block.tensor
        def _(pe):
            xs = at(o_wout, 5, D_MODEL)
            pe.wait_ge(x_loaded, 48)
            for c in range(KC):
                pe.transpose(banks[:, 7, c * NB:(c + 1) * NB], xs[0:NB, 4, c * P:(c + 1) * P], ident[0:NB, 0:NB])
            for c in range(KC):
                if c >= 4:
                    pe.wait_ge(h_ready, c - 3)
                for i in range(NT):
                    last = pe.transpose(banks[:, c % 4, i * P:(i + 1) * P], xs[:, i, c * P:(c + 1) * P], ident)
                last.then_inc(x_turned, 1)
            pe.wait_ge(rows_loaded, 12 * 16)
            pe.transpose(banks[:, 6, 0:NCOL], at(o_n, P)[0:NCOL], ident[0:NCOL, 0:NCOL]).then_inc(cols_turned, 1)
            pe.wait_ge(init_done, 1)
            pe.wait_ge(h_ready, KC)
            pe_pre_stats(pe, 0)
            pe_ffn(pe, 0)
            pe.wait_ge(y_kept, 8)
            pe_post_stats(pe, 0)
            pe.wait_ge(rs_read, 2)
            pe_pre_stats(pe, 1)
            for j in range(PROJ_G):
                s = j % 4
                turn = sum(64 if q in (6, 7) else 16 for q in range(j + 1) if q % 4 == s)
                pe.wait_ge(win_loaded[s], win_base["proj"][s] + turn)
                for c in range(2):
                    m = 2 * j + c
                    if m == 0:
                        pe.wait_ge(rs_read, 3)
                    if m >= 4:
                        pe.wait_ge(proj_kept_v if m % 2 else proj_kept_a, (m - 4) // 2 + 1)
                    n_wait = (lambda k: pe.wait_ge(n_ready, KC + k + 1)) if m == 0 else None
                    pe_chunk(pe, 2 * (m % 4), lambda k: win[:, s, k, c * P:(c + 1) * P], nT, KC, n_wait)\
                        .then_inc(proj_ready, 1)
            pe_mixer_prep(pe)
            pe_turn(pe)
            pe_position(pe)
            pe_cache(pe)
            pe_window(pe)
            pe_softmaxes(pe)
            pe_gla(pe)
            pe_attention(pe)
            pe_out(pe)
            pe_pre_stats(pe, 2)
            pe_ffn(pe, 1)
            pe.wait_ge(y_kept, 24)
            pe_post_stats(pe, 2)
            pe.wait_ge(rs_read, 6)
            pe_pre_stats(pe, 3)
            pe_ple(pe)
            pe_post_stats(pe, 3)
            pe_outputs(pe)

        def act_root(act, k):
            act.wait_ge(stat_ready, k + 1)
            act.activation(halves(rs), pair(0), ACT.Sqrt, bias=eps_col).then_inc(rs_read, 1)

        def act_pre_squares(act, k):
            for c in range(KC):
                act.wait_ge(h_ready, KC * k + c + 1)
                act.activation(sq[:, c], hT[:, c], ACT.Square).then_inc(sq_ready, 1)

        def act_ffn(act, n):
            def chunk(k, c, first=False):
                act.wait_ge(g_ready, k + 1)
                if not first:
                    act.wait_ge(hid_ready, k - 1)
                act.activation(halves(gtmp2 if c else gtmp), pair(4 * c), ACT.Silu).then_inc(silu_ready, 1)

            for c in range(2):
                chunk(22 * n + c, c, first=(n == 0))
            with act.Fori(1, 11) as j:
                for c in range(2):
                    chunk(22 * n + 2 * j + c, c)
            act_keep_y(act, f"ffn{n + 1}")

        def act_keep_y(act, phase):
            y0 = Y0[phase]
            for m in range(KC):
                act.wait_ge(y_ready, y0 + m + 1)
                act.activation(halves(nT[:, m]), pair(2 * (m % 4)), ACT.Copy)
                if y0 + m >= 2:
                    act.wait_ge(ysq_used, y0 + m - 1)
                act.activation(halves(sq2[:, m % 2]), pair(2 * (m % 4)), ACT.Square).then_inc(y_kept, 1)

        @block.scalar
        def _(act):
            steps = [0]

            def link(ins_):
                steps[0] += 1
                ins_.then_inc(act_step, 1)
                act.wait_ge(act_step, steps[0])
                return ins_

            act_pre_squares(act, 0)
            act_root(act, 0)
            act_ffn(act, 0)
            act_root(act, 1)
            act_pre_squares(act, 1)
            act_root(act, 2)
            for m in range(0, 2 * PROJ_G, 2):
                act.wait_ge(proj_ready, m + 1)
                act.activation(halves(hid[:, m]), pair(2 * (m % 4)), ACT.Copy).then_inc(proj_kept_a, 1)
            act_mixer_prep(act, link)
            keep_turned(act, lambda o, i: act.activation(o, i, ACT.Copy), kept_a, 0)
            act_gates(act)
            act_cache(act, link)
            act_window(act)
            act_softmaxes(act)
            act_gla(act, link)
            act_attention(act)
            act_keep_y(act, "out")
            act_root(act, 3)
            act_embedding(act)
            act_pre_squares(act, 2)
            act_root(act, 4)
            act_ffn(act, 1)
            act_root(act, 5)
            act_pre_squares(act, 3)
            act_root(act, 6)
            act_ple(act)
            act_root(act, 7)
            keep_outputs(act, lambda o, i: act.activation(o, i, ACT.Copy), yo_a, 0)

        def dve_helpers(dve):
            steps = [0]

            def link(ins_):
                steps[0] += 1
                ins_.then_inc(dve_step, 1)
                dve.wait_ge(dve_step, steps[0])

            return link

        def dve_rs(dve, link, k):
            dve.wait_ge(rs_read, k + 1)
            link(dve.reciprocal(rs, rs))

        def dve_pre_norm(dve, link, k, gi):
            dve_rs(dve, link, k)
            for c in range(KC):
                dve.scalar_tensor_tensor(out=nT[:, c], in0=hT[:, c], scalar=gains[:, gi, c:c + 1], in1=rs,
                                         op0=ALU.mult, op1=ALU.mult).then_inc(n_ready, 1)

        def dve_sum_squares(dve, phase, k):
            y0 = Y0[phase]
            for m in range(KC):
                dve.wait_ge(y_kept, y0 + m + 1)
                if m == 0:
                    dve.tensor_copy(ssum, sq2[:, 0]).then_inc(ysq_used, 1)
                else:
                    dve.wait_ge(ysq_used, y0 + m)
                    last = dve.tensor_tensor(ssum, ssum, sq2[:, m % 2], ALU.add).then_inc(ysq_used, 1)
            dve.wait_ge(ysq_used, y0 + KC)
            dve.sem_inc(ssum_ready, 1)

        def dve_post_norm(dve, link, k, gi, y=None):
            dve_rs(dve, link, k)
            y = nT if y is None else y
            for c in range(KC):
                link(dve.scalar_tensor_tensor(out=y[:, c], in0=y[:, c], scalar=gains[:, gi, c:c + 1], in1=rs,
                                              op0=ALU.mult, op1=ALU.mult))
                dve.tensor_tensor(hT[:, c], hT[:, c], y[:, c], ALU.add).then_inc(h_ready, 1)

        def dve_ffn(dve, n):
            def chunk(k, kk, c):
                dve.wait_ge(u_ready, k + 1)
                dve.wait_ge(silu_ready, k + 1)
                dve.tensor_tensor(hid[:, kk], gtmp, pair(4 * c + 2), ALU.mult).then_inc(hid_ready, 1)
            with dve.Fori(0, 11) as j:
                for c in range(2):
                    k = 2 * j + c
                    dve.wait_ge(u_ready, 22 * n + k + 1)
                    dve.wait_ge(silu_ready, 22 * n + k + 1)
                    o = at(o_hid, FC, 2, HT)[:, bass.ds(k, 1)].rearrange("p k a t -> p (k a) t")
                    dve.tensor_tensor(o, halves(gtmp2 if c else gtmp), pair(4 * c + 2), ALU.mult).then_inc(hid_ready, 1)

        @block.vector
        def _(dve):
            link = dve_helpers(dve)
            link(dve.memset(eps_col, EPS))
            dve.memset(ones, 1.0 / D_MODEL).then_inc(init_done, 1)
            dve.wait_ge(x_turned, 1)
            link(dve.tensor_copy(hT[:, :, SEQ:T], banks[:, 7, 0:KC * NB].rearrange("p (c t) -> p c t", c=KC)))
            for c in range(KC):
                dve.wait_ge(x_turned, c + 1)
                dve.tensor_copy(hT[:, c, 0:SEQ], banks[:, c % 4, :]).then_inc(h_ready, 1)
            dve.wait_ge(cols_turned, 1)
            link(dve.tensor_copy(cols, banks[:, 6, 0:NCOL]))
            for gi in (1, 5):
                link(dve.tensor_scalar(gains[:, gi], gains[:, gi], 0.5, None, ALU.mult))
            dve.wait_ge(h_ready, KC)
            dve_pre_norm(dve, link, 0, 0)
            dve_ffn(dve, 0)
            dve_sum_squares(dve, "ffn1", 0)
            dve_post_norm(dve, link, 1, 1)
            dve.wait_ge(h_ready, 2 * KC)
            dve_pre_norm(dve, link, 2, 2)
            for m in range(1, 2 * PROJ_G, 2):
                dve.wait_ge(proj_ready, m + 1)
                dve.tensor_copy(halves(hid[:, m]), pair(2 * (m % 4))).then_inc(proj_kept_v, 1)
            dve_mixer_prep(dve, link)
            keep_turned(dve, dve.tensor_copy, kept_v, 1)
            dve_cache(dve, link)
            dve_softmaxes(dve, link)
            dve_gla(dve, link)
            dve_attention(dve, link)
            dve_sample_out(dve)
            dve_sum_squares(dve, "out", 1)
            dve_post_norm(dve, link, 3, 3)
            dve.wait_ge(h_ready, 3 * KC)
            dve_pre_norm(dve, link, 4, 4)
            dve_ffn(dve, 1)
            dve_sum_squares(dve, "ffn2", 2)
            dve_post_norm(dve, link, 5, 5)
            dve.wait_ge(h_ready, 4 * KC)
            dve_pre_norm(dve, link, 6, 6)
            dve_ple(dve)
            dve_post_norm(dve, link, 7, 7, hid)
            keep_outputs(dve, dve.tensor_copy, yo_v, 1)

        @block.gpsimd
        def _(pool):
            pool_mixer_prep(pool)
            pool_stores(pool)



OUTS = [("y_prompt", (1, SEQ, D_MODEL)), ("y_sample", (NB, 1, D_MODEL)),
        ("nsa_rows_prompt", (1, 1, SEQ, 4, G, D)), ("win_prompt", (1, 1, WINDOW, 2, G, D)),
        ("gla_prompt", (1, 1, H_GLA, DK, DV)), ("nsa_rows_sample", (1, NB, 1, 4, G, D)),
        ("win_sample", (1, NB, WINDOW, 2, G, D)), ("gla_sample", (1, NB, H_GLA, DK, DV))]


def kernel(**inputs):
    import concourse.bacc as bacc
    from concourse.bass_utils import run_bass_kernel_spmd

    nc = bacc.Bacc("TRN2", target_bir_lowering=False, num_devices=1)
    arrays, ins, consts, outs = {}, {}, {}, {}
    for name, a in inputs.items():
        a = np.ascontiguousarray(a)
        arrays["in_" + name] = a
        ins[name] = nc.dram_tensor("in_" + name, a.shape, mybir.dt.from_np(a.dtype), kind="ExternalInput").ap()
    for name, a in constants().items():
        arrays["const_" + name] = a
        consts[name] = nc.dram_tensor("const_" + name, a.shape, F32, kind="ExternalInput").ap()
    for name, shape in OUTS:
        outs[name] = nc.dram_tensor(name, shape, F32, kind="ExternalOutput").ap()
    build(nc, ins, outs, consts)
    r = run_bass_kernel_spmd(nc, [arrays], core_ids=[0])
    return tuple(r.results[0][name] for name, _ in OUTS)
```

```python
from contextlib import ExitStack

import numpy as np

import concourse.bass as bass
from concourse import mybir

F32 = mybir.dt.float32
I32 = mybir.dt.int32
ACT = mybir.ActivationFunctionType
ALU = mybir.AluOpType
AX_X = mybir.AxisListType.X

P = 128
D_MODEL, D_FF, PLE_DIM = 1024, 2816, 256
SEQ, NB = 512, 8
T = SEQ + NB
HT = T // 2
KC = D_MODEL // P
FC = D_FF // P
GW = 256
EPS = 1e-6
H_GLA, DK, DV, RANK = 4, 64, 128, 16
H_NSA, G, R, D = 8, 2, 4, 64
PAST, PAGE = 2048, 128
NPG = PAST // PAGE
CMP_LEN, STRIDE, HIDDEN = 32, 16, 128
SELB, N_SEL, WINDOW = 64, 16, 512
NCP = (SEQ - CMP_LEN) // STRIDE + 1
NCS = (PAST + 1 - CMP_LEN) // STRIDE + 1
NSB = PAST // SELB + 1
SCALE = D ** -0.5
NEG = -1e30
C_QG, C_KG, C_VG, C_RG = 0, 256, 512, 1024
C_LR, C_QN, C_KV, C_GT = 1536, 1552, 2064, 2832
COL_GO, COL_BA, COL_PK, COL_PV = 64, 65, 67, 83
NCOL = 99
QG, KG, VG, RG, QN, KCM, VCM, KSL, VSL, KWN, VWN = 0, 2, 4, 8, 12, 16, 17, 18, 19, 20, 21
NT = SEQ // P


def constants():
    f = np.float32
    c = {}
    c["ident"] = np.eye(P, dtype=f)
    s, t = np.arange(P)[:, None], np.arange(P)[None, :]
    c["causal_t"] = (s <= t).astype(f)
    c["causal_add"] = np.where(t <= s, 0.0, NEG).astype(f)
    half = 8
    inv = (f(500000.0) ** (-np.arange(half, dtype=f) * f(2.0) / f(16))).astype(f)
    pos = np.concatenate([np.arange(SEQ), np.full(NB, PAST)]).astype(f)
    ang = (pos[:, None] * inv[None, :]).astype(f)
    cos, sin = np.cos(ang).astype(f), np.sin(ang).astype(f)
    rc, rs, sw = np.ones((P, T), f), np.zeros((P, T), f), np.zeros((P, P), f)
    for g in range(2):
        for j in range(half):
            a, b = g * D + j, g * D + half + j
            rc[a], rc[b] = cos[:, j], cos[:, j]
            rs[a], rs[b] = -sin[:, j], sin[:, j]
            sw[b, a] = sw[a, b] = 1.0
    c["rope_cos"], c["rope_sin"], c["rope_swap"] = rc, rs, sw
    n = np.arange(NCP)
    q = np.arange(SEQ)
    ok = (n[None, :] * STRIDE + CMP_LEN - 1 <= q[:, None]).astype(f)
    c["cmp_ok"] = ok.reshape(NT, P, NCP).transpose(1, 0, 2).copy()
    c["cmp_add"] = ((c["cmp_ok"] - 1) * f(1e30)).astype(f)
    st, ss = np.arange(NCS) * STRIDE, np.arange(NSB) * SELB
    c["overlap"] = ((st[:, None] < ss[None, :] + SELB) & (st[:, None] + CMP_LEN > ss[None, :])).astype(f)
    r = np.arange(NB * H_NSA)
    c["group_sum"] = (r[:, None] // R == r[None, :] // R).astype(f)
    c["own_row"] = (r[:, None] // H_NSA == np.arange(NB)[None, :]).astype(f)
    forced = np.zeros(NSB, f)
    forced[[0, NSB - 2, NSB - 1]] = 1
    c["forced"] = np.tile(np.stack([1 - forced, forced * f(1e4)]), (NB * H_NSA, 1, 1)).astype(f)
    c["earlier"] = np.tile((np.arange(NSB)[None, :] < np.arange(NSB)[:, None]).astype(f).reshape(1, -1), (NB * H_NSA, 1))
    c["pick"] = np.repeat(np.eye(NB, dtype=f)[:, :, None], P, 2).copy()
    return c


CONSTS = {k: v.shape for k, v in constants().items()}


def build(nc, ins, outs, consts):
    ctx = ExitStack()
    with ctx:
        def sb(name, cols, dt=F32, parts=P):
            return ctx.enter_context(nc.sbuf_tensor(name, [parts, cols], dt))

        def sem(name):
            return ctx.enter_context(nc.semaphore(name))

        banks = ctx.enter_context(nc.psum_tensor("banks", [P, 8, 512], F32))

        ARENA = 53080
        arena = sb("arena", ARENA)
        ptab = sb("page_table", NB * NPG, I32, 1)[:, :]
        top = [0]

        def cut(cols):
            o = top[0]
            top[0] += cols
            assert top[0] <= ARENA, top[0]
            return o

        def at(o, *dims):
            n = int(np.prod(dims))
            v = arena[:, o:o + n]
            if len(dims) == 1:
                return v
            names = "abcde"[:len(dims)]
            return v.rearrange(f"p ({' '.join(names)}) -> p {' '.join(names)}",
                               **{k: d for k, d in zip(names, dims)})

        o_h, o_n, o_hid = cut(KC * T), cut(KC * T), cut(FC * T)
        o_win, o_wout = cut(2 * 2 * KC * GW), cut(2 * FC * GW)
        hT = at(o_h, KC, T)
        nT = at(o_n, KC, T)
        hid = at(o_hid, FC, T)
        win = at(o_win, 4, KC, GW)
        wout = at(o_wout, 2, FC, GW)

        ident = at(cut(P), P)
        ones = at(cut(P), P)
        causal_t = at(cut(P), P)
        causal_add = at(cut(P), P)
        cols = at(cut(NCOL), NCOL)
        gains = cols[:, 0:8 * KC].rearrange("p (i k) -> p i k", k=KC)
        o_tmp = top[0]
        gtmp = at(cut(T), T)
        gtmp2 = at(cut(T), T)
        sq2 = at(cut(2 * T), 2, T)
        ssum = at(cut(T), T)
        rs = at(cut(T), T)
        small = at(cut(64), 64)
        eps_col = small[:, 0:1]
        ckv = small[:, 1:3]
        sq = at(o_hid, KC, T)

        kct = at(cut((NB + 1) * NCS), NB + 1, NCS)
        vcm = at(cut((NB + 1) * P), NB + 1, P)
        qb_raw, qb_rot = at(cut(NB * 72), NB, 72), at(cut(NB * 72), NB, 72)
        o_qbraw, o_qbrot = top[0] - 2 * NB * 72, top[0] - NB * 72
        qb_cur = at(cut(64), 64)
        o_kvtok = top[0]
        kvtok = at(cut(NT * 6 * P), NT, 6, P)
        kvs = at(cut(6 * P), 6, P)[0:NB]
        vts = at(cut(H_GLA * DV), H_GLA * DV)[0:NB]
        ag = at(cut(T), T)
        wa2 = at(cut(256), 256)
        la = at(cut(2 * T), 2, T)
        keys_g1 = at(top[0] - 2 * T, 2, SEQ)
        gates = at(cut(NT * 24), NT, 24)
        gates_s = at(cut(24), 24)[0:NB]
        gates_h = at(cut(3), 3)[0:64]
        overlap = at(cut(NSB), NSB)
        group_sum = at(cut(64), 64)
        own_row = at(cut(NB), NB)
        forced = at(cut(2 * NSB), 2, NSB)
        w1 = at(o_wout, 2, 16, HIDDEN)
        pages = at(o_wout + 4096, 4, 2, 2, 3 * P)
        kvr = [at(o, 2, 4, 2, D) for o in (o_n + R * T, o_n + R * T + 1024, o_tmp, o_tmp + 1024)]
        kwin = [at(o, NT, P) for o in (o_tmp + 2048, o_tmp + 2560, o_wout + 5120, o_wout + 5632)]
        hk = at(o_wout + 10240, 2, 2 * NCS)
        w2 = at(o_wout + 10748, 2, D)
        rope_c, rope_s = at(o_wout + 8828, T), at(o_wout + 9348, T)
        rope_swap = at(o_wout + 9868, P)
        agw = at(o_wout + 9996, KC, 56)
        assert 10748 + 2 * D <= 2 * FC * GW and 2048 + 2 * SEQ <= 6 * T
        xk, xv = at(o_win, 2, 1024), at(o_win + 2048, 2, 1024)
        xs_ = at(o_win + 4096, 16, P)
        vtok = at(o_win + 6144, NT, H_GLA * DV)
        qr = at(o_n, R, T)
        ssel = at(o_n + R * T, PAST + 1)[0:64]
        o_b = o_wout
        gb = at(o_b, 2, SEQ)
        e1, e2 = at(o_b + 1024, 2, SEQ), at(o_b + 2048, 2, SEQ)
        kft = at(o_b + 3072, NT, 2, P)
        gs, gsd = at(o_b + 4096, 2, DV), at(o_b + 4352, 2, DV)
        att = at(o_b + 4608, H_GLA, P)
        cp = [at(o, G, R, NCP) for o in (o_b + 5120, o_b + 8688)]
        ptc = [at(o, G, R * P) for o in (o_b + 5368, o_b + 9777)]
        cmp_ok, cmp_add = at(o_b + 6392, NT, NCP), at(o_b + 6516, NT, NCP)
        sst = at(o_b + 6640, NB, 2, DV)
        earlier = at(o_b + 8688, NSB, NSB)[0:64]
        pr = at(o_win + 4096, 2, G, 512)
        pick = at(o_win + 4096, NB, P)[0:NB]
        qg_pair = at(o_win + 5168, 2, NB, 2)
        prt = at(o_win + 6144, 2, G, 512)
        pts = at(o_hid + KCM * T, 16, 64)
        sw = at(o_hid + VSL * T, WINDOW + 1)[0:64]
        o_m = o_hid + VWN * T
        pcs, pcg = at(o_m, NCS)[0:64], at(o_m + NCS, NCS)[0:64]
        pct, pcgt = at(o_m + 256, 64), at(o_m + 320, 64)
        imp1, imp = at(o_m + 384, NSB)[0:64], at(o_m + 417, NSB)[0:64]
        rank = at(o_m + 450, NSB)[0:64]
        cmps = at(o_tmp, 2, NSB, NSB)[0:64]

        gname = ["ffn1_norm_pre", "ffn1_norm_post", "mix_norm_pre", "mix_norm_post",
                 "ffn2_norm_pre", "ffn2_norm_post", "ple_norm_pre", "ple_norm_post"]

        x_loaded, const_loaded = sem("x_loaded"), sem("const_loaded")
        rows_loaded = sem("rows_loaded")
        cols_turned, cols_made = sem("cols_turned"), sem("cols_made")
        g_scaled, silu_scaled = sem("g_scaled"), sem("silu_scaled")
        x_turned = sem("x_turned")
        h_ready = sem("h_ready")
        sq_ready = sem("sq_ready")
        ssum_ready = sem("ssum_ready")
        ysq_used = sem("ysq_used")
        stat_ready = sem("stat_ready")
        n_ready = sem("n_ready")
        win_loaded = [sem(f"win_loaded{i}") for i in range(4)]
        g_ready, u_ready = sem("g_ready"), sem("u_ready")
        silu_ready, hid_ready = sem("silu_ready"), sem("hid_ready")
        wout_loaded = [sem(f"wout_loaded{i}") for i in range(2)]
        y_ready = sem("y_ready")
        y_kept = sem("y_kept")
        proj_ready, proj_kept_a, proj_kept_v = sem("proj_ready"), sem("proj_kept_a"), sem("proj_kept_v")
        rs_read = sem("rs_read")
        init_done = sem("init_done")
        dve_step, act_step, pool_step = sem("dve_step"), sem("act_step"), sem("pool_step")

        block = ctx.enter_context(nc.Block())

        def pair(b):
            return banks[:, b:b + 2, 0:HT]

        def halves(v):
            return v.rearrange("p (a t) -> p a t", a=2)

        NG = FC * P // GW
        PROJ_G = 11
        win_base = {}
        cnt = [0, 0, 0, 0]
        for phase in ("ffn1", "proj", "out", "ffn2", "ple"):
            win_base[phase] = list(cnt)
            if phase.startswith("ffn"):
                for j in range(NG):
                    cnt[2 * (j % 2)] += 16
                    cnt[2 * (j % 2) + 1] += 16
            elif phase == "proj":
                for j in range(PROJ_G):
                    cnt[j % 4] += 64 if j in (6, 7) else 16
            elif phase == "out":
                for j in range(4):
                    cnt[j] += 48
            else:
                for j in range(4):
                    cnt[j] += 16

        def sp_ffn_in(sp, n, w_in, prev_use):
            base = win_base[f"ffn{n + 1}"]
            src = w_in.rearrange("(k p) n -> p k n", p=P)

            def group(j, s, i):
                sp.dma_start(win[:, 2 * s], src[:, :, bass.ds(j * GW, GW)]).then_inc(win_loaded[2 * s], 16)
                sp.dma_start(win[:, 2 * s + 1], src[:, :, bass.ds(D_FF + j * GW, GW)]).then_inc(win_loaded[2 * s + 1], 16)

            prev_use(sp)
            group(0, 0, 0)
            group(1, 1, 0)
            with sp.Fori(1, 5) as i:
                for s in range(2):
                    sp.wait_ge(u_ready, 22 * n + 4 * i + 2 * s - 2)
                    group(2 * i + s, s, i)
            sp.wait_ge(u_ready, 22 * n + 18)
            group(10, 0, 5)

        def sp_ffn_out(sp, n, w_out, first):
            src = w_out.rearrange("(k p) n -> p k n", p=P)
            for q in (range(2) if first else range(2, 4)):
                if q >= 2:
                    sp.wait_ge(y_ready, Y0[f"ffn{n + 1}"] + 2 * (q - 1))
                sp.dma_start(wout[:, q % 2], src[:, :, q * GW:(q + 1) * GW]).then_inc(wout_loaded[q % 2], 16)

        Y0 = {"ffn1": 0, "out": 8, "ffn2": 16, "ple": 24}

        agw_zeroed, small_loaded = sem("agw_zeroed"), sem("small_loaded")
        rope_loaded = sem("rope_loaded")
        swapped, roped, cos_made = sem("swapped"), sem("roped"), sem("cos_made")
        z_ready, z_read, z_log, la_ready = sem("z_ready"), sem("z_read"), sem("z_log"), sem("la_ready")
        turned, kept_a, kept_v = sem("turned"), sem("kept_a"), sem("kept_v")
        w1_loaded, pages_loaded = sem("w1_loaded"), [sem(f"pages_loaded{i}") for i in range(4)]
        table_loaded = sem("table_loaded")
        ring_filled = sem("ring_filled")
        ring_a, ring_v = sem("ring_a"), sem("ring_v")
        ckv_ready, ckv_made = sem("ckv_ready"), sem("ckv_made")
        ckv_row_kept = sem("ckv_row_kept")
        ckv_row = at(o_wout + 10240, 2 * HIDDEN)[0:1]
        qcur_ready, sel_scored = sem("qcur_ready"), sem("sel_scored")
        sel_kept, ea_made = sem("sel_kept"), sem("ea_made")
        gates_made, gates_moved, rows_stored = sem("gates_made"), sem("gates_moved"), sem("rows_stored")

        ROPE = [KSL, KWN, QN, QN + 1, QN + 2, QN + 3]

        def rope_out(q):
            return hid[:, ROPE[q]] if q < 2 else qr[:, q - 2]

        def sp_mixer_small(sp):
            sp.dma_start(wa2[0:RANK], ins["w_gla_a2"][0]).then_inc(small_loaded, 16)
            sp.dma_start(overlap[0:NCS], consts["overlap"]).then_inc(small_loaded, 16)
            sp.dma_start(group_sum[0:64], consts["group_sum"]).then_inc(small_loaded, 16)
            sp.dma_start(own_row[0:64], consts["own_row"]).then_inc(small_loaded, 16)
            sp.dma_start(forced[0:64], consts["forced"]).then_inc(small_loaded, 16)
            sp.wait_ge(y_ready, 8)
            sp.wait_ge(agw_zeroed, 1)
            wm = ins["w_mix_in"][0].rearrange("(k p) n -> p k n", p=P)
            with nc.allow_non_contiguous_dma(reason="narrow columns"):
                sp.dma_start(agw[:, :, 0:RANK], wm[:, :, C_LR:C_LR + RANK]).then_inc(rope_loaded, 16)
                sp.dma_start(agw[:, :, 32:56], wm[:, :, C_GT:C_GT + 24]).then_inc(rope_loaded, 16)
            sp.dma_start(rope_c, consts["rope_cos"]).then_inc(rope_loaded, 16)
            sp.dma_start(rope_s, consts["rope_sin"]).then_inc(rope_loaded, 16)
            sp.dma_start(rope_swap, consts["rope_swap"]).then_inc(rope_loaded, 16)
            for i, (a, b) in enumerate((("w_cmp_k1", "w_cmp_k2"), ("w_cmp_v1", "w_cmp_v2"))):
                sp.dma_start(w1[:, i], ins[a][0].rearrange("(m p) h -> p m h", p=P)).then_inc(w1_loaded, 16)
                sp.dma_start(w2[:, i], ins[b][0]).then_inc(w1_loaded, 16)

        def sp_cache(sp):
            cache = ins["cache_nsa"][0].rearrange("n (p t) k g d -> n p t (k g d)", t=2)
            sp.dma_start(ptab, ins["page_table"].rearrange("b (o n) -> o (b n)", o=1)).then_inc(table_loaded, 16)
            sp.wait_ge(table_loaded, 16)

            def quarter(b, qd, first=False):
                if not first:
                    sp.wait_ge(ring_filled, 16 * b + 3 * qd - 13)
                elif qd == 2:
                    sp.wait_ge(roped, 6)
                    sp.wait_ge(proj_ready, 23)
                for tile in range(2):
                    for hh in range(2):
                        n = sp.value_load(ptab[0:1, bass.ds(b * NPG + qd * 4 + tile * 2 + hh, 1)],
                                          min_val=0, max_val=cache.shape[0] - 1)
                        sp.dma_start(pages[64 * hh:64 * hh + 64, qd, tile],
                                     cache[bass.ds(n, 1), :, :, 0:3 * P].rearrange("o p t c -> p (o t) c"))\
                            .then_inc(pages_loaded[qd], 16)

            for qd in range(4):
                quarter(0, qd, first=True)
            sp_stores(sp)
            with sp.Fori(1, NB) as b:
                for qd in range(4):
                    quarter(b, qd)

        def sp_stores(sp):
            sp.wait_ge(kept_a, 8)
            sp.wait_ge(kept_v, 7)
            rp = outs["nsa_rows_prompt"].rearrange("l b (i p) k g d -> p (l b i) (k g d)", p=P)
            sp.dma_start(rp, kvtok[:, :, 0:4].rearrange("p i k c -> p i (k c)")).then_inc(rows_stored, 16)
            wpo = outs["win_prompt"].rearrange("l b (i p) k g d -> p (l b i) (k g d)", p=P)
            sp.dma_start(wpo, kvtok[:, :, 4:6].rearrange("p i k c -> p i (k c)")).then_inc(rows_stored, 16)
            sp.dma_start(outs["nsa_rows_sample"].rearrange("l b s k g d -> (l b s) (k g d)"),
                           kvs[:, 0:4].rearrange("p k c -> p (k c)")).then_inc(rows_stored, 16)
            ws = outs["win_sample"].rearrange("l b s k g d -> (l b) s (k g d)")
            sp.dma_start(ws[:, WINDOW - 1, :], kvs[:, 4:6].rearrange("p k c -> p (k c)")).then_inc(rows_stored, 16)
            sp.wait_ge(gates_made, 1)
            sp.dma_start(gates_h, gates_s.rearrange("b (h k) -> b h k", k=3)).then_inc(gates_moved, 16)
            sp.dma_start(ws[:, 0:WINDOW - 1, :], ins["state_win"].rearrange("l b s k g d -> (l b) s (k g d)")[:, 1:WINDOW, :])\
                .then_inc(rows_stored, 16)

        kvr_made, kvr_begun = sem("kvr_made"), sem("kvr_begun")

        def pool_cache(pool):
            pool.wait_ge(proj_ready, 23)
            pool.wait_ge(roped, 6)

            def quarter(b, qd, first=False):
                pool.wait_ge(pages_loaded[qd], 64 * b + 64)
                if not first:
                    pool.wait_ge(ring_filled, 16 * b + 3 * qd - 13)
                    pool.sem_inc(kvr_begun, 1)
                for tile in range(2):
                    cp_ = pool.tensor_copy(kvr[qd][:, tile], pages[:, qd, tile, :, 0:4 * D].rearrange("p t (c d) -> p c t d", d=D))
                cp_.then_inc(kvr_made, 1)

            for qd in range(4):
                quarter(0, qd, first=True)
            with pool.Fori(1, NB) as b:
                for qd in range(4):
                    quarter(b, qd)

        def pe_mixer_prep(pe):
            pe.wait_ge(rope_loaded, 80)
            pe.wait_ge(proj_kept_a, 10)
            for k in range(KC):
                for a in range(2):
                    last = pe.matmul(banks[0:56, 4 + a, 0:HT], agw[:, k, :], nT[:, k, a * HT:(a + 1) * HT],
                                     start=(k == 0), stop=(k == KC - 1))
            last.then_inc(proj_ready, 1)
            pe.wait_ge(proj_kept_a, 12)
            pe.wait_ge(proj_kept_v, 11)
            for q in range(6):
                if q >= 4:
                    pe.wait_ge(roped, q - 3)
                for a in range(2):
                    last = pe.matmul(banks[:, 2 * (q % 4) + a, 0:HT], rope_swap, hid[:, ROPE[q], a * HT:(a + 1) * HT],
                                     start=True, stop=True)
                last.then_inc(swapped, 1)
            pe.wait_ge(small_loaded, 80)
            for hp in range(2):
                pe.wait_ge(roped, 3 + hp)
                for a in range(2):
                    last = pe.matmul(banks[:, 4 + 2 * hp + a, 0:HT], wa2[0:RANK, hp * P:(hp + 1) * P],
                                     ag[0:RANK, a * HT:(a + 1) * HT], start=True, stop=True)
                last.then_inc(z_ready, 1)

        def pool_mixer_prep(pool):
            pool.wait_ge(y_ready, 8)
            pool.memset(agw[:, :, RANK:32], 0.0).then_inc(agw_zeroed, 1)
            pool.wait_ge(rope_loaded, 80)
            pool.wait_ge(proj_kept_a, 12)
            pool.wait_ge(proj_kept_v, 11)
            for q in range(6):
                if q >= 2:
                    pool.wait_ge(roped, q - 1)
                pool.tensor_tensor(sq2[:, q % 2], hid[:, ROPE[q]], rope_c, ALU.mult).then_inc(cos_made, 1)

        log_tmp = (rs, ssum)

        def act_log_decay(act, link):
            for hp in range(2):
                act.wait_ge(z_read, hp + 1)
                link(act.activation(log_tmp[hp], la[:, hp], ACT.Abs))
            for hp in range(2):
                link(act.activation(log_tmp[hp], log_tmp[hp], ACT.Exp, scale=-1.0))
            for hp in range(2):
                act.activation(log_tmp[hp], log_tmp[hp], ACT.Ln, bias=1.0).then_inc(z_log, 1)

        def dve_mixer_prep(dve, link):
            dve.wait_ge(rope_loaded, 80)
            for q in range(6):
                dve.wait_ge(swapped, q + 1)
                if q >= 2:
                    dve.wait_ge(roped, q - 1)
                v = gtmp2 if q % 2 else gtmp
                link(dve.tensor_tensor(halves(v), pair(2 * (q % 4)), halves(rope_s), ALU.mult))
                dve.wait_ge(cos_made, q + 1)
                dve.tensor_tensor(rope_out(q), v, sq2[:, q % 2], ALU.add).then_inc(roped, 1)
            for hp in range(2):
                dve.wait_ge(z_ready, hp + 1)
                dve.tensor_scalar(halves(la[:, hp]), pair(4 + 2 * hp), cols[:, COL_BA + hp:COL_BA + hp + 1], None,
                                  ALU.add).then_inc(z_read, 1)
            link(dve.memset(arena[:, o_qbraw:o_qbraw + 2 * NB * 72], 0.0))
            dve.wait_ge(roped, 6)
            for o, src in ((qb_raw, hid[:, QN:QN + R, SEQ:T]), (qb_rot, qr[:, :, SEQ:T])):
                for g in range(G):
                    link(dve.tensor_copy(o[D * g:D * g + D, :, R * g:R * g + R],
                                         src[D * g:D * g + D].rearrange("p r b -> p b r")))

        def dve_log_decay(dve):
            for hp in range(2):
                dve.wait_ge(z_log, hp + 1)
                dve.scalar_tensor_tensor(out=la[:, hp], in0=la[:, hp], scalar=0.0, in1=log_tmp[hp],
                                         op0=ALU.min, op1=ALU.subtract).then_inc(la_ready, 1)

        def turn_jobs():
            jobs = []
            for i in range(NT):
                t0 = i * P
                for hf in range(2):
                    jobs.append(([(c * P, hid[:, KCM + 3 * hf + c, t0:t0 + P], P) for c in range(3)],
                                 kvtok[:, i, 3 * hf:3 * hf + 3].rearrange("p k c -> p (k c)"), 3 * P, P))
                jobs.append(([(c * P, hid[:, VG + c, t0:t0 + P], P) for c in range(4)], vtok[:, i], 4 * P, P))
            jobs.append(([(c * P, hid[:, KCM + c, SEQ:T], NB) for c in range(4)],
                         kvs[:, 0:4].rearrange("p k c -> p (k c)"), 4 * P, NB))
            jobs.append(([(c * P, hid[:, KCM + 4 + c, SEQ:T], NB) for c in range(2)],
                         kvs[:, 4:6].rearrange("p k c -> p (k c)"), 2 * P, NB))
            jobs.append(([(c * P, hid[:, VG + c, SEQ:T], NB) for c in range(4)], vts, 4 * P, NB))
            return jobs

        JOBS = turn_jobs()

        def pe_turn(pe):
            for n, (moves, _, _, m) in enumerate(JOBS):
                if n >= 8:
                    pe.wait_ge(kept_v if n % 2 else kept_a, (n - 8) // 2 + 1)
                elif n == 0:
                    pe.wait_ge(roped, 6)
                    pe.wait_ge(z_read, 2)
                for c, src, _ in moves:
                    last = pe.transpose(banks[0:m, n % 8, c:c + P], src, ident)
                last.then_inc(turned, 1)
            pe.wait_ge(kept_v, 4)
            for i in range(NT):
                pe.transpose(banks[:, 7, 24 * i:24 * i + 24], ag[32:56, i * P:(i + 1) * P], ident[32:56, 32:56])
            pe.transpose(banks[0:NB, 7, 96:120], ag[32:56, SEQ:T], ident[32:56, 32:56]).then_inc(turned, 1)

        def keep_turned(eng, copy, sem_, parity):
            for n, (_, dst, width, m) in enumerate(JOBS):
                if n % 2 == parity:
                    eng.wait_ge(turned, n + 1)
                    copy(dst, banks[0:m, n % 8, 0:width]).then_inc(sem_, 1)

        def act_gates(act):
            act.wait_ge(turned, len(JOBS) + 1)
            act.activation(gates.rearrange("p i c -> p (i c)"), banks[:, 7, 0:96], ACT.Sigmoid)
            act.activation(gates_s, banks[0:NB, 7, 96:120], ACT.Sigmoid).then_inc(gates_made, 1)

        def free(pe, b, u, first):
            if not first or u >= 4:
                pe.wait_ge(ring_v if u % 2 else ring_a, 8 * b + (u - 4) // 2 + 1)

        def pe_hidden(pe, bank, kind, n):
            src = xv if kind else xk
            for m in range(16):
                rhs = src.rearrange("p g (n s) -> p g n s", s=8)[:, :, m // 8:m // 8 + n, m % 8]
                mm = pe.matmul(banks[:, bank, 0:2 * n].rearrange("p (g n) -> p g n", g=G), w1[:, kind, m, :], rhs,
                               start=(m == 0), stop=(m == 15))
            mm.then_inc(ring_filled, 1)

        def pe_second(pe, bank, kind, n):
            for g in range(G):
                h = hk[:, kind, g * n:(g + 1) * n]
                if kind == 0:
                    mm = pe.matmul(banks[D * g:D * g + D, bank, 0:n], w2[:, 0, :], h, start=True, stop=True)
                else:
                    mm = pe.matmul(banks[0:n, bank, g * D:g * D + D], h, w2[:, 1, :], start=True, stop=True)
            mm.then_inc(ring_filled, 1)

        def pe_position(pe):
            pe.wait_ge(w1_loaded, 64)
            pe.wait_ge(kept_a, len(JOBS) // 2 + 1)
            pe.wait_ge(kept_v, len(JOBS) // 2)
            for kind, o in ((0, COL_PK), (1, COL_PV)):
                for m in range(16):
                    mm = pe.matmul(banks[0:1, 4, kind * HIDDEN:(kind + 1) * HIDDEN], cols[:, o + m:o + m + 1], w1[:, kind, m, :],
                                   start=(m == 0), stop=(m == 15))
            mm.then_inc(ckv_ready, 1)
            pe.wait_ge(ckv_row_kept, 1)
            for kind in range(2):
                tr = pe.transpose(banks[:, 4, kind:kind + 1], ckv_row[:, kind * HIDDEN:(kind + 1) * HIDDEN], ident[0:1, 0:1])
            tr.then_inc(ckv_ready, 1)

        def pe_sample(pe, b, first=False, last_b=False):
            for qd in range(4):
                pe.wait_ge(kvr_made, 4 * b + qd + 1)
                for kind in range(3):
                    u = 3 * qd + kind
                    free(pe, b, u, first)
                    for tile in range(2):
                        for x in range(2):
                            src = (kvr[qd][:, tile, 2 * kind + x].rearrange("p t d -> p (t d)") if kind < 2
                                   else pages[:, qd, tile, x, 2 * P:3 * P])
                            c = x * 256 + tile * P if kind < 2 else (2 * tile + x) * P
                            tr = pe.transpose(banks[:, u % 4, c:c + P], src, ident)
                    tr.then_inc(ring_filled, 1)
            if first:
                pe.wait_ge(ckv_made, 1)
            pe.wait_ge(qcur_ready, b + 1)
            pe.wait_ge(ring_a, 8 * b + 5)
            pe.wait_ge(ring_v, 8 * b + 3)

            def scores(js):
                for j in js:
                    sc = pe.matmul(banks[0:64, 4 + j, :], qb_cur, xs_[:, 4 * j:4 * j + 4, :],
                                   start=first, stop=last_b, skip_group_check=True)
                return sc

            scores(range(3))
            pe.wait_ge(ring_a, 8 * b + 6)
            pe.wait_ge(ring_v, 8 * b + 6)
            pe_hidden(pe, 0, 0, NCS)
            pe_hidden(pe, 2, 1, NCS)
            scores(range(3, 4)).then_inc(sel_scored, 1)
            pe.wait_ge(ring_a, 8 * b + 7)
            pe_second(pe, 1, 0, NCS)
            pe.wait_ge(ring_a, 8 * b + 8)
            pe_second(pe, 3, 1, NCS)

        def pe_cache(pe):
            pe_sample(pe, 0, first=True)
            with pe.Fori(1, NB - 1) as b:
                pe_sample(pe, b)
            pe_sample(pe, NB - 1, last_b=True)
            for kind, src in ((0, KCM), (1, VCM)):
                free(pe, NB, kind, False)
                for g in range(G):
                    for t in range(2):
                        mm = pe.matmul(banks[D * t:D * t + D, kind, g * 256:(g + 1) * 256], ident[:, D * g:D * g + D],
                                       hid[:, src, 0:SEQ].rearrange("p (n t) -> p n t", t=2)[:, :, t],
                                       start=True, stop=True)
                mm.then_inc(ring_filled, 1)
            pe.wait_ge(ring_a, 8 * NB + 1)
            pe.wait_ge(ring_v, 8 * NB + 1)
            pe_hidden(pe, 2, 0, NCP)
            pe.wait_ge(ring_a, 8 * NB + 2)
            pe_second(pe, 3, 0, NCP)
            pe_hidden(pe, 0, 1, NCP)
            pe.wait_ge(ring_a, 8 * NB + 3)
            pe_second(pe, 1, 1, NCP)

        def read_turn(copy, b, u):
            kind, qd = u % 3, u // 3
            if kind < 2:
                return copy((xv if kind else xk)[:, :, qd * 256:(qd + 1) * 256],
                            banks[:, u % 4, :].rearrange("p (g c) -> p g c", g=G)).then_inc(ring_v if u % 2 else ring_a, 1)
            return copy(xs_[:, 4 * qd:4 * qd + 4].rearrange("p j c -> p (j c)"), banks[:, u % 4, :])\
                .then_inc(ring_v if u % 2 else ring_a, 1)

        def act_gelu(act, bank, kind, n):
            act.activation(hk[:, kind, 0:2 * n], banks[:, bank, 0:2 * n], ACT.Gelu_apprx_tanh,
                           bias=ckv[:, kind:kind + 1]).then_inc(ring_a, 1)

        def act_cache(act, link):
            act.wait_ge(ckv_ready, 1)
            act.activation(ckv_row, banks[0:1, 4, 0:2 * HIDDEN], ACT.Copy).then_inc(ckv_row_kept, 1)
            act.wait_ge(ckv_ready, 2)
            link(act.activation(ckv, banks[:, 4, 0:2], ACT.Copy))
            act.sem_inc(ckv_made, 1)

            def copy(o, i):
                return act.activation(o, i, ACT.Copy)

            with act.Fori(0, NB) as b:
                for u in range(0, 12, 2):
                    act.wait_ge(ring_filled, 16 * b + u + 1)
                    read_turn(copy, b, u)
                for kind in range(2):
                    act.wait_ge(ring_filled, 16 * b + 13 + kind)
                    act_gelu(act, 2 * kind, kind, NCS)
            act.wait_ge(ring_filled, 16 * NB + 1)
            copy(xk[:, :, 0:256], banks[:, 0, :].rearrange("p (g c) -> p g c", g=G)).then_inc(ring_a, 1)
            act.wait_ge(sel_scored, NB)
            act.wait_ge(kvr_made, 4 * NB)
            for k in range(4):
                act.activation(ssel[:, k * 512:(k + 1) * 512], banks[0:64, 4 + k, :], ACT.Copy).then_inc(sel_kept, 1)
            for kind in range(2):
                act.wait_ge(ring_filled, 16 * NB + 3 + 2 * kind)
                act_gelu(act, 2 - 2 * kind, kind, NCP)

        def dve_cache(dve, link):
            def copy(o, i):
                return dve.tensor_copy(o, i)

            dve.wait_ge(ckv_made, 1)
            def sample(b, first=False):
                if not first:
                    dve.wait_ge(sel_scored, b)
                dve.tensor_copy(qb_cur, at(o_qbrot, 9, 64)[:, bass.ds(b, 1)].rearrange("p o c -> p (o c)")).then_inc(qcur_ready, 1)
                for u in range(1, 12, 2):
                    dve.wait_ge(ring_filled, 16 * b + u + 1)
                    read_turn(copy, b, u)
                dve.wait_ge(ring_filled, 16 * b + 15)
                copy(kct[:, bass.ds(b, 1)].rearrange("p o c -> p (o c)"), banks[:, 1, 0:NCS]).then_inc(ring_v, 1)
                dve.wait_ge(ring_filled, 16 * b + 16)
                copy(vcm[0:NCS, bass.ds(b, 1)].rearrange("p o c -> p (o c)"), banks[0:NCS, 3, 0:P]).then_inc(ring_v, 1)

            sample(0, first=True)
            with dve.Fori(1, NB) as b:
                sample(b)
            dve.wait_ge(ring_filled, 16 * NB + 2)
            copy(xv[:, :, 0:256], banks[:, 1, :].rearrange("p (g c) -> p g c", g=G)).then_inc(ring_v, 1)
            dve.wait_ge(ring_filled, 16 * NB + 4)
            link(dve.memset(kct[:, NB, 0:G * NCP], 0.0))
            link(copy(kct[0:D, NB, 0:NCP], banks[0:D, 3, 0:NCP]))
            copy(kct[D:P, NB, NCP:G * NCP], banks[D:P, 3, 0:NCP]).then_inc(ring_v, 1)
            dve.wait_ge(ring_filled, 16 * NB + 6)
            copy(vcm[0:NCP, NB], banks[0:NCP, 1, 0:P]).then_inc(ring_v, 1)

        kwin_loaded = [sem(f"kwin_loaded{i}") for i in range(4)]
        kwin_turned, kwt_made, win_scored = sem("kwin_turned"), sem("kwt_made"), sem("win_scored")
        rest_scored = sem("rest_scored")
        kwts = at(o_wout + 4096, 2, 512)

        def sp_window(sp):
            sp.wait_ge(la_ready, 2)
            for b in range(NB):
                if b == 2:
                    sp.wait_ge(sel_scored, NB)
                if b == 4:
                    sp_late(sp)
                if b >= 4:
                    sp.wait_ge(kwin_turned, b - 3)
                sp.dma_start(kwin[b % 4], ins["state_win"][0, b].rearrange("(w p) v g d -> p w v (g d)", p=P)[:, :, 0])\
                    .then_inc(kwin_loaded[b % 4], 16)

        def pe_window(pe):
            for b in range(NB + 1):
                if b < NB:
                    pe.wait_ge(kwin_loaded[b % 4], 16 * (b // 4 + 1))
                    if b == 0:
                        pe.wait_ge(ring_a, 8 * NB + 3)
                        pe.wait_ge(ring_v, 8 * NB + 3)
                    elif b >= 2:
                        pe.wait_ge(kwt_made, b - 1)
                    for w in range(NT):
                        tr = pe.transpose(banks[:, b % 2, w * P:(w + 1) * P], kwin[b % 4][:, w], ident)
                    tr.then_inc(kwin_turned, 1)
                if b >= 1:
                    if b == 1:
                        pe.wait_ge(pick_loaded, 16)
                        pe.wait_ge(sel_kept, 4)
                    elif b >= 3:
                        pe.wait_ge(vb_used, H_GLA * (b - 2))
                    pe.matmul(banks[:, 4 + (b - 1) % 2, :], pick[:, b - 1], vts, start=True, stop=True).then_inc(vb_ready, 1)
                    pe.wait_ge(kwt_made, b)
                    q = at(o_qbrot, 9, 64)[:, b - 1]
                    mm = pe.matmul(banks[0:64, 2, :], q, kwts[:, (b - 1) % 2], start=(b == 1), stop=(b == NB))
                    mm.then_inc(win_scored, 1)
            for col, key in ((0, KWN), (1, KSL)):
                for b in range(NB):
                    pe.matmul(banks[0:64, 3, col:col + 1], at(o_qbrot, 9, 64)[:, b], hid[:, key, SEQ + b:SEQ + b + 1],
                              start=(b == 0), stop=(b == NB - 1))
            for b in range(NB):
                mm = pe.matmul(banks[0:64, 3, 8:8 + NCS], at(o_qbraw, 9, 64)[:, b], kct[:, b], start=(b == 0), stop=(b == NB - 1))
            mm.then_inc(rest_scored, 1)

        def act_window(act, link):
            for b in range(NB):
                act.wait_ge(kwin_turned, b + 1)
                if b >= 2:
                    act.wait_ge(win_scored, b - 1)
                act.activation(kwts[:, b % 2], banks[:, b % 2, :], ACT.Copy).then_inc(kwt_made, 1)
                if b == 2:
                    act_decay(act, link)

        pick_loaded, qg_made = sem("pick_loaded"), sem("qg_made")
        sst_scaled = sem("sst_scaled")
        gla_stored, st_stored = sem("gla_stored"), sem("st_stored")
        dscan = sem("dscan")
        st = small[0:64, 16:32]
        new2 = small[0:64, 32:34]
        ptw = at(o_m, NT, 64)
        pn = at(o_m + 484, 2, NB)[0:64]
        pnt = at(o_qbraw, 2, 64)[0:NB]
        o_dec = o_wout + 10880
        dec = at(o_dec, 3, 2, NT)
        ea = at(o_dec + 24, NB, 2)
        cmp_max, cmp_exp, cmp_probs, cmp_turned, pct_made = (
            sem("cmp_max"), sem("cmp_exp"), sem("cmp_probs"), sem("cmp_turned"), sem("pct_made"))
        imp1_ready, imp1_kept, imp_ready = sem("imp1_ready"), sem("imp1_kept"), sem("imp_ready")
        win_max, win_exp, win_probs = sem("win_max"), sem("win_exp"), sem("win_probs")
        sel_max, sel_exp, sel_probs = sem("sel_max"), sem("sel_exp"), sem("sel_probs")
        p_turned, pt_made = sem("p_turned"), sem("pt_made")
        late_loaded = sem("late_loaded")
        st_loaded = sem("st_loaded")

        def sp_late(sp):
            sp.dma_start(pick, consts["pick"]).then_inc(pick_loaded, 16)
            for hh in range(2):
                sp.dma_start(sst[DK * hh:DK * hh + DK].rearrange("p b c e -> p (b c) e"),
                             ins["state_gla"][0].rearrange("b (c h) d e -> h d (b c) e", h=2)[hh]).then_inc(st_loaded, 16)
            sp.dma_start(earlier, consts["earlier"].rearrange("p (a b) -> p a b", a=NSB)).then_inc(late_loaded, 16)
            sp.dma_start(cmp_ok, consts["cmp_ok"]).then_inc(late_loaded, 16)
            sp.dma_start(cmp_add, consts["cmp_add"]).then_inc(late_loaded, 16)

        X = AX_X

        def dve_maxima(dve, link):
            dve.wait_ge(rest_scored, 1)
            dve.wait_ge(gates_moved, 16)
            link(dve.tensor_copy(new2, banks[0:64, 3, 0:2]))
            link(dve.tensor_reduce(st[:, 0:1], banks[0:64, 3, 8:8 + NCS], X, ALU.max))
            dve.tensor_scalar(st[:, 1:2], st[:, 0:1], -SCALE, None, ALU.mult).then_inc(cmp_max, 1)
            link(dve.tensor_copy(sw[:, 1:WINDOW], banks[0:64, 2, 1:WINDOW]))
            link(dve.memset(sw[:, 0:1], NEG))
            link(dve.tensor_copy(sw[:, WINDOW:WINDOW + 1], new2[:, 0:1]))
            link(dve.tensor_reduce(st[:, 4:5], sw, X, ALU.max))
            dve.tensor_scalar(st[:, 5:6], st[:, 4:5], -SCALE, None, ALU.mult).then_inc(win_max, 1)

        def dve_probs(dve, link):
            dve.wait_ge(cmp_exp, 1)
            link(dve.reciprocal(st[:, 3:4], st[:, 2:3]))
            link(dve.tensor_scalar(pcs, pcs, st[:, 3:4], None, ALU.mult))
            dve.tensor_scalar(pcg, pcs, gates_h[:, 0:1], None, ALU.mult).then_inc(cmp_probs, 1)
            dve.wait_ge(win_exp, 1)
            link(dve.reciprocal(st[:, 7:8], st[:, 6:7]))
            link(dve.tensor_tensor(st[:, 7:8], st[:, 7:8], gates_h[:, 2:3], ALU.mult))
            link(dve.tensor_scalar(sw, sw, st[:, 7:8], None, ALU.mult))
            dve.tensor_scalar(pn[:, 1], own_row[0:64], sw[:, WINDOW:WINDOW + 1], None, ALU.mult).then_inc(win_probs, 1)

        def dve_select(dve, link):
            dve.wait_ge(imp1_ready, 1)
            dve.tensor_copy(imp1, banks[0:64, 1, 0:NSB]).then_inc(imp1_kept, 1)
            dve.wait_ge(imp_ready, 1)
            link(dve.tensor_tensor(imp, banks[0:64, 1, 0:NSB], forced[0:64, 0], ALU.mult))
            link(dve.tensor_tensor(imp, imp, forced[0:64, 1], ALU.add))
            other = imp.unsqueeze(1).broadcast_to([64, NSB, NSB])
            mine = imp.unsqueeze(2).broadcast_to([64, NSB, NSB])
            link(dve.tensor_tensor(cmps[:, 1], other, mine, ALU.is_equal))
            dve.wait_ge(late_loaded, 48)
            link(dve.tensor_tensor(cmps[:, 1], cmps[:, 1], earlier, ALU.mult))
            link(dve.tensor_tensor(cmps[:, 0], other, mine, ALU.is_gt))
            link(dve.tensor_tensor(cmps[:, 0], cmps[:, 0], cmps[:, 1], ALU.add))
            link(dve.tensor_reduce(rank, cmps[:, 0], X, ALU.add))
            link(dve.tensor_scalar(rank, rank, N_SEL - 0.5, 1.0, ALU.is_lt, ALU.subtract))
            link(dve.tensor_scalar(rank, rank, -NEG, None, ALU.mult))
            dve.wait_ge(sel_kept, 4)
            sv = ssel[:, 0:PAST].rearrange("p (j t s q) -> p j t s q", j=8, t=2, s=4)
            mask = rank[:, 0:NSB - 1].rearrange("p (j s) -> p j s", j=8).unsqueeze(3).broadcast_to([64, 8, 4, 32])
            for t in range(2):
                link(dve.tensor_tensor(sv[:, :, t], sv[:, :, t], mask, ALU.add))
            link(dve.tensor_copy(ssel[:, PAST:PAST + 1], new2[:, 1:2]))
            link(dve.tensor_reduce(st[:, 8:9], ssel, X, ALU.max))
            dve.tensor_scalar(st[:, 9:10], st[:, 8:9], -SCALE, None, ALU.mult).then_inc(sel_max, 1)

        def dve_sel_probs(dve, link):
            dve.wait_ge(sel_exp, 1)
            link(dve.reciprocal(st[:, 11:12], st[:, 10:11]))
            link(dve.tensor_tensor(st[:, 11:12], st[:, 11:12], gates_h[:, 1:2], ALU.mult))
            link(dve.tensor_scalar(ssel, ssel, st[:, 11:12], None, ALU.mult))
            dve.tensor_scalar(pn[:, 0], own_row[0:64], ssel[:, PAST:PAST + 1], None, ALU.mult).then_inc(sel_probs, 1)

        def act_exps(act):
            act.wait_ge(cmp_max, 1)
            act.activation(pcs, banks[0:64, 3, 8:8 + NCS], ACT.Exp, bias=st[:, 1:2], scale=SCALE,
                           accum_out=st[:, 2:3]).then_inc(cmp_exp, 1)
            act.wait_ge(win_max, 1)
            act.activation(sw, sw, ACT.Exp, bias=st[:, 5:6], scale=SCALE, accum_out=st[:, 6:7]).then_inc(win_exp, 1)

        def act_keep_cmp(act):
            act.wait_ge(cmp_turned, 1)
            act.activation(at(o_m + 256, P)[0:NCS], banks[0:NCS, 0, 0:P], ACT.Copy).then_inc(pct_made, 1)

        def act_sel_exp(act):
            act.wait_ge(sel_max, 1)
            act.activation(ssel, ssel, ACT.Exp, bias=st[:, 9:10], scale=SCALE, accum_out=st[:, 10:11]).then_inc(sel_exp, 1)

        def act_keep_probs(act):
            for k, (o, i) in enumerate((
                    (pts[:, 0:8].rearrange("p a c -> p (a c)"), banks[:, 1, :]),
                    (pts[:, 8:16].rearrange("p a c -> p (a c)"), banks[:, 4, :]),
                    (ptw.rearrange("p a c -> p (a c)"), banks[:, 5, 0:256]),
                    (pnt.rearrange("p a c -> p (a c)"), banks[0:NB, 5, 256:256 + P]))):
                act.wait_ge(p_turned, min(k, 2) + 1)
                act.activation(o, i, ACT.Copy).then_inc(pt_made, 1)

        def pe_turn_cmp(pe):
            pe.wait_ge(cmp_probs, 1)
            pe.transpose(banks[0:NCS, 0, 0:64], pcs, ident[0:64, 0:64])
            pe.transpose(banks[0:NCS, 0, 64:128], pcg, ident[0:64, 0:64]).then_inc(cmp_turned, 1)

        def pe_importance(pe):
            pe.wait_ge(pct_made, 1)
            pe.matmul(banks[0:64, 1, 0:NSB], pct[0:NCS], overlap[0:NCS], start=True, stop=True).then_inc(imp1_ready, 1)
            pe.wait_ge(imp1_kept, 1)
            pe.matmul(banks[0:64, 1, 0:NSB], group_sum[0:64], imp1, start=True, stop=True).then_inc(imp_ready, 1)

        def pe_turn_sample_probs(pe):
            pe.wait_ge(sel_probs, 1)
            pe.wait_ge(win_probs, 1)
            for j in range(16):
                tr = pe.transpose(banks[:, 4 if j // 8 else 1, j % 8 * 64:(j % 8 + 1) * 64], ssel[:, j * P:(j + 1) * P],
                                  ident[0:64, 0:64])
                if j % 8 == 7:
                    tr.then_inc(p_turned, 1)
            for w in range(NT):
                pe.transpose(banks[:, 5, w * 64:(w + 1) * 64], sw[:, w * P:(w + 1) * P], ident[0:64, 0:64])
            for k in range(2):
                tr = pe.transpose(banks[0:NB, 5, 256 + k * 64:256 + (k + 1) * 64], pn[:, k], ident[0:64, 0:64])
            tr.then_inc(p_turned, 1)

        b_ready, e_ready, qk_ready = sem("b_ready"), sem("e_ready"), sem("qk_ready")
        kf_turned, kf_made = sem("kf_turned"), sem("kf_made")
        a_ready, att_made, o_ready, o_kept = sem("a_ready"), sem("att_made"), sem("o_ready"), sem("o_kept")
        kv_ready, kv_used, gs_ready, gs_done = sem("kv_ready"), sem("kv_used"), sem("gs_ready"), sem("gs_done")
        vb_ready, vb_used, os_ready, os_kept = sem("vb_ready"), sem("vb_used"), sem("os_ready"), sem("os_kept")
        gsq, gstat, groot, gsilu, mix_g = sem("gsq"), sem("gstat"), sem("groot"), sem("gsilu"), sem("mix_g")

        def dve_decay(dve, link):
            dve.wait_ge(la_ready, 2)
            for hp in range(2):
                for c in range(NT):
                    x = slice(c * P, (c + 1) * P)
                    dve.tensor_tensor_scan(gb[:, hp, x], la[:, hp, x], la[:, hp, x], 0.0, ALU.add, ALU.bypass).then_inc(dscan, 1)
            dve.wait_ge(dscan, 8)
            for hp in range(2):
                for c in range(NT):
                    x = slice(c * P, (c + 1) * P)
                    dve.tensor_scalar(e1[:, hp, x], gb[:, hp, x], gb[:, hp, c * P + 63:c * P + 64], None,
                                      ALU.subtract).then_inc(b_ready, 1)

        def dve_decayed(dve, link):
            dve.wait_ge(e_ready, 1)
            link(dve.tensor_copy(dec[:, 2], e1.rearrange("p h (c t) -> p h c t", c=NT)[:, :, :, P - 1]))
            dve.scalar_tensor_tensor(out=e1, in0=hid[:, QG:QG + 2, 0:SEQ], scalar=DK ** -0.5, in1=e1,
                                     op0=ALU.mult, op1=ALU.mult).then_inc(qk_ready, 1)
            dve.tensor_tensor(e2, hid[:, KG:KG + 2, 0:SEQ], e2, ALU.mult).then_inc(qk_ready, 1)

        def dve_sample_states(dve, link):
            for b in range(NB):
                if b == 0:
                    dve.wait_ge(sst_scaled, 1)
                dve.wait_ge(vb_ready, b + 1)
                for h in range(H_GLA):
                    hp, x = h // 2, slice(DK * (h % 2), DK * (h % 2) + DK)
                    dve.scalar_tensor_tensor(out=sst[x, b, hp], in0=banks[x, 4 + b % 2, h * DV:(h + 1) * DV],
                                             scalar=hid[x, KG + hp, SEQ + b:SEQ + b + 1], in1=sst[x, b, hp],
                                             op0=ALU.mult, op1=ALU.add).then_inc(vb_used, 1)
                if b == 3:
                    dve_decayed(dve, link)

        def dve_gla_chunk(dve, link, c):
            if c:
                dve.wait_ge(o_ready, 2 * c)
            for hh in range(2):
                dve.wait_ge(a_ready, 2 * c + hh + 1)
                dve.scalar_tensor_tensor(out=att.rearrange("p (c h) t -> p h c t", h=2)[:, hh],
                                         in0=banks[:, 4 + hh, 0:256].rearrange("p (c t) -> p c t", c=2), scalar=-NEG,
                                         in1=causal_t.unsqueeze(1).broadcast_to([P, 2, P]),
                                         op0=ALU.min, op1=ALU.mult).then_inc(att_made, 1)
            dve.wait_ge(kv_ready, c + 1)
            for hp in range(2):
                kv = banks[:, 2, hp * P:(hp + 1) * P]
                if c == 0:
                    link(dve.tensor_scalar(gs[:, hp], kv, dec[:, 2, hp, c:c + 1], None, ALU.mult))
                else:
                    link(dve.tensor_scalar(gs[:, hp], gs[:, hp], dec[:, 1, hp, c:c + 1], None, ALU.mult))
                    link(dve.scalar_tensor_tensor(out=gs[:, hp], in0=kv, scalar=dec[:, 2, hp, c:c + 1], in1=gs[:, hp],
                                                  op0=ALU.mult, op1=ALU.add))
            dve.sem_inc(kv_used, 1)
            if c < NT - 1:
                if c:
                    dve.wait_ge(o_ready, 2 * c + 2)
                for hp in range(2):
                    dve.tensor_scalar(gsd[:, hp], gs[:, hp], dec[:, 0, hp, c + 1:c + 2], None, ALU.mult).then_inc(gs_ready, 1)
            else:
                dve.sem_inc(gs_done, 1)

        head_root = [gtmp, gtmp2, ssum, rs]

        def dve_gla_norm(dve, link, h):
            v = head_root[h]
            dve.wait_ge(groot, h + 1)
            link(dve.reciprocal(v, v))
            link(dve.scalar_tensor_tensor(out=hid[:, VG + h], in0=hid[:, VG + h], scalar=cols[:, COL_GO:COL_GO + 1],
                                          in1=v, op0=ALU.mult, op1=ALU.mult))
            dve.wait_ge(gsilu, h + 1)
            dve.tensor_tensor(hid[:, RG + h], hid[:, RG + h], hid[:, VG + h], ALU.mult).then_inc(mix_g, 1)

        def act_decay(act, link):
            T16 = 1.0 / 16.0
            act.wait_ge(b_ready, 8)
            g4 = gb.rearrange("p h (c t) -> p h c t", c=NT)
            act.activation(dec[:, 0], g4[:, :, :, 63], ACT.Exp, scale=T16)
            act.activation(dec[:, 1], g4[:, :, :, P - 1], ACT.Exp, scale=T16)
            link(act.activation(e2, e1, ACT.Exp, scale=-T16))
            act.activation(e1, e1, ACT.Exp, scale=T16).then_inc(e_ready, 1)

        def act_keep_keys(act):
            for k in range(2):
                act.wait_ge(kf_turned, k + 1)
                act.activation(kft[:, 2 * k:2 * k + 2].rearrange("p c h d -> p (c h d)"), banks[:, k, :], ACT.Copy).then_inc(kf_made, 1)

        def act_gla_chunk(act, c):
            for hh in range(2):
                act.wait_ge(o_ready, 2 * c + hh + 1)
                act.activation(hid[:, VG + hh:VG + hh + 3:2, c * P:(c + 1) * P],
                               banks[:, 6 + hh, 0:256].rearrange("p (c t) -> p c t", c=2), ACT.Copy).then_inc(o_kept, 1)

        def act_sample_out(act):
            act.wait_ge(os_ready, 1)
            for hh in range(2):
                act.activation(hid[:, VG + hh:VG + hh + 3:2, SEQ:T],
                               banks[:, 3, 0:4 * NB].rearrange("p (c b h) -> p c b h", c=2, h=2)[:, :, :, hh], ACT.Copy,
                               scale=DK ** -0.5).then_inc(os_kept, 1)

        def act_gate(act):
            act.wait_ge(proj_kept_v, 6)
            act.wait_ge(proj_kept_a, 6)
            for h in range(H_GLA):
                act.activation(hid[:, RG + h], hid[:, RG + h], ACT.Silu).then_inc(gsilu, 1)

        def act_gla_norm(act):
            act.wait_ge(os_kept, 2)
            act.wait_ge(o_kept, 8)
            for h in range(2):
                act.activation(sq2[:, h], hid[:, VG + h], ACT.Square).then_inc(gsq, 1)
            for h in range(H_GLA):
                act.wait_ge(gstat, h + 1)
                if h < 2:
                    act.activation(sq2[:, h], hid[:, VG + h + 2], ACT.Square).then_inc(gsq, 1)
                act.activation(halves(head_root[h]), pair(2 if h % 2 else 6), ACT.Sqrt, bias=eps_col,
                               scale=float(D_MODEL // DV)).then_inc(groot, 1)

        def pe_gla_keys(pe):
            pe.wait_ge(qk_ready, 2)
            for k in range(2):
                for c in range(2):
                    for hp in range(2):
                        x = (2 * k + c) * P
                        tr = pe.transpose(banks[:, k, (2 * c + hp) * P:(2 * c + hp + 1) * P], e2[:, hp, x:x + P], ident)
                tr.then_inc(kf_turned, 1)

        def pe_gla_scores(pe, c):
            x = slice(c * P, (c + 1) * P)
            if c == 0:
                pe.wait_ge(vb_used, H_GLA * NB)
            else:
                pe.wait_ge(att_made, 2 * c)
            for hh in range(2):
                r_ = slice(DK * hh, DK * hh + DK)
                for hp in range(2):
                    mm = pe.matmul(banks[:, 4 + hh, hp * P:(hp + 1) * P], e2[r_, hp, x], e1[r_, hp, x], start=True, stop=True)
                mm.then_inc(a_ready, 1)
            if c == 0:
                pe.wait_ge(kf_made, 2)
                pe.wait_ge(win_max, 1)
            else:
                pe.wait_ge(kv_used, c)
            for hh in range(2):
                for hp in range(2):
                    h = 2 * hp + hh
                    mm = pe.matmul(banks[DK * hh:DK * hh + DK, 2, hp * P:(hp + 1) * P],
                                   kft[:, c, hp, DK * hh:DK * hh + DK], vtok[:, c, h * DV:(h + 1) * DV],
                                   start=True, stop=True)
            mm.then_inc(kv_ready, 1)

        def pe_gla_out(pe, c):
            x = slice(c * P, (c + 1) * P)
            if c == 0:
                pe.wait_ge(sel_kept, 4)
            else:
                pe.wait_ge(o_kept, 2 * c)
                pe.wait_ge(gs_ready, 2 * c)
            for hh in range(2):
                pe.wait_ge(att_made, 2 * c + hh + 1)
                r_ = slice(DK * hh, DK * hh + DK)
                for hp in range(2):
                    h = 2 * hp + hh
                    o = banks[:, 6 + hh, hp * P:(hp + 1) * P]
                    mm = pe.matmul(o, vtok[:, c, h * DV:(h + 1) * DV], att[:, h], start=True, stop=(c == 0))
                    if c > 0:
                        mm = pe.matmul(o, gsd[r_, hp], e1[r_, hp, x], start=False, stop=True)
                mm.then_inc(o_ready, 1)

        def pe_sample_gla(pe):
            pe.wait_ge(qg_made, 2)
            for hp in range(2):
                for b in range(NB):
                    o = 2 * (hp * NB + b)
                    mm = pe.matmul(banks[:, 3, o:o + 2], sst[:, b, hp], qg_pair[:, hp, b], start=True, stop=True)
            mm.then_inc(os_ready, 1)

        def pe_gla_norm(pe):
            pe.wait_ge(o_kept, 8)
            pe.wait_ge(os_kept, 2)
            pe.wait_ge(kv_used, NT)
            for h in range(H_GLA):
                pe.wait_ge(gsq, h + 1)
                if h >= 2:
                    pe.wait_ge(groot, h - 1)
                for a in range(2):
                    mm = pe.matmul(banks[:, (2 if h % 2 else 6) + a, 0:HT], ones, sq2[:, h % 2, a * HT:(a + 1) * HT], start=True, stop=True)
                mm.then_inc(gstat, 1)

        def pe_gla_and_softmaxes(pe):
            pe_gla_keys(pe)
            pe_gla_scores(pe, 0)
            pe_gla_out(pe, 0)
            pe_gla_scores(pe, 1)
            pe_turn_cmp(pe)
            pe_gla_out(pe, 1)
            pe_importance(pe)
            pe_sample_gla(pe)
            for c in (2, 3):
                pe_gla_scores(pe, c)
                pe_gla_out(pe, c)
            pe_gla_norm(pe)
            pe_turn_sample_probs(pe)

        def dve_gla_and_softmaxes(dve, link):
            dve_maxima(dve, link)
            dve_gla_chunk(dve, link, 0)
            dve_probs(dve, link)
            dve_gla_chunk(dve, link, 1)
            dve_select(dve, link)
            dve_gla_chunk(dve, link, 2)
            dve_gla_chunk(dve, link, 3)
            dve_sel_probs(dve, link)

        def act_gla_and_softmaxes(act):
            act_keep_keys(act)
            act_exps(act)
            act_gla_chunk(act, 0)
            act_keep_cmp(act)
            act_gla_chunk(act, 1)
            act_sample_out(act)
            act_sel_exp(act)
            act_gla_chunk(act, 2)
            act_gla_chunk(act, 3)
            act_gla_norm(act)
            act_keep_probs(act)

        def tile_units(i):
            return [("c", i, 0)] + [(kind, i, r) for r in range(R) for kind in ("s", "w")]

        PAIRS = ((3, 0), (2, 1))
        UNITS = [x for a, b in PAIRS for two in zip(tile_units(a), tile_units(b)) for x in two]
        TILES = [i for two in PAIRS for i in two]
        NORM_AT = (9, 13, 17, 21)
        SAMPLE_AT = tuple(range(5, 5 + 4 * NB, 4))
        before = lambda u, kinds: sum(x[0] in kinds for x in UNITS[:u])
        place = lambda i: TILES.index(i) % 2
        last_of = lambda i: max(u for u, x in enumerate(UNITS) if x[1] == i)
        s_scored, c_read, c_sub, m_made, p_made = (sem("s_scored"), sem("c_read"), sem("c_sub"), sem("m_made"), sem("p_made"))
        c_exp, p_scaled, t_done, pt_kept, pv_done = sem("c_exp"), sem("p_scaled"), sem("t_done"), sem("pt_kept"), sem("pv_done")
        ao_kept, keys_split = sem("ao_kept"), sem("keys_split")
        amx, anm = small[:, 34:38], small[:, 38:42]
        asu, acf = small[:, 42:46], small[:, 46:50]
        amx8, acf8 = small[:, 50:58], at(o_b + 10801, 8)

        def pe_scores(pe, u):
            kind, i, r = UNITS[u]
            q = slice(i * P, (i + 1) * P)
            if u >= 2:
                if UNITS[u - 2][0] == "c":
                    pe.wait_ge(c_read, 2 * (before(u - 2, "c") + 1))
                else:
                    pe.wait_ge(p_made, 2 * (before(u - 2, "sw") + 1))
            if kind == "c":
                for r in range(R):
                    mm = pe.matmul(banks[:, 2 * (u % 2), r * G * NCP:(r + 1) * G * NCP], hid[:, QN + r, q], kct[:, NB, 0:G * NCP],
                                   start=True, stop=True)
            else:
                for g in range(G):
                    which = 0 if kind == "s" else 1
                    key = keys_g1[:, which] if g else hid[:, (KSL, KWN)[which]]
                    mm = pe.matmul(banks[:, 2 * (u % 2) + g, 0:(i + 1) * P], qr[:, r, q], key[:, 0:(i + 1) * P],
                                   start=True, stop=True)
            mm.then_inc(s_scored, 1)

        def pe_turn_probs(pe, u):
            kind, i, r = UNITS[u]
            pe.wait_ge(p_scaled, 2 * (u + 1))
            if u:
                pe.wait_ge(pt_kept, u)
            for g in range(G):
                if g == 1 and u - 1 in SAMPLE_AT:
                    pe.wait_ge(so_kept, SAMPLE_AT.index(u - 1) + 1)
                if kind == "c":
                    for r in range(R):
                        tr = pe.transpose(banks[0:NCP, 4 + g, r * P:(r + 1) * P], cp[place(i)][:, g, r], ident)
                else:
                    for j in range(i + 1):
                        tr = pe.transpose(banks[:, 4 + g, j * P:(j + 1) * P], pr[:, u % 2, g, j * P:(j + 1) * P], ident)
            tr.then_inc(t_done, 1)

        def pe_values(pe, u):
            kind, i, r = UNITS[u]
            if kind == "c":
                return
            pe.wait_ge(pt_kept, u + 1)
            if kind == "s" and r == 0 and TILES.index(i) >= 2:
                pe.wait_ge(ao_kept, TILES.index(i) - 1)
            for g in range(G):
                o = banks[D * g:D * g + D, 6 + place(i), r * P:(r + 1) * P]
                if kind == "s":
                    pe.matmul(o, vcm[0:NCP, NB, D * g:D * g + D], ptc[place(i)][0:NCP, g, r * P:(r + 1) * P],
                              start=True, stop=False, skip_group_check=True)
                for j in range(i + 1):
                    mm = pe.matmul(o, kvtok[:, j, 3 if kind == "s" else 5, D * g:D * g + D],
                                   prt[:, u % 2, g, j * P:(j + 1) * P], start=False, stop=(kind == "w" and j == i),
                                   skip_group_check=True)
            mm.then_inc(pv_done, 1)

        def pe_attention(pe):
            pe.wait_ge(groot, 4)
            pe.wait_ge(pt_made, 4)
            pe.wait_ge(keys_split, 6)
            pe_scores(pe, 0)
            pe_scores(pe, 1)
            for u in range(len(UNITS)):
                if u + 2 < len(UNITS):
                    pe_scores(pe, u + 2)
                pe_turn_probs(pe, u)
                if u:
                    pe_values(pe, u - 1)
                if u in SAMPLE_AT:
                    pe.wait_ge(pt_kept, u + 1)
                    pe_sample_values(pe, SAMPLE_AT.index(u))
            pe_values(pe, len(UNITS) - 1)
            pe_sample_turn(pe)

        def dve_attention(dve, link):
            dve.wait_ge(late_loaded, 48)

            def maxima(u):
                kind, i, r = UNITS[u]
                b = 2 * (u % 2)
                dve.wait_ge(s_scored, u + 1)
                if kind == "c":
                    c, n = cp[place(i)], before(u, "c")
                    if n >= 2:
                        dve.wait_ge(t_done, UNITS.index(("c", TILES[n - 2], 0)) + 1)
                    add = cmp_add[:, i].unsqueeze(1).broadcast_to([P, R, NCP])
                    for g in range(G):
                        dve.tensor_tensor(c[:, g], banks[:, b, 0:G * R * NCP].rearrange("p (r g n) -> p g r n", g=G, r=R)[:, g], add,
                                          ALU.add).then_inc(c_read, 1)
                    dve.wait_ge(c_read, 2 * (n + 1))
                    c8 = c.rearrange("p g r n -> p (g r) n")
                    link(dve.tensor_reduce(amx8, c8, AX_X, ALU.max))
                    dve.tensor_tensor(c8, c8, amx8.unsqueeze(2).broadcast_to([P, G * R, NCP]), ALU.subtract).then_inc(c_sub, 1)
                else:
                    d = banks[:, b:b + 2, i * P:(i + 1) * P]
                    link(dve.tensor_tensor(d, d, causal_add.unsqueeze(1).broadcast_to([P, 2, P]), ALU.add))
                    m = slice(2 * (u % 2), 2 * (u % 2) + 2)
                    link(dve.tensor_reduce(amx[:, m], banks[:, b:b + 2, 0:(i + 1) * P], AX_X, ALU.max))
                    dve.tensor_scalar(anm[:, m], amx[:, m], -SCALE, None, ALU.mult).then_inc(m_made, 1)

            def scales(u):
                kind, i, r = UNITS[u]
                if kind == "c":
                    dve.wait_ge(c_exp, before(u, "c") + 1)
                    c8 = cp[place(i)].rearrange("p g r n -> p (g r) n")
                    link(dve.tensor_reduce(acf8, c8, AX_X, ALU.add))
                    link(dve.reciprocal(acf8, acf8))
                    link(dve.tensor_tensor(acf8, acf8, gates[:, i, 0:24:3], ALU.mult))
                    link(dve.tensor_tensor(c8, c8, cmp_ok[:, i].unsqueeze(1).broadcast_to([P, G * R, NCP]), ALU.mult))
                    dve.tensor_tensor(c8, c8, acf8.unsqueeze(2).broadcast_to([P, G * R, NCP]), ALU.mult).then_inc(p_scaled, 2)
                else:
                    m = 2 * (u % 2)
                    dve.wait_ge(p_made, 2 * (before(u, "sw") + 1))
                    link(dve.reciprocal(acf[:, m:m + 2], asu[:, m:m + 2]))
                    br = 1 if kind == "s" else 2
                    link(dve.tensor_tensor(acf[:, m:m + 2], acf[:, m:m + 2], gates[:, i, 3 * r + br:24:12], ALU.mult))
                    for g in range(G):
                        w = pr[:, u % 2, g, 0:(i + 1) * P]
                        dve.tensor_scalar(w, w, acf[:, m + g:m + g + 1], None, ALU.mult).then_inc(p_scaled, 1)

            maxima(0)
            maxima(1)
            for u in range(len(UNITS)):
                scales(u)
                if u in NORM_AT:
                    dve_gla_norm(dve, link, NORM_AT.index(u))
                if u + 2 < len(UNITS):
                    maxima(u + 2)

        def act_attention(act):
            def exps(u):
                kind, i, r = UNITS[u]
                if kind == "c":
                    act.wait_ge(c_sub, before(u, "c") + 1)
                    c_ = cp[place(i)].rearrange("p g r n -> p (g r n)")
                    act.activation(c_, c_, ACT.Exp, scale=SCALE).then_inc(c_exp, 1)
                    return
                act.wait_ge(m_made, before(u, "sw") + 1)
                if u >= 2:
                    act.wait_ge(t_done, u - 1)
                for g in range(G):
                    m = 2 * (u % 2) + g
                    act.activation(pr[:, u % 2, g, 0:(i + 1) * P], banks[:, m, 0:(i + 1) * P], ACT.Exp,
                                   bias=anm[:, m:m + 1], scale=SCALE, accum_out=asu[:, m:m + 1]).then_inc(p_made, 1)

            def keep_turned_probs(u):
                kind, i, r = UNITS[u]
                if kind == "c":
                    n = before(u, "c")
                    if n >= 2:
                        act.wait_ge(pv_done, before(last_of(TILES[n - 2]), "sw") + 1)
                    act.activation(ptc[place(i)][0:NCP], banks[0:NCP, 4:6, :], ACT.Copy).then_inc(pt_kept, 1)
                else:
                    users = [v for v in range(u) if v % 2 == u % 2 and UNITS[v][0] != "c"]
                    if users:
                        act.wait_ge(pv_done, before(users[-1], "sw") + 1)
                    act.activation(prt[:, u % 2, :, 0:(i + 1) * P], banks[:, 4:6, 0:(i + 1) * P], ACT.Copy).then_inc(pt_kept, 1)

            def keep_out(i):
                act.wait_ge(pv_done, before(last_of(i), "sw") + 1)
                act.activation(hid[:, QN:QN + R, i * P:(i + 1) * P],
                               banks[:, 6 + place(i), :].rearrange("p (r t) -> p r t", r=R), ACT.Copy).then_inc(ao_kept, 1)

            def keep_sample(b):
                act.wait_ge(so_used, b + 1)
                if b == 0:
                    act.wait_ge(st_stored, 32)
                act.activation(so_tok[:, b], banks[0:H_NSA, 5, 0:P], ACT.Copy).then_inc(so_kept, 1)

            exps(0)
            exps(1)
            for u in range(len(UNITS)):
                act.wait_ge(t_done, u + 1)
                keep_turned_probs(u)
                for i in TILES:
                    if last_of(i) == u - 2:
                        keep_out(i)
                if u + 2 < len(UNITS):
                    exps(u + 2)
                if u in SAMPLE_AT:
                    keep_sample(SAMPLE_AT.index(u))
            for i in TILES:
                if last_of(i) >= len(UNITS) - 2:
                    keep_out(i)

        vbuf = [at(o_b + 2560 * s, 8, 2, P) for s in range(2)]
        vwbuf = [at(o_b + 2560 * s + 2048, NT, P) for s in range(2)]
        v_loaded = [sem("v_loaded0"), sem("v_loaded1")]
        so_ready, mix_s = sem("so_ready"), sem("mix_s")
        so_used, so_kept, vload_begun = sem("so_used"), sem("so_kept"), sem("vload_begun")

        def load_values(eng, s):
            cache = ins["cache_nsa"][0].rearrange("n (p t) k g d -> n p t (k g d)", t=2)
            eng.wait_ge(o_ready, 2 * NT)
            eng.wait_ge(o_kept, 2 * NT)
            eng.wait_ge(gla_stored, 32)

            def sample(b):
                for pg in range(NPG):
                    n = eng.value_load(ptab[0:1, bass.ds(b * NPG + pg, 1)], min_val=0, max_val=cache.shape[0] - 1)
                    eng.dma_start(vbuf[s][64 * (pg % 2):64 * (pg % 2) + 64, pg // 2],
                                  cache[bass.ds(n, 1), :, :, 3 * P:4 * P].rearrange("o p t c -> p (o t) c")).then_inc(v_loaded[s], 16)
                eng.dma_start(vwbuf[s], ins["state_win"][0, bass.ds(b, 1)].rearrange("o (w p) v g d -> p (o w) v (g d)", p=P)[:, :, 1])\
                    .then_inc(v_loaded[s], 16)

            sample(s)
            with eng.Fori(1, NB // 2) as i:
                eng.wait_ge(so_used, 2 * i + s - 1)
                if s:
                    eng.sem_inc(vload_begun, 1)
                sample(2 * i + s)

        so_tok = at(o_b + 6640, NB, P)[0:H_NSA]

        def pe_sample_values(pe, b):
            s = b % 2
            o, x = banks[0:H_NSA, 5, 0:P], slice(H_NSA * b, H_NSA * b + H_NSA)

            def add(p, v, **flags):
                return pe.matmul(o, p, v, **{"start": False, "stop": False, **flags})

            add(pnt[:, 0, x], kvs[:, 3], start=True)
            add(pnt[:, 1, x], kvs[:, 5])
            add(pcgt[0:NCS, x], vcm[0:NCS, b])
            pe.wait_ge(v_loaded[s], 16 * (NPG + 1) * (b // 2 + 1))
            for j in range(16):
                add(pts[:, j, x], vbuf[s][:, j // 2, j % 2])
            for w in range(NT):
                mm = add(ptw[:, w, x], vwbuf[s][:, w], stop=(w == NT - 1))
            mm.then_inc(so_used, 1)

        def pe_sample_turn(pe):
            pe.wait_ge(so_kept, NB)
            for b in range(NB):
                tr = pe.transpose(banks[:, 5, H_NSA * b:H_NSA * b + H_NSA], so_tok[:, b], ident[0:H_NSA, 0:H_NSA])
            tr.then_inc(so_ready, 1)

        def dve_sample_out(dve):
            dve.wait_ge(so_ready, 1)
            for g in range(G):
                x = slice(D * g, D * g + D)
                dve.tensor_copy(hid[x, QN:QN + R, SEQ:T],
                                banks[x, 5, 0:64].rearrange("p (b h r) -> p h r b", h=G, r=R)[:, g]).then_inc(mix_s, 1)

        p_loaded, p_turned2, p_kept = sem("p_loaded"), sem("p_turned2"), sem("p_kept")
        sig_made, ple_y = sem("sig_made"), sem("ple_y")
        wp_loaded = sem("wp_loaded")
        yo_turned, yo_a, yo_v, y_stored = sem("yo_turned"), sem("yo_a"), sem("yo_v"), sem("y_stored")
        o_kv = o_kvtok
        pstage = at(o_kv, 5, PLE_DIM)
        pT = at(o_kv + 5 * PLE_DIM, 2, T)
        wp = at(o_wout, 2, D_MODEL)
        yo, yo_s = at(o_n, NT, D_MODEL), at(o_tmp, D_MODEL)[0:NB]

        def pool_stores(pool):
            pool_cache(pool)
            pool.wait_ge(sel_scored, NB)
            pool.memset(qg_pair, 0.0).then_inc(pool_step, 1)
            pool.wait_ge(pool_step, 1)
            for hh in range(2):
                x = slice(DK * hh, DK * hh + DK)
                pool.tensor_copy(qg_pair[x, :, :, hh], hid[x, QG:QG + 2, SEQ:T]).then_inc(qg_made, 1)
                pool.wait_ge(qg_made, hh + 1)
            pool.wait_ge(st_loaded, 32)
            pool.wait_ge(ea_made, 1)
            pool.tensor_tensor(sst.rearrange("p b h e -> p (b h) e"), sst.rearrange("p b h e -> p (b h) e"),
                               ea.rearrange("p b h -> p (b h)").unsqueeze(2).broadcast_to([P, 2 * NB, DV]), ALU.mult)\
                .then_inc(sst_scaled, 1)
            pool.wait_ge(b_ready, 8)
            steps = [0]
            for w, chunk in enumerate((KSL, KWN)):
                for made in (lambda: pool.memset(keys_g1[0:D, w], 0.0),
                             lambda: pool.tensor_copy(keys_g1[D:P, w], hid[D:P, chunk, 0:SEQ]),
                             lambda: pool.memset(hid[D:P, chunk, 0:SEQ], 0.0)):
                    made().then_inc(keys_split, 1)
                    steps[0] += 1
                    pool.wait_ge(keys_split, steps[0])
            pool.wait_ge(vb_used, H_GLA * NB)
            for hh in range(2):
                pool.dma_start(outs["gla_sample"][0].rearrange("b (c h) d e -> h d (b c) e", h=2)[hh],
                               sst[DK * hh:DK * hh + DK].rearrange("p b c e -> p (b c) e")).then_inc(st_stored, 16)
            pool.wait_ge(gs_done, 1)
            for hh in range(2):
                pool.dma_start(outs["gla_prompt"].rearrange("l b (c h) d e -> h d (l b c) e", h=2)[hh],
                               gs[DK * hh:DK * hh + DK]).then_inc(gla_stored, 16)
            load_values(pool, 1)
            pool.wait_ge(rows_stored, 80)
            pool.wait_ge(gla_stored, 32)
            pool.wait_ge(st_stored, 32)


        def sp_out_first(sp):
            sp_out_weights(sp, (0, 1))

        def sp_out_last(sp):
            sp_out_weights(sp, (2, 3))

        def sp_out_weights(sp, groups):
            wo = ins["w_mix_out"][0]
            for q in groups:
                sp.wait_ge(rest_scored, 1) if q < 2 else sp.wait_ge(pv_done, 2 * R * NT)
                c = slice(q * GW, (q + 1) * GW)
                sp.dma_start(win[:, q, 0:4], wo[0:512, c].rearrange("(k p) n -> p k n", p=P)).then_inc(win_loaded[q], 16)
                for g in range(G):
                    sp.dma_start(win[D * g:D * g + D, q, 4:8],
                                 wo[512 + g * 256:512 + (g + 1) * 256, c].rearrange("(r d) n -> d r n", d=D)).then_inc(win_loaded[q], 16)

        def sp_rest(sp):
            sp.wait_ge(rows_stored, 80)
            sp.wait_ge(so_ready, 1)
            sp.wait_ge(pv_done, 2 * R * NT)
            sp.dma_start(pstage[:, 0:4], ins["p_prompt"][0, 0].rearrange("(i p) d -> p i d", p=P)).then_inc(p_loaded, 16)
            sp.dma_start(pstage[0:NB, 4], ins["p_sample"][0].rearrange("b s d -> (b s) d")).then_inc(p_loaded, 16)
            sp.wait_ge(st_stored, 32)
            sp_ffn_out(sp, 1, ins["ffn2_w_out"][0], first=True)
            sp_ffn_in(sp, 1, ins["ffn2_w_in"][0], lambda e: e.wait_ge(y_ready, 16))
            sp_ffn_out(sp, 1, ins["ffn2_w_out"][0], first=False)
            wg = ins["ple_w_gate"][0].rearrange("(k p) n -> p k n", p=P)
            for q in range(4):
                sp.wait_ge(u_ready, 44 if q < 2 else 42)
                sp.dma_start(win[:, q], wg[:, :, q * GW:(q + 1) * GW]).then_inc(win_loaded[q], 16)
            sp.wait_ge(y_ready, 22)
            sp.dma_start(wp, ins["ple_w_proj"][0].rearrange("(k p) n -> p k n", p=P)).then_inc(wp_loaded, 16)
            yp = outs["y_prompt"][0].rearrange("(i p) d -> p i d", p=P)
            for i in range(NT):
                sp.wait_ge(yo_a, i + 1)
                sp.dma_start(yp[:, i, 0:512], yo[:, i, 0:512]).then_inc(y_stored, 16)
            for i in range(NT):
                sp.wait_ge(yo_v if i % 2 else yo_a, i // 2 + 1 + (0 if i % 2 else NT))
                sp.dma_start(yp[:, i, 512:], yo[:, i, 512:]).then_inc(y_stored, 16)
            sp.wait_ge(yo_a, NT + 3)
            sp.wait_ge(yo_v, 3)
            sp.dma_start(outs["y_sample"].rearrange("b s d -> (b s) d"), yo_s).then_inc(y_stored, 16)
            sp.wait_ge(y_stored, 16 * (2 * NT + 1))

        def pe_out(pe):
            pe.wait_ge(ao_kept, NT)
            pe.wait_ge(mix_s, 2)
            pe.wait_ge(mix_g, 4)
            for m in range(KC):
                if m % 2 == 0:
                    pe.wait_ge(win_loaded[m // 2], win_base["out"][m // 2] + 48)
                if m >= 4:
                    pe.wait_ge(y_kept, Y0["out"] + m - 3)
                pe_chunk(pe, 2 * (m % 4), lambda k: win[:, m // 2, k, m % 2 * P:(m % 2 + 1) * P], hid[:, RG:RG + KC], KC)\
                    .then_inc(y_ready, 1)
            pe.wait_ge(y_kept, Y0["out"] + KC)
            pe_post_stats(pe, 1)
            pe.wait_ge(p_loaded, 32)
            for c in range(2):
                for i in range(NT):
                    tr = pe.transpose(banks[:, 2 + c, i * P:(i + 1) * P], pstage[:, i, c * P:(c + 1) * P], ident)
            for c in range(2):
                tr = pe.transpose(banks[:, 4, c * NB:(c + 1) * NB], pstage[0:NB, 4, c * P:(c + 1) * P], ident[0:NB, 0:NB])
            tr.then_inc(p_turned2, 1)
            pe.wait_ge(p_kept, 1)

        def act_embedding(act):
            act.wait_ge(p_turned2, 1)
            act.activation(pT[:, :, 0:SEQ], banks[:, 2:4, :], ACT.Copy)
            act.activation(pT[:, :, SEQ:T], banks[:, 4, 0:2 * NB].rearrange("p (c t) -> p c t", c=2), ACT.Copy).then_inc(p_kept, 1)

        def pe_ple(pe):
            def beside(c):
                if c == 0:
                    pe.wait_ge(win_loaded[0], win_base["ple"][0] + 16)
                for m in range(2):
                    pe_beside(pe, 4 * m, win[:, 0, c, m * P:(m + 1) * P], c, g_ready)

            pe_pre_stats(pe, 3, beside)
            pe.wait_ge(wp_loaded, 16)
            for m in range(KC):
                b = 4 * (m % 2)
                if m >= 2:
                    if m % 2 == 0:
                        pe.wait_ge(win_loaded[m // 2], win_base["ple"][m // 2] + 16)
                    pe.wait_ge(ple_y, m - 1)
                    pe_chunk(pe, b, lambda k: win[:, m // 2, k, m % 2 * P:(m % 2 + 1) * P], nT, KC).then_inc(g_ready, 1)
                elif m == 1:
                    pe.wait_ge(rs_read, 7)
                pe_chunk(pe, b + 2, lambda k: wp[:, k, m * P:(m + 1) * P], pT, 2).then_inc(u_ready, 1)

        def act_ple(act):
            def square(m):
                act.wait_ge(ple_y, m + 1)
                act.wait_ge(ysq_used, Y0["ple"] + m - 1)
                act.activation(sq2[:, m % 2], hid[:, m], ACT.Square).then_inc(y_kept, 1)

            for m in range(KC):
                act.wait_ge(g_scaled, 44 + m + 1)
                act.activation(gtmp2 if m % 2 else gtmp, gtmp2 if m % 2 else gtmp, ACT.Sigmoid).then_inc(sig_made, 1)
                if m:
                    square(m - 1)
            square(KC - 1)

        def dve_ple(dve):
            y0 = Y0["ple"]
            def total(m):
                dve.wait_ge(y_kept, y0 + m + 1)
                dve.wait_ge(ysq_used, y0 + m)
                if m == 0:
                    dve.tensor_copy(ssum, sq2[:, 0]).then_inc(ysq_used, 1)
                else:
                    dve.tensor_tensor(ssum, ssum, sq2[:, m % 2], ALU.add).then_inc(ysq_used, 1)

            for m in range(KC):
                dve.wait_ge(g_ready, 44 + m + 1)
                if m >= 2:
                    dve.wait_ge(ple_y, m - 1)
                dve.tensor_tensor(halves(gtmp2 if m % 2 else gtmp), pair(4 * (m % 2)), halves(rs), ALU.mult).then_inc(g_scaled, 1)
                dve.wait_ge(u_ready, 44 + m + 1)
                dve.wait_ge(sig_made, m + 1)
                dve.tensor_tensor(halves(hid[:, m]), halves(gtmp2 if m % 2 else gtmp), pair(4 * (m % 2) + 2), ALU.mult).then_inc(ple_y, 1)
                if m:
                    total(m - 1)
            total(KC - 1)
            dve.wait_ge(ysq_used, y0 + KC)
            dve.sem_inc(ssum_ready, 1)

        def pe_outputs(pe):
            pe.wait_ge(rs_read, 8)
            for c in range(KC):
                pe.wait_ge(h_ready, 4 * KC + c + 1)
                for i in range(NT):
                    tr = pe.transpose(banks[:, 2 * i + c // 4, c % 4 * P:(c % 4 + 1) * P], hT[:, c, i * P:(i + 1) * P], ident)
                    if c == KC - 1:
                        tr.then_inc(yo_turned, 1)
                if c == 3:
                    tr.then_inc(yo_turned, 1)
            pe.wait_ge(yo_a, NT + 1)
            for c in range(KC):
                tr = pe.transpose(banks[0:NB, c // 4, c % 4 * P:(c % 4 + 1) * P], hT[:, c, SEQ:T], ident)
            tr.then_inc(yo_turned, 1)

        def act_outputs(act):
            act.wait_ge(yo_turned, 1)
            for i in range(NT):
                act.activation(yo[:, i, 0:512], banks[:, 2 * i, :], ACT.Copy).then_inc(yo_a, 1)
            for i in (0, 2):
                act.wait_ge(yo_turned, i + 2)
                act.activation(yo[:, i, 512:], banks[:, 2 * i + 1, :], ACT.Copy).then_inc(yo_a, 1)
            act.wait_ge(yo_turned, NT + 2)
            act.activation(yo_s[:, 0:512], banks[0:NB, 0, :], ACT.Copy).then_inc(yo_a, 1)

        def dve_outputs(dve):
            for i in (1, 3):
                dve.wait_ge(yo_turned, i + 2)
                dve.tensor_copy(yo[:, i, 512:], banks[:, 2 * i + 1, :]).then_inc(yo_v, 1)
            dve.wait_ge(yo_turned, NT + 2)
            dve.tensor_copy(yo_s[:, 512:], banks[0:NB, 1, :]).then_inc(yo_v, 1)

        @block.sync
        def _(sp):
            xs = at(o_wout, 5, D_MODEL)
            sp.dma_start(xs[:, 0:4], ins["x_prompt"][0].rearrange("(i p) d -> p i d", p=P)).then_inc(x_loaded, 16)
            sp.dma_start(xs[0:NB, 4], ins["x_sample"].rearrange("b s d -> (b s) d")).then_inc(x_loaded, 16)
            sp.dma_start(ident, consts["ident"]).then_inc(x_loaded, 16)
            rows = at(o_n, P)
            for i, name in enumerate(gname):
                sp.dma_start(rows[KC * i:KC * (i + 1)], ins[name][0].rearrange("(k p) -> k p", p=P)).then_inc(rows_loaded, 16)
            sp.dma_start(rows[COL_GO:COL_GO + 1], ins["gla_out_norm"]).then_inc(rows_loaded, 16)
            sp.dma_start(rows[COL_BA:COL_BA + 2], ins["b_gla_a"][0].rearrange("(k p) -> k p", p=P)).then_inc(rows_loaded, 16)
            for o, name in ((COL_PK, "cmp_pos_k"), (COL_PV, "cmp_pos_v")):
                sp.dma_start(rows[o:o + 16], ins[name][0].rearrange("(m t) d -> m (t d)", t=2)).then_inc(rows_loaded, 16)
            sp.dma_start(causal_t, consts["causal_t"]).then_inc(const_loaded, 16)
            sp.dma_start(causal_add, consts["causal_add"]).then_inc(const_loaded, 16)
            sp_ffn_in(sp, 0, ins["ffn1_w_in"][0], lambda e: None)
            sp.wait_ge(x_turned, KC)
            sp_ffn_out(sp, 0, ins["ffn1_w_out"][0], first=True)
            sp_ffn_out(sp, 0, ins["ffn1_w_out"][0], first=False)
            wm = ins["w_mix_in"][0].rearrange("(k p) n -> p k n", p=P)
            for j in range(PROJ_G):
                if j < 4:
                    sp.wait_ge(u_ready, 22 if j < 2 else 20)
                else:
                    sp.wait_ge(proj_ready, 2 * (j - 3))
                if j in (6, 7):
                    for rr in range(2):
                        for g in range(G):
                            c0 = C_QN + g * R * D + (2 * (j - 6) + rr) * D
                            sp.dma_start(win[:, j % 4, :, rr * P + g * D:rr * P + (g + 1) * D],
                                         wm[:, :, c0:c0 + D]).then_inc(win_loaded[j % 4], 16)
                else:
                    c0 = j * GW if j < 6 else C_KV + (j - 8) * GW
                    sp.dma_start(win[:, j % 4], wm[:, :, c0:c0 + GW]).then_inc(win_loaded[j % 4], 16)
            sp_mixer_small(sp)
            sp_cache(sp)
            sp_window(sp)
            sp_out_first(sp)
            load_values(sp, 0)
            sp_out_last(sp)
            sp_rest(sp)

        def pe_pre_stats(pe, k, beside):
            for c in range(KC):
                pe.wait_ge(sq_ready, KC * k + c + 1)
                for a in range(2):
                    last = pe.matmul(banks[:, 6 + a, 0:HT], ones[:, :], sq[:, c, a * HT:(a + 1) * HT],
                                     start=(c == 0), stop=(c == KC - 1))
                if c == KC - 1:
                    last.then_inc(stat_ready, 1)
                pe.wait_ge(n_ready, KC * k + c + 1)
                beside(c)

        def pe_beside(pe, b, w, c, done):
            for a in range(2):
                last = pe.matmul(banks[:, b + a, 0:HT], w, nT[:, c, a * HT:(a + 1) * HT], start=(c == 0), stop=(c == KC - 1))
            if c == KC - 1:
                last.then_inc(done, 1)

        def pe_post_stats(pe, k):
            pe.wait_ge(ssum_ready, k + 1)
            for a in range(2):
                last = pe.matmul(banks[:, a, 0:HT], ones[:, :], ssum[:, a * HT:(a + 1) * HT], start=True, stop=True)
            last.then_inc(stat_ready, 1)

        def pe_chunk(pe, b, w, src, nk):
            for k in range(nk):
                for a in range(2):
                    last = pe.matmul(banks[:, b + a, 0:HT], w(k), src[:, k, a * HT:(a + 1) * HT],
                                     start=(k == 0), stop=(k == nk - 1))
            return last

        def pe_ffn(pe, n):
            base = win_base[f"ffn{n + 1}"]

            def group(j, s, i, first=False):
                if not first:
                    pe.wait_ge(win_loaded[2 * s], base[2 * s] + 16 * (i + 1))
                    pe.wait_ge(win_loaded[2 * s + 1], base[2 * s + 1] + 16 * (i + 1))
                for c in range(2):
                    if not first:
                        pe.wait_ge(hid_ready, 22 * n + 2 * j + c - 1)
                        pe_chunk(pe, 4 * c, lambda k: win[:, 2 * s, k, c * P:(c + 1) * P], nT, KC).then_inc(g_ready, 1)
                    elif c == 0:
                        continue
                    else:
                        pe.wait_ge(rs_read, 4 * n + 1)
                    pe_chunk(pe, 4 * c + 2, lambda k: win[:, 2 * s + 1, k, c * P:(c + 1) * P], nT, KC).then_inc(u_ready, 1)

            def beside(c):
                if c == 0:
                    pe.wait_ge(win_loaded[0], base[0] + 16)
                    pe.wait_ge(win_loaded[1], base[1] + 16)
                pe_beside(pe, 0, win[:, 0, c, 0:P], c, g_ready)
                pe_beside(pe, 2, win[:, 1, c, 0:P], c, u_ready)
                pe_beside(pe, 4, win[:, 0, c, P:2 * P], c, g_ready)

            if n:
                pe.wait_ge(rs_read, 4 * n)
            pe_pre_stats(pe, 2 * n, beside)
            group(0, 0, 0, True)
            group(1, 1, 0)
            with pe.Fori(1, 5) as i:
                for s in range(2):
                    group(2 * i + s, s, i)
            group(10, 0, 5)
            pe.wait_ge(hid_ready, 22 * (n + 1))
            for m in range(KC):
                if m % 2 == 0:
                    pe.wait_ge(wout_loaded[m // 2 % 2], 32 * n + 16 * (m // 4 + 1))
                if m >= 4:
                    pe.wait_ge(y_kept, Y0[f"ffn{n + 1}"] + m - 3)
                pe_chunk(pe, 2 * (m % 4), lambda k: wout[:, m // 2 % 2, k, m % 2 * P:(m % 2 + 1) * P], hid, FC)\
                    .then_inc(y_ready, 1)

        @block.tensor
        def _(pe):
            xs = at(o_wout, 5, D_MODEL)
            pe.wait_ge(x_loaded, 48)
            for c in range(KC):
                pe.transpose(banks[:, 7, c * NB:(c + 1) * NB], xs[0:NB, 4, c * P:(c + 1) * P], ident[0:NB, 0:NB])
            for c in range(KC):
                if c >= 4:
                    pe.wait_ge(h_ready, c - 3)
                for i in range(NT):
                    last = pe.transpose(banks[:, c % 4, i * P:(i + 1) * P], xs[:, i, c * P:(c + 1) * P], ident)
                last.then_inc(x_turned, 1)
            pe.wait_ge(rows_loaded, 12 * 16)
            pe.transpose(banks[:, 6, 0:NCOL], at(o_n, P)[0:NCOL], ident[0:NCOL, 0:NCOL]).then_inc(cols_turned, 1)
            pe.wait_ge(init_done, 1)
            pe.wait_ge(cols_made, 1)
            pe.wait_ge(h_ready, KC)
            pe_ffn(pe, 0)
            pe.wait_ge(y_kept, 8)
            pe_post_stats(pe, 0)
            pe.wait_ge(rs_read, 2)

            def beside(c):
                if c == 0:
                    pe.wait_ge(win_loaded[0], win_base["proj"][0] + 16)
                    pe.wait_ge(win_loaded[1], win_base["proj"][1] + 16)
                for m in range(3):
                    pe_beside(pe, 2 * m, win[:, m // 2, c, m % 2 * P:(m % 2 + 1) * P], c, proj_ready)

            pe_pre_stats(pe, 1, beside)
            for j in range(PROJ_G):
                s = j % 4
                turn = sum(64 if q in (6, 7) else 16 for q in range(j + 1) if q % 4 == s)
                pe.wait_ge(win_loaded[s], win_base["proj"][s] + turn)
                for c in range(2):
                    m = 2 * j + c
                    if m < 3:
                        continue
                    if m == 3:
                        pe.wait_ge(rs_read, 3)
                    if m >= 4:
                        pe.wait_ge(proj_kept_v if m % 2 else proj_kept_a, (m - 4) // 2 + 1)
                    pe_chunk(pe, 2 * (m % 4), lambda k: win[:, s, k, c * P:(c + 1) * P], nT, KC)\
                        .then_inc(proj_ready, 1)
            pe_mixer_prep(pe)
            pe_turn(pe)
            pe_position(pe)
            pe_cache(pe)
            pe_window(pe)
            pe_gla_and_softmaxes(pe)
            pe_attention(pe)
            pe_out(pe)
            pe_ffn(pe, 1)
            pe.wait_ge(y_kept, 24)
            pe_post_stats(pe, 2)
            pe.wait_ge(rs_read, 6)
            pe_ple(pe)
            pe_post_stats(pe, 3)
            pe_outputs(pe)

        def act_root(act, k):
            act.wait_ge(stat_ready, k + 1)
            act.activation(halves(rs), pair(0 if k % 2 else 6), ACT.Sqrt, bias=eps_col).then_inc(rs_read, 1)

        def act_pre_norm(act, k, gi):
            for c in range(KC):
                act.wait_ge(h_ready, KC * k + c + 1)
                act.activation(sq[:, c], hT[:, c], ACT.Square).then_inc(sq_ready, 1)
                if c == 0 and k == 0:
                    act.wait_ge(cols_made, 1)
                act.activation(nT[:, c], hT[:, c], ACT.Copy, scale=gains[:, gi, c:c + 1]).then_inc(n_ready, 1)
            act_root(act, 2 * k)

        def act_ffn(act, n):
            with act.Fori(0, 11) as j:
                for c in range(2):
                    v = gtmp2 if c else gtmp
                    act.wait_ge(g_scaled, 22 * n + 2 * j + c + 1)
                    act.activation(v, v, ACT.Silu).then_inc(silu_ready, 1)
            act_keep_y(act, f"ffn{n + 1}")

        def act_keep_y(act, phase):
            y0 = Y0[phase]
            for m in range(KC):
                act.wait_ge(y_ready, y0 + m + 1)
                act.activation(halves(nT[:, m]), pair(2 * (m % 4)), ACT.Copy)
                if y0 + m >= 2:
                    act.wait_ge(ysq_used, y0 + m - 1)
                act.activation(halves(sq2[:, m % 2]), pair(2 * (m % 4)), ACT.Square).then_inc(y_kept, 1)

        @block.scalar
        def _(act):
            steps = [0]

            def link(ins_):
                steps[0] += 1
                ins_.then_inc(act_step, 1)
                act.wait_ge(act_step, steps[0])
                return ins_

            act_pre_norm(act, 0, 0)
            act_ffn(act, 0)
            act_root(act, 1)
            act_pre_norm(act, 1, 2)
            keep_turned(act, lambda o, i: act.activation(o, i, ACT.Copy), kept_a, 0)
            act_gates(act)
            act_log_decay(act, link)
            act_gate(act)
            act.wait_ge(la_ready, 2)
            act.activation(ea.rearrange("p b h -> p h b"), la[:, :, SEQ:T], ACT.Exp, scale=1.0 / 16.0).then_inc(ea_made, 1)
            act_cache(act, link)
            act_window(act, link)
            act_gla_and_softmaxes(act)
            act_attention(act)
            act_keep_y(act, "out")
            act_root(act, 3)
            act_embedding(act)
            act_pre_norm(act, 2, 4)
            act_ffn(act, 1)
            act_root(act, 5)
            act_pre_norm(act, 3, 6)
            act_ple(act)
            act_root(act, 7)
            act_outputs(act)

        def dve_helpers(dve):
            steps = [0]

            def link(ins_):
                steps[0] += 1
                ins_.then_inc(dve_step, 1)
                dve.wait_ge(dve_step, steps[0])

            return link

        def dve_rs(dve, link, k):
            dve.wait_ge(rs_read, k + 1)
            link(dve.reciprocal(rs, rs))

        def dve_sum_squares(dve, phase, k):
            y0 = Y0[phase]
            for m in range(KC):
                dve.wait_ge(y_kept, y0 + m + 1)
                if m == 0:
                    dve.tensor_copy(ssum, sq2[:, 0]).then_inc(ysq_used, 1)
                else:
                    dve.wait_ge(ysq_used, y0 + m)
                    last = dve.tensor_tensor(ssum, ssum, sq2[:, m % 2], ALU.add).then_inc(ysq_used, 1)
            dve.wait_ge(ysq_used, y0 + KC)
            dve.sem_inc(ssum_ready, 1)

        def dve_post_norm(dve, link, k, gi, y=None):
            dve_rs(dve, link, k)
            y = nT if y is None else y
            for c in range(KC):
                link(dve.scalar_tensor_tensor(out=y[:, c], in0=y[:, c], scalar=gains[:, gi, c:c + 1], in1=rs,
                                              op0=ALU.mult, op1=ALU.mult))
                dve.tensor_tensor(hT[:, c], hT[:, c], y[:, c], ALU.add).then_inc(h_ready, 1)

        def dve_ffn(dve, n):
            def gate(k, c, first=False):
                dve.wait_ge(g_ready, k + 1)
                if not first:
                    dve.wait_ge(hid_ready, k - 1)
                dve.tensor_tensor(halves(gtmp2 if c else gtmp), pair(4 * c), halves(rs), ALU.mult).then_inc(g_scaled, 1)

            def up(k, kk, c):
                v = gtmp2 if c else gtmp
                dve.wait_ge(silu_ready, k + 1)
                dve.tensor_tensor(v, v, rs, ALU.mult).then_inc(silu_scaled, 1)
                dve.wait_ge(u_ready, k + 1)
                dve.wait_ge(silu_scaled, k + 1)
                o = at(o_hid, FC, 2, HT)[:, bass.ds(kk, 1)].rearrange("p k a t -> p (k a) t")
                dve.tensor_tensor(o, halves(v), pair(4 * c + 2), ALU.mult).then_inc(hid_ready, 1)

            for c in range(2):
                gate(22 * n + c, c, first=True)
                up(22 * n + c, c, c)
            with dve.Fori(1, 11) as j:
                for c in range(2):
                    gate(22 * n + 2 * j + c, c)
                    up(22 * n + 2 * j + c, 2 * j + c, c)

        @block.vector
        def _(dve):
            link = dve_helpers(dve)
            link(dve.memset(eps_col, EPS))
            dve.memset(ones, 1.0 / D_MODEL).then_inc(init_done, 1)
            dve.wait_ge(x_turned, 1)
            link(dve.tensor_copy(hT[:, :, SEQ:T], banks[:, 7, 0:KC * NB].rearrange("p (c t) -> p c t", c=KC)))
            for c in range(KC):
                dve.wait_ge(x_turned, c + 1)
                dve.tensor_copy(hT[:, c, 0:SEQ], banks[:, c % 4, :]).then_inc(h_ready, 1)
            dve.wait_ge(cols_turned, 1)
            link(dve.tensor_copy(cols, banks[:, 6, 0:NCOL]))
            dve.sem_inc(cols_made, 1)
            for gi in (1, 5):
                link(dve.tensor_scalar(gains[:, gi], gains[:, gi], 0.5, None, ALU.mult))
            dve_rs(dve, link, 0)
            dve_ffn(dve, 0)
            dve_sum_squares(dve, "ffn1", 0)
            dve_post_norm(dve, link, 1, 1)
            dve_rs(dve, link, 2)
            for m in range(2 * PROJ_G):
                dve.wait_ge(proj_ready, m + 1)
                dve.tensor_tensor(halves(hid[:, m]), pair(2 * (m % 4)), halves(rs), ALU.mult)\
                    .then_inc(proj_kept_v if m % 2 else proj_kept_a, 1)
            dve.wait_ge(proj_ready, 23)
            dve.tensor_tensor(halves(ag[0:56]), pair(4)[0:56], halves(rs)[0:56], ALU.mult).then_inc(proj_kept_a, 1)
            dve_mixer_prep(dve, link)
            keep_turned(dve, dve.tensor_copy, kept_v, 1)
            dve_log_decay(dve)
            dve_cache(dve, link)
            dve_decay(dve, link)
            dve_sample_states(dve, link)
            dve_gla_and_softmaxes(dve, link)
            dve_attention(dve, link)
            dve_sample_out(dve)
            dve_sum_squares(dve, "out", 1)
            dve_post_norm(dve, link, 3, 3)
            dve_rs(dve, link, 4)
            dve_ffn(dve, 1)
            dve_sum_squares(dve, "ffn2", 2)
            dve_post_norm(dve, link, 5, 5)
            dve_rs(dve, link, 6)
            dve_ple(dve)
            dve_post_norm(dve, link, 7, 7, hid)
            dve_outputs(dve)

        @block.gpsimd
        def _(pool):
            pool_mixer_prep(pool)
            pool_stores(pool)



OUTS = [("y_prompt", (1, SEQ, D_MODEL)), ("y_sample", (NB, 1, D_MODEL)),
        ("nsa_rows_prompt", (1, 1, SEQ, 4, G, D)), ("win_prompt", (1, 1, WINDOW, 2, G, D)),
        ("gla_prompt", (1, 1, H_GLA, DK, DV)), ("nsa_rows_sample", (1, NB, 1, 4, G, D)),
        ("win_sample", (1, NB, WINDOW, 2, G, D)), ("gla_sample", (1, NB, H_GLA, DK, DV))]


def kernel(**inputs):
    import concourse.bacc as bacc
    from concourse.bass_utils import run_bass_kernel_spmd

    nc = bacc.Bacc("TRN2", target_bir_lowering=False, num_devices=1)
    arrays, ins, consts, outs = {}, {}, {}, {}
    for name, a in inputs.items():
        a = np.ascontiguousarray(a)
        arrays["in_" + name] = a
        ins[name] = nc.dram_tensor("in_" + name, a.shape, mybir.dt.from_np(a.dtype), kind="ExternalInput").ap()
    for name, a in constants().items():
        arrays["const_" + name] = a
        consts[name] = nc.dram_tensor("const_" + name, a.shape, F32, kind="ExternalInput").ap()
    for name, shape in OUTS:
        outs[name] = nc.dram_tensor(name, shape, F32, kind="ExternalOutput").ap()
    build(nc, ins, outs, consts)
    r = run_bass_kernel_spmd(nc, [arrays], core_ids=[0])
    return tuple(r.results[0][name] for name, _ in OUTS)
```
